# Optimizing a Trainium2 kernel written in Bass

```python
import jax, jax.numpy as jnp
from jax import lax
import numpy as np

D_MODEL = 1024
BATCH = 1
SEQ = 1024
DEPTH = 1

N_MIXERS = 2
EPS = 1e-6
GLA_HEADS = 4
GLA_DK = D_MODEL // 2 // GLA_HEADS
GLA_DV = D_MODEL // GLA_HEADS
GLA_GATE_RANK = 16
GLA_GATE_TAU = 16.0
GLA_CHUNK = 64
GLA_IN = 2 * GLA_HEADS * GLA_DK + GLA_HEADS * GLA_DV + GLA_GATE_RANK + GLA_HEADS * GLA_DV
MLA_HEADS = 8
MLA_NOPE = 128
MLA_ROPE = 64
MLA_V = D_MODEL // MLA_HEADS
MLA_Q_LORA = D_MODEL // 4
MLA_KV_LORA = D_MODEL // 8
MLA_IN = MLA_Q_LORA + MLA_KV_LORA + MLA_ROPE
MLA_SCALE = (MLA_NOPE + MLA_ROPE) ** -0.5
ROPE_THETA = 10000.0
Q_BLOCK = 128
MOE_GROUPS = 8
MOE_PER_GROUP = 8
MOE_EXPERTS = MOE_GROUPS * MOE_PER_GROUP
MOE_TOPK = 2
MOE_FF = D_MODEL // 4
MOE_BLOCK = 128


def rmsnorm(x, g):
    x32 = x.astype(jnp.float32)
    y = x32 * lax.rsqrt(jnp.mean(x32 * x32, axis=-1, keepdims=True) + EPS)
    return (y * g.astype(jnp.float32)).astype(x.dtype)

def rope_tables(positions):
    inv_freq = 1.0 / (ROPE_THETA ** (jnp.arange(0, MLA_ROPE, 2, dtype=jnp.float32) / MLA_ROPE))
    ang = positions.astype(jnp.float32)[..., None] * inv_freq
    return jnp.cos(ang), jnp.sin(ang)

def apply_rope(t, cos, sin):
    t32 = t.astype(jnp.float32)
    t1, t2 = jnp.split(t32, 2, axis=-1)
    return jnp.concatenate([t1 * cos - t2 * sin, t2 * cos + t1 * sin], axis=-1).astype(t.dtype)

def gla_mixer(h, w_in, w_gate, b_gate, out_norm, w_o):
    bsz, seq, _ = h.shape
    nc = seq // GLA_CHUNK
    qk = GLA_HEADS * GLA_DK
    vd = GLA_HEADS * GLA_DV
    proj = h @ w_in
    q, k, v, a_lr, r = jnp.split(proj, [qk, 2 * qk, 2 * qk + vd, 2 * qk + vd + GLA_GATE_RANK], axis=-1)
    log_a = jax.nn.log_sigmoid((a_lr @ w_gate + b_gate).astype(jnp.float32)) / GLA_GATE_TAU

    def chunks(t, d):
        return t.reshape(bsz, nc, GLA_CHUNK, GLA_HEADS, d).transpose(0, 3, 1, 2, 4).astype(jnp.float32)

    qc = chunks(q, GLA_DK) * (GLA_DK ** -0.5)
    kc = chunks(k, GLA_DK)
    vc = chunks(v, GLA_DV)
    g = jnp.cumsum(chunks(log_a, GLA_DK), axis=3)
    g_mid = g[:, :, :, GLA_CHUNK // 2:GLA_CHUNK // 2 + 1]
    g_last = g[:, :, :, -1:]
    causal = jnp.tril(jnp.ones((GLA_CHUNK, GLA_CHUNK), dtype=bool))
    a_intra = jnp.einsum('bhnid,bhnjd->bhnij', qc * jnp.exp(g - g_mid), kc * jnp.exp(g_mid - g))
    o_intra = jnp.einsum('bhnij,bhnjv->bhniv', jnp.where(causal, a_intra, 0.0), vc)
    q_inter = jnp.moveaxis(qc * jnp.exp(g), 2, 0)
    k_state = jnp.moveaxis(kc * jnp.exp(g_last - g), 2, 0)
    decay = jnp.moveaxis(jnp.exp(g_last[:, :, :, 0]), 2, 0)
    v_s = jnp.moveaxis(vc, 2, 0)

    def step(state, inp):
        q_i, k_i, v_i, d_i = inp
        o_i = jnp.einsum('bhid,bhdv->bhiv', q_i, state)
        state = state * d_i[..., None] + jnp.einsum('bhjd,bhjv->bhdv', k_i, v_i)
        return state, o_i

    s0 = jnp.zeros((bsz, GLA_HEADS, GLA_DK, GLA_DV), jnp.float32)
    _, o_inter = lax.scan(step, s0, (q_inter, k_state, v_s, decay))
    o = o_intra + jnp.moveaxis(o_inter, 0, 2)
    o = o.transpose(0, 2, 3, 1, 4).reshape(bsz, seq, GLA_HEADS, GLA_DV)
    o = o * lax.rsqrt(jnp.mean(o * o, axis=-1, keepdims=True) + EPS) * out_norm.astype(jnp.float32)
    o = o.reshape(bsz, seq, vd) * jax.nn.silu(r.astype(jnp.float32))
    return o.astype(h.dtype) @ w_o

def mla_mixer(h, cos, sin, w_in, q_norm, w_uq, kv_norm, w_uk, w_uv, w_o):
    bsz, seq, _ = h.shape
    nqb = seq // Q_BLOCK
    proj = h @ w_in
    c_q, c_kv, k_rope = jnp.split(proj, [MLA_Q_LORA, MLA_Q_LORA + MLA_KV_LORA], axis=-1)
    c_q = rmsnorm(c_q, q_norm)
    c_kv = rmsnorm(c_kv, kv_norm)
    q = jnp.einsum('bsc,chd->bshd', c_q, w_uq)
    q_nope, q_rope = q[..., :MLA_NOPE], q[..., MLA_NOPE:]
    q_rope = apply_rope(q_rope, cos[:, :, None, :], sin[:, :, None, :])
    k_rope = apply_rope(k_rope, cos, sin)
    q_lat = jnp.einsum('bshn,chn->bshc', q_nope, w_uk)
    q_cat = jnp.concatenate([q_lat, q_rope], axis=-1) * MLA_SCALE
    k_cat = jnp.concatenate([c_kv, k_rope], axis=-1)
    q_blocks = q_cat.reshape(bsz, nqb, Q_BLOCK, MLA_HEADS, MLA_KV_LORA + MLA_ROPE).transpose(1, 0, 2, 3, 4)
    k_pos = jnp.arange(seq)

    def attend(args):
        q_b, b_idx = args
        s = jnp.einsum('bqhc,bkc->bhqk', q_b, k_cat).astype(jnp.float32)
        q_pos = b_idx * Q_BLOCK + jnp.arange(Q_BLOCK)
        s = jnp.where(k_pos[None, :] <= q_pos[:, None], s, -jnp.inf)
        p = jax.nn.softmax(s, axis=-1).astype(c_kv.dtype)
        return jnp.einsum('bhqk,bkc->bqhc', p, c_kv)

    o_lat = lax.map(attend, (q_blocks, jnp.arange(nqb)))
    o_lat = o_lat.transpose(1, 0, 2, 3, 4).reshape(bsz, seq, MLA_HEADS, MLA_KV_LORA)
    o = jnp.einsum('bshc,chv->bshv', o_lat, w_uv).reshape(bsz, seq, MLA_HEADS * MLA_V)
    return o @ w_o

def hier_moe(h, w_group, w_expert, w1, w3, w2):
    bsz, seq, dm = h.shape
    n_tok = bsz * seq
    xf = h.reshape(n_tok, dm)
    tok = jnp.arange(n_tok)
    g_logits = (xf @ w_group).astype(jnp.float32)
    g_prob = jax.nn.softmax(g_logits, axis=-1)
    g_sel = jnp.argmax(g_logits, axis=-1)
    g_w = g_prob[tok, g_sel]
    e_logits = (xf @ w_expert).astype(jnp.float32).reshape(n_tok, MOE_GROUPS, MOE_PER_GROUP)
    e_prob = jax.nn.softmax(e_logits[tok, g_sel], axis=-1)
    top_p, top_i = lax.top_k(e_prob, MOE_TOPK)
    gates = g_w[:, None] * top_p / jnp.sum(top_p, axis=-1, keepdims=True)
    expert_id = g_sel[:, None] * MOE_PER_GROUP + top_i
    n_asg = n_tok * MOE_TOPK
    flat_e = expert_id.reshape(n_asg)
    flat_tok = jnp.arange(n_asg) // MOE_TOPK
    flat_gate = gates.reshape(n_asg)
    order = jnp.argsort(flat_e)
    se, stok, sgate = flat_e[order], flat_tok[order], flat_gate[order]
    counts = jax.ops.segment_sum(jnp.ones_like(flat_e), flat_e, num_segments=MOE_EXPERTS)
    starts = jnp.cumsum(counts) - counts
    padded = (counts + MOE_BLOCK - 1) // MOE_BLOCK * MOE_BLOCK
    pend = jnp.cumsum(padded)
    pstarts = pend - padded
    dest = pstarts[se] + (jnp.arange(n_asg) - starts[se])
    n_slots = n_asg + MOE_EXPERTS * MOE_BLOCK
    n_blocks = n_slots // MOE_BLOCK
    slot_tok = jnp.full((n_slots,), n_tok, dtype=jnp.int32).at[dest].set(stok.astype(jnp.int32))
    slot_gate = jnp.zeros((n_slots,), jnp.float32).at[dest].set(sgate)
    block_e = jnp.minimum(jnp.searchsorted(pend, jnp.arange(n_blocks) * MOE_BLOCK, side='right'), MOE_EXPERTS - 1)
    x_pad = jnp.concatenate([xf, jnp.zeros((1, dm), xf.dtype)], axis=0)
    xs = x_pad[slot_tok].reshape(n_blocks, MOE_BLOCK, dm)

    def expert_block(args):
        xb, e = args
        hid = jax.nn.silu(xb @ w1[e]) * (xb @ w3[e])
        return hid @ w2[e]

    ys = lax.map(expert_block, (xs, block_e)).reshape(n_slots, dm)
    ys = ys * slot_gate[:, None].astype(ys.dtype)
    out = jnp.zeros((n_tok + 1, dm), ys.dtype).at[slot_tok].add(ys)[:n_tok]
    return out.reshape(bsz, seq, dm)

def first_inputs(seed: int = 0) -> dict:
    key = jax.random.key(seed)
    ks = jax.random.split(key, 24)
    f32 = jnp.float32
    n_gla = (DEPTH + N_MIXERS - 1) // N_MIXERS
    n_mla = DEPTH // N_MIXERS

    def nrm(k, shape, fan_in):
        return jax.random.normal(k, shape, f32) * (fan_in ** -0.5)

    def gain(k, shape):
        return 1.0 + 0.1 * jax.random.normal(k, shape, f32)

    x = jax.random.normal(ks[0], (BATCH, SEQ, D_MODEL), f32)
    offsets = jax.random.randint(ks[1], (BATCH, 1), 0, 4096, dtype=jnp.int32)
    positions = offsets + jnp.arange(SEQ, dtype=jnp.int32)[None, :]
    return {
        'x': x,
        'positions': positions,
        'attn_norm': gain(ks[2], (DEPTH, D_MODEL)),
        'ffn_norm': gain(ks[3], (DEPTH, D_MODEL)),
        'final_norm': gain(ks[4], (D_MODEL,)),
        'gla_w_in': nrm(ks[5], (n_gla, D_MODEL, GLA_IN), D_MODEL),
        'gla_w_gate': nrm(ks[6], (n_gla, GLA_GATE_RANK, GLA_HEADS * GLA_DK), GLA_GATE_RANK),
        'gla_b_gate': 0.1 * jax.random.normal(ks[7], (n_gla, GLA_HEADS * GLA_DK), f32),
        'gla_out_norm': gain(ks[8], (n_gla, GLA_DV)),
        'gla_w_o': nrm(ks[9], (n_gla, GLA_HEADS * GLA_DV, D_MODEL), GLA_HEADS * GLA_DV),
        'mla_w_in': nrm(ks[10], (n_mla, D_MODEL, MLA_IN), D_MODEL),
        'mla_q_norm': gain(ks[11], (n_mla, MLA_Q_LORA)),
        'mla_w_uq': nrm(ks[12], (n_mla, MLA_Q_LORA, MLA_HEADS, MLA_NOPE + MLA_ROPE), MLA_Q_LORA),
        'mla_kv_norm': gain(ks[13], (n_mla, MLA_KV_LORA)),
        'mla_w_uk': nrm(ks[14], (n_mla, MLA_KV_LORA, MLA_HEADS, MLA_NOPE), MLA_KV_LORA),
        'mla_w_uv': nrm(ks[15], (n_mla, MLA_KV_LORA, MLA_HEADS, MLA_V), MLA_KV_LORA),
        'mla_w_o': nrm(ks[16], (n_mla, MLA_HEADS * MLA_V, D_MODEL), MLA_HEADS * MLA_V),
        'moe_w_group': nrm(ks[17], (DEPTH, D_MODEL, MOE_GROUPS), D_MODEL),
        'moe_w_expert': nrm(ks[18], (DEPTH, D_MODEL, MOE_EXPERTS), D_MODEL),
        'moe_w1': nrm(ks[19], (DEPTH, MOE_EXPERTS, D_MODEL, MOE_FF), D_MODEL),
        'moe_w3': nrm(ks[20], (DEPTH, MOE_EXPERTS, D_MODEL, MOE_FF), D_MODEL),
        'moe_w2': nrm(ks[21], (DEPTH, MOE_EXPERTS, MOE_FF, D_MODEL), MOE_FF),
    }

def first_block(x, positions, attn_norm, ffn_norm, final_norm,
              gla_w_in, gla_w_gate, gla_b_gate, gla_out_norm, gla_w_o,
              mla_w_in, mla_q_norm, mla_w_uq, mla_kv_norm, mla_w_uk, mla_w_uv, mla_w_o,
              moe_w_group, moe_w_expert, moe_w1, moe_w3, moe_w2):
    cos, sin = rope_tables(positions)
    for i in range(DEPTH):
        j = i // N_MIXERS
        h = rmsnorm(x, attn_norm[i])
        if i % N_MIXERS == 0:
            m = gla_mixer(h, gla_w_in[j], gla_w_gate[j], gla_b_gate[j], gla_out_norm[j], gla_w_o[j])
        else:
            m = mla_mixer(h, cos, sin, mla_w_in[j], mla_q_norm[j], mla_w_uq[j], mla_kv_norm[j],
                          mla_w_uk[j], mla_w_uv[j], mla_w_o[j])
        x = x + m.astype(x.dtype)
        h = rmsnorm(x, ffn_norm[i])
        x = x + hier_moe(h, moe_w_group[i], moe_w_expert[i], moe_w1[i], moe_w3[i], moe_w2[i]).astype(x.dtype)
    return rmsnorm(x, final_norm)


CHUNK = 64
D_MIX = D_MODEL
SSD_WIDTH = D_MIX // 2
ATTN_WIDTH = D_MIX - SSD_WIDTH
SSD_HEAD_DIM = 64
SSD_HEADS = SSD_WIDTH // SSD_HEAD_DIM
SSD_GROUPS = 2
SSD_HPG = SSD_HEADS // SSD_GROUPS
SSD_STATE = 128
SSD_CONV = 4
SSD_CHUNK = CHUNK
XBC_DIM = SSD_WIDTH + 2 * SSD_GROUPS * SSD_STATE
ATTN_HEAD_DIM = 64
ATTN_HEADS = ATTN_WIDTH // ATTN_HEAD_DIM
LEFT_CHUNKS = 8
BAND = (LEFT_CHUNKS + 1) * CHUNK
MAX_REL = 128
N_REL = 2 * MAX_REL + 1
FFN_DIM = 2816
FFN_CONV = 3
ADA_DIM = 6 * D_MODEL
IN_SIZES = (SSD_WIDTH, XBC_DIM, SSD_HEADS, ATTN_WIDTH, ATTN_WIDTH, ATTN_WIDTH)
IN_DIM = sum(IN_SIZES)
IN_SPLITS = [int(v) for v in np.cumsum(IN_SIZES)[:-1]]


def rmsnorm_2(x, w):
    xf = x.astype(jnp.float32)
    y = xf * lax.rsqrt(jnp.mean(xf * xf, axis=-1, keepdims=True) + EPS)
    return (y * w.astype(jnp.float32)).astype(x.dtype)

def causal_dwconv(x, w):
    k, ch = w.shape
    return lax.conv_general_dilated(x, w[:, None, :].astype(x.dtype), window_strides=(1,),
                                    padding=[(k - 1, 0)], dimension_numbers=('NWC', 'WIO', 'NWC'),
                                    feature_group_count=ch)

def ssd_scan(xdt, adt, bm, cm):
    b, s = xdt.shape[:2]
    nc = s // SSD_CHUNK
    L = SSD_CHUNK
    X = xdt.reshape(b, nc, L, SSD_GROUPS, SSD_HPG, SSD_HEAD_DIM)
    A = adt.reshape(b, nc, L, SSD_GROUPS, SSD_HPG)
    Bm = bm.reshape(b, nc, L, SSD_GROUPS, SSD_STATE)
    Cm = cm.reshape(b, nc, L, SSD_GROUPS, SSD_STATE)
    a_cs = jnp.cumsum(A, axis=2)
    seg = a_cs[:, :, :, None] - a_cs[:, :, None]
    causal = jnp.tril(jnp.ones((L, L), dtype=bool))[:, :, None, None]
    decay_ls = jnp.exp(jnp.where(causal, seg, -jnp.inf))
    cb = jnp.einsum('bclgn,bcsgn->bclsg', Cm, Bm)
    y_diag = jnp.einsum('bclsg,bclsge,bcsgep->bclgep', cb, decay_ls, X)
    decay_to_end = jnp.exp(a_cs[:, :, -1:] - a_cs)
    states = jnp.einsum('bclgn,bclge,bclgep->bcgepn', Bm, decay_to_end, X)
    chunk_decay = jnp.exp(a_cs[:, :, -1])

    def step(h, inp):
        st, dec = inp
        return h * dec[..., None, None] + st, h

    _, prev = lax.scan(step, jnp.zeros_like(states[:, 0]),
                       (jnp.moveaxis(states, 1, 0), jnp.moveaxis(chunk_decay, 1, 0)))
    prev = jnp.moveaxis(prev, 0, 1)
    y_off = jnp.einsum('bclgn,bcgepn,bclge->bclgep', Cm, prev, jnp.exp(a_cs))
    return (y_diag + y_off).reshape(b, s, SSD_HEADS, SSD_HEAD_DIM)

def ssd_mixer(z, xbc, dt_raw, conv_w, conv_b, dt_bias, a_log, d_skip, norm_w):
    b, s, _ = xbc.shape
    xbc = jax.nn.silu(causal_dwconv(xbc, conv_w) + conv_b.astype(xbc.dtype))
    xs, bm, cm = jnp.split(xbc.astype(jnp.float32), [SSD_WIDTH, SSD_WIDTH + SSD_GROUPS * SSD_STATE], axis=-1)
    xs = xs.reshape(b, s, SSD_HEADS, SSD_HEAD_DIM)
    bm = bm.reshape(b, s, SSD_GROUPS, SSD_STATE)
    cm = cm.reshape(b, s, SSD_GROUPS, SSD_STATE)
    dt = jax.nn.softplus(dt_raw.astype(jnp.float32) + dt_bias.astype(jnp.float32))
    A = -jnp.exp(a_log.astype(jnp.float32))
    y = ssd_scan(xs * dt[..., None], dt * A, bm, cm)
    y = y + d_skip.astype(jnp.float32)[:, None] * xs
    y = y.reshape(b, s, SSD_WIDTH) * jax.nn.silu(z.astype(jnp.float32))
    return rmsnorm_2(y, norm_w).astype(z.dtype)

def chunk_attention(q, k, v, rel_bias):
    b, s, _ = q.shape
    nc = s // CHUNK
    pad = LEFT_CHUNKS * CHUNK
    qc = q.reshape(b, nc, CHUNK, ATTN_HEADS, ATTN_HEAD_DIM)

    def band(t):
        tp = jnp.pad(t.reshape(b, s, ATTN_HEADS, ATTN_HEAD_DIM), ((0, 0), (pad, 0), (0, 0), (0, 0)))
        tp = tp.reshape(b, nc + LEFT_CHUNKS, CHUNK, ATTN_HEADS, ATTN_HEAD_DIM)
        return jnp.concatenate([tp[:, w:w + nc] for w in range(LEFT_CHUNKS + 1)], axis=2)

    kb, vb = band(k), band(v)
    scores = jnp.einsum('bcqhd,bckhd->bhcqk', qc, kb).astype(jnp.float32) * (ATTN_HEAD_DIM ** -0.5)
    qi = jnp.arange(CHUNK)[:, None]
    kj = jnp.arange(BAND)[None, :]
    rel_idx = jnp.clip(qi - kj + pad, -MAX_REL, MAX_REL) + MAX_REL
    bias = rel_bias.astype(jnp.float32)[:, rel_idx]
    key_pos = jnp.arange(nc)[:, None] * CHUNK - pad + kj
    valid = (key_pos >= 0)[:, None, :]
    scores = jnp.where(valid, scores + bias[:, None], jnp.finfo(jnp.float32).min)
    p = jax.nn.softmax(scores, axis=-1).astype(v.dtype)
    o = jnp.einsum('bhcqk,bckhd->bcqhd', p, vb)
    return o.reshape(b, s, ATTN_WIDTH)

def conv_ffn(h, w_up, conv_w, w_down):
    u = causal_dwconv(h @ w_up, conv_w)
    g, val = jnp.split(u, 2, axis=-1)
    return (jax.nn.silu(g) * val) @ w_down

def second_inputs(seed: int = 0) -> dict:
    key = jax.random.key(seed)
    ks = jax.random.split(key, 24)
    f32 = jnp.float32
    nrm = lambda k, shape, sc: jax.random.normal(k, shape, f32) * sc
    u = jax.random.uniform(ks[10], (DEPTH, SSD_HEADS), f32)
    dt0 = jnp.exp(u * (jnp.log(0.1) - jnp.log(0.001)) + jnp.log(0.001))
    return {
        "x": nrm(ks[0], (BATCH, SEQ, D_MODEL), 1.0),
        "c": nrm(ks[1], (BATCH, D_MODEL), 1.0),
        "norm_mix_w": 1.0 + nrm(ks[2], (DEPTH, D_MODEL), 0.05),
        "w_ada": nrm(ks[3], (DEPTH, D_MODEL, ADA_DIM), 0.02),
        "b_ada": nrm(ks[4], (DEPTH, ADA_DIM), 0.02),
        "w_in": nrm(ks[5], (DEPTH, D_MODEL, IN_DIM), D_MODEL ** -0.5),
        "ssd_conv_w": nrm(ks[6], (DEPTH, SSD_CONV, XBC_DIM), SSD_CONV ** -0.5),
        "ssd_conv_b": nrm(ks[7], (DEPTH, XBC_DIM), 0.02),
        "dt_bias": dt0 + jnp.log(-jnp.expm1(-dt0)),
        "a_log": jnp.log(jax.random.uniform(ks[8], (DEPTH, SSD_HEADS), f32, 1.0, 16.0)),
        "d_skip": 1.0 + nrm(ks[9], (DEPTH, SSD_HEADS), 0.1),
        "ssd_norm_w": 1.0 + nrm(ks[11], (DEPTH, SSD_WIDTH), 0.05),
        "rel_bias": nrm(ks[12], (DEPTH, ATTN_HEADS, N_REL), 0.5),
        "w_out": nrm(ks[13], (DEPTH, D_MIX, D_MODEL), D_MIX ** -0.5),
        "norm_ffn_w": 1.0 + nrm(ks[14], (DEPTH, D_MODEL), 0.05),
        "w_up": nrm(ks[15], (DEPTH, D_MODEL, 2 * FFN_DIM), D_MODEL ** -0.5),
        "ffn_conv_w": nrm(ks[16], (DEPTH, FFN_CONV, 2 * FFN_DIM), FFN_CONV ** -0.5),
        "w_down": nrm(ks[17], (DEPTH, FFN_DIM, D_MODEL), FFN_DIM ** -0.5),
        "final_norm_w": 1.0 + nrm(ks[18], (D_MODEL,), 0.05),
    }

def second_block(x, c, norm_mix_w, w_ada, b_ada, w_in, ssd_conv_w, ssd_conv_b, dt_bias, a_log, d_skip,
              ssd_norm_w, rel_bias, w_out, norm_ffn_w, w_up, ffn_conv_w, w_down, final_norm_w):
    c_act = jax.nn.silu(c)
    for l in range(DEPTH):
        mod = (c_act @ w_ada[l] + b_ada[l])[:, None, :]
        sh_m, sc_m, g_m, sh_f, sc_f, g_f = jnp.split(mod, 6, axis=-1)
        h = rmsnorm_2(x, norm_mix_w[l]) * (1 + sc_m) + sh_m
        z, xbc, dt_raw, q, k, v = jnp.split(h @ w_in[l], IN_SPLITS, axis=-1)
        y_ssd = ssd_mixer(z, xbc, dt_raw, ssd_conv_w[l], ssd_conv_b[l], dt_bias[l], a_log[l],
                          d_skip[l], ssd_norm_w[l])
        y_att = chunk_attention(q, k, v, rel_bias[l])
        x = x + g_m * (jnp.concatenate([y_ssd, y_att], axis=-1) @ w_out[l])
        h = rmsnorm_2(x, norm_ffn_w[l]) * (1 + sc_f) + sh_f
        x = x + g_f * conv_ffn(h, w_up[l], ffn_conv_w[l], w_down[l])
    return rmsnorm_2(x, final_norm_w)


def setup_inputs(seed=0):
    out = dict(first_inputs(seed))
    for name, value in second_inputs(seed + 1).items():
        if name != "x":
            out[name + "_2"] = value
    return out


def reference(
    x, positions, attn_norm, ffn_norm, final_norm, gla_w_in, gla_w_gate, gla_b_gate,
    gla_out_norm, gla_w_o, mla_w_in, mla_q_norm, mla_w_uq, mla_kv_norm, mla_w_uk, mla_w_uv,
    mla_w_o, moe_w_group, moe_w_expert, moe_w1, moe_w3, moe_w2, c_2, norm_mix_w_2, w_ada_2,
    b_ada_2, w_in_2, ssd_conv_w_2, ssd_conv_b_2, dt_bias_2, a_log_2, d_skip_2, ssd_norm_w_2,
    rel_bias_2, w_out_2, norm_ffn_w_2, w_up_2, ffn_conv_w_2, w_down_2, final_norm_w_2,
):
    x = first_block(
        x, positions, attn_norm, ffn_norm, final_norm, gla_w_in, gla_w_gate, gla_b_gate,
        gla_out_norm, gla_w_o, mla_w_in, mla_q_norm, mla_w_uq, mla_kv_norm, mla_w_uk, mla_w_uv,
        mla_w_o, moe_w_group, moe_w_expert, moe_w1, moe_w3, moe_w2,
    )
    return second_block(
        x, c_2, norm_mix_w_2, w_ada_2, b_ada_2, w_in_2, ssd_conv_w_2, ssd_conv_b_2, dt_bias_2,
        a_log_2, d_skip_2, ssd_norm_w_2, rel_bias_2, w_out_2, norm_ffn_w_2, w_up_2,
        ffn_conv_w_2, w_down_2, final_norm_w_2,
    )


_drawn_inputs = setup_inputs


def setup_inputs(seed=0):
    import zlib

    import numpy as np

    out = dict(_drawn_inputs(seed))
    spreads = {}
    factors = {'norm_mix_w_2': 2.916,
     'ssd_conv_b_2': 8.0,
     'd_skip_2': 23.2,
     'ssd_norm_w_2': 3.731,
     'rel_bias_2': 3.55,
     'norm_ffn_w_2': 2.987}
    for name, (base, spread) in spreads.items():
        noise = np.random.default_rng([zlib.crc32(name.encode()), seed]).standard_normal(out[name].shape)
        drawn = base * np.exp(spread * noise) if base else spread * noise
        out[name] = __import__('jax').numpy.asarray(drawn.astype(out[name].dtype))
    for name, factor in factors.items():
        out[name] = (out[name] * factor).astype(out[name].dtype)
    return out
```

```python
import numpy as np
import concourse.bass as bass
from concourse import mybir
from contextlib import ExitStack

F32 = mybir.dt.float32
I32 = mybir.dt.int32
U32 = mybir.dt.uint32
ALU = mybir.AluOpType
ACT = mybir.ActivationFunctionType
AX = mybir.AxisListType

P = 128
T = 1024
D = 1024
TT = T // P
KT = D // P
HALF = 512
EPS = 1e-6
CH = 64

GH, GDK, GDV, RANK, TAU = 4, 128, 256, 16, 16.0
GROUPS, PER_GROUP, EXPERTS, FF = 8, 8, 64, 256
SLOTS = 64
NOWHERE = 8192
SH, SHD, SG, SN = 8, 64, 2, 128
HPG = SH // SG
TAPS = 4
AH, AHD = 8, 64
BANDT = 5
BAND = BANDT * P
NREL, MAXREL = 257, 128
MASKED = -1e30
FDIM = 2816
FT = FDIM // P
FTAPS = 3

IN_AT = {"z": 0, "xbc": 512, "dt": 1536, "q": 1544, "k": 2056, "v": 2568}

VEC = {}
_row = 0
for _name, _n in (("attn_norm", KT), ("ffn_norm", KT), ("gla_b_gate", GH), ("norm_mix_w_2", KT), ("norm_ffn_w_2", KT),
                  ("ssd_norm_w_2", 4), ("ssd_conv_b_2", KT), ("ssd_conv_w_2", TAPS * KT), ("c_2", KT)):
    VEC[_name] = (_row, _n)
    _row += _n
VROWS = _row
FROWS = FTAPS * 2 * FT
FSPLIT = FROWS // 2


_names = {}


def fresh(name):
    _names[name] = _names.get(name, 0) + 1
    return f"{name}_{_names[name]}"


def rows_of(ap):
    return ap.rearrange("(r c) -> r c", c=P)


def spread(ap, n=P):
    return ap.to_broadcast([n, ap.shape[1]])


class Parts:
    pass


def carry(engine, m):
    engine.sem_inc(m.carried, 1)



def transposes(pe, m, src, tiles_ready, ps, ps_ready, ps_free):
    for n in range(2 * KT):
        k, half = n // 2, n % 2
        if n == 0:
            tiles_ready(pe)
        if n >= 4:
            pe.wait_ge(ps_free, n - 3)
        for j in range(4):
            last = pe.transpose(ps[:, n % 4, j * P:(j + 1) * P], src[:, 4 * half + j, k * P:(k + 1) * P],
                                m.ident[:, :])
        last.then_inc(ps_ready, 1)


def transposes_out(dve, dst, gain, bias, ps, ps_ready, ps_free):
    for n in range(2 * KT):
        k, half = n // 2, n % 2
        dve.wait_ge(ps_ready, n + 1)
        out = dst[:, k, half * HALF:(half + 1) * HALF]
        g = gain(k)
        if g is None:
            ins = dve.tensor_copy(out, ps[:, n % 4, :])
        elif bias is None:
            ins = dve.tensor_scalar(out, ps[:, n % 4, :], g, None, ALU.mult)
        else:
            ins = dve.tensor_scalar(out, ps[:, n % 4, :], g, bias(k), ALU.mult, ALU.add)
        ins.then_inc(ps_free, 1)


def inverse_rms(act, dve, ss, root, inv, width, squares, roots):
    if act is not None:
        act.wait_ge(squares, 1)
        act.activation(root, ss, ACT.Sqrt).then_inc(roots, 1)
    if dve is not None:
        dve.wait_ge(roots, 1)
        dve.reciprocal(inv, root)
        dve.drain()


def rms_to_channels(nc, m, src, xn, dst, gain, bias, loads=None, to_dram=None, spill=None):
    with ExitStack() as ctx:
        sem = lambda n: nc.alloc_semaphore(fresh(n))
        arrived = [sem(f"x_tile_arrived{t}") for t in range(TT)] if loads is not None else None
        squares, roots, scaled = sem("squares_summed"), sem("roots_taken"), sem("tiles_scaled")
        ps_ready, ps_free, stored = sem("transposed"), sem("transposed_out"), sem("normed_stored")
        ss = ctx.enter_context(nc.sbuf_tensor(fresh("sum_sq"), [P, TT], F32))
        root = ctx.enter_context(nc.sbuf_tensor(fresh("root"), [P, TT], F32))
        inv = ctx.enter_context(nc.sbuf_tensor(fresh("inv_rms"), [P, TT], F32))
        junk = ctx.enter_context(nc.sbuf_tensor(fresh("squares"), [P, D], F32))
        sums = sem("act_sums")
        ps = ctx.enter_context(nc.psum_tensor(fresh("ps_transposed"), [P, 4, HALF], F32))
        block = ctx.enter_context(nc.Block())

        @block.sync
        def _(sp):
            if loads is not None:
                for t in range(TT):
                    sp.dma_start(src[:, t, :], loads[t * P:(t + 1) * P, :]).then_inc(arrived[t], 16)
            if spill is not None:
                sp.dma_start(spill.rearrange("(t p) d -> p t d", p=P), src).then_inc(stored, 16)
                sp.wait_ge(stored, 16)
            if to_dram is not None:
                sp.wait_ge(scaled, TT)
                sp.dma_start(to_dram.rearrange("(t p) d -> p t d", p=P), xn).then_inc(stored, 16)
                sp.wait_ge(stored, 16)

        @block.scalar
        def _(act):
            for t in range(TT):
                if arrived:
                    act.wait_ge(arrived[t], 16)
                act.activation(junk[:, :], src[:, t, :], ACT.Square, accum_out=ss[:, t:t + 1]).then_inc(sums, 1)
                act.drain()
            inverse_rms(act, None, ss[:, :], root[:, :], None, D, squares, roots)

        @block.vector
        def _(dve):
            dve.wait_ge(sums, TT)
            dve.tensor_scalar(ss[:, :], ss[:, :], 1.0 / D, EPS, ALU.mult, ALU.add).then_inc(squares, 1)
            inverse_rms(None, dve, None, root[:, :], inv[:, :], D, squares, roots)
            for t in range(TT):
                dve.tensor_scalar(xn[:, t, :], src[:, t, :], inv[:, t:t + 1], None, ALU.mult).then_inc(scaled, 1)
            transposes_out(dve, dst, gain, bias, ps, ps_ready, ps_free)

        @block.tensor
        def _(pe):
            transposes(pe, m, xn, lambda e: e.wait_ge(scaled, TT), ps, ps_ready, ps_free)


class Ring:

    def __init__(self, nc, ctx, sources):
        self.buf = ctx.enter_context(nc.sbuf_tensor("weight_ring", [P, 2, KT, HALF], F32))
        self.loaded = [ctx.enter_context(nc.semaphore(f"weights_loaded{s}")) for s in range(2)]
        self.used = ctx.enter_context(nc.semaphore("weights_used"))
        self.sources, self.issued = sources, 0

    def issue(self, sp, first, end):
        for b in range(first, end):
            assert b == self.issued
            self.issued += 1
            if b >= 2:
                sp.wait_ge(self.used, b - 1)
            at = 0
            for src in self.sources[b]:
                n = src.shape[1]
                sp.dma_start(self.buf[:, b % 2, :, at:at + n],
                             src.rearrange("(k p) n -> p k n", p=P)).then_inc(self.loaded[b % 2], 16)
                at += n

    def release(self, engine):
        engine.sem_inc(self.used, 1)

    def loads_before(self, b):
        return 16 * sum(len(self.sources[c]) for c in range(b % 2, b + 1, 2))


def gemm_tokens(pe, ring, slot, act_t, ps, n0, ps_ready, ps_free, banks):
    for t in range(TT):
        pe.wait_ge(ps_free, n0 + t + 1)
        for k in range(KT):
            last = pe.matmul(ps[:, t % banks, :], act_t[:, k, t * P:(t + 1) * P], ring.buf[:, slot, k, :],
                             start=(k == 0), stop=(k == KT - 1))
        last.then_inc(ps_ready, 1)
    return last


def gemm_channels(pe, ring, slot, tiles, act_t, ps, n0, ps_ready, ps_free, banks):
    for j, c in enumerate(tiles):
        for half in range(2):
            n = 2 * j + half
            pe.wait_ge(ps_free, n0 + n + 1)
            for k in range(KT):
                last = pe.matmul(ps[:, n % banks, :], ring.buf[:, slot, k, c * P:(c + 1) * P],
                                 act_t[:, k, half * HALF:(half + 1) * HALF], start=(k == 0), stop=(k == KT - 1))
            last.then_inc(ps_ready, 1)
    return last



def constants(nc, m, a):
    with ExitStack() as ctx:
        sem = lambda n: nc.alloc_semaphore(fresh(n))
        sb = lambda n, s, d=F32: ctx.enter_context(nc.sbuf_tensor(n, s, d))
        rows_arrived, rel_arrived, made, cast = sem("rows_arrived"), sem("rel_arrived"), sem("masks_made"), sem("columns")
        frows_arrived, bias_rows, bias_stored, filled = sem("conv_rows"), sem("bias_rows"), sem("bias_stored"), sem("filled")
        vrows = sb("vector_rows", [VROWS, P])
        frows = sb("conv_rows", [FSPLIT, 2, P])
        rel = sb("rel_bias_rows", [AH, NREL])
        line = sb("bias_line", [AH, BAND + P])
        nowhere = sb("nowhere", [P, T * EXPERTS // P], I32)
        ps = ctx.enter_context(nc.psum_tensor("ps_columns", [P, 3, HALF], F32))
        block = ctx.enter_context(nc.Block())

        @block.sync
        def _(sp):
            for name, (row, n) in VEC.items():
                src = a[name]
                if name == "ssd_conv_w_2":
                    src = src[0].rearrange("k (r c) -> (k r) c", c=P)
                else:
                    src = rows_of(src[0] if len(src.shape) == 2 else src)
                sp.dma_start(vrows[row:row + n, :], src).then_inc(rows_arrived, 16)
            conv = a["ffn_conv_w_2"][0].rearrange("k (r c) -> (k r) c", c=P)
            for s in range(2):
                sp.dma_start(frows[:, s, :], conv[s * FSPLIT:(s + 1) * FSPLIT, :]).then_inc(frows_arrived, 16)
            sp.dma_start(rel[:, :], a["rel_bias_2"][0]).then_inc(rel_arrived, 16)
            m.ring.issue(sp, 0, 2)
            sp.wait_ge(filled, 1)
            sp.dma_start(m.codes.rearrange("(p n) o -> p (n o)", p=P), nowhere[:, :]).then_inc(bias_stored, 16)
            sp.wait_ge(bias_rows, 1)
            for h in range(AH):
                sp.dma_start(m.bias_lines[h], line[h:h + 1, None, :].to_broadcast([1, P, BAND + P])).then_inc(bias_stored, 16)
            sp.wait_ge(bias_stored, 16 * (AH + 1))

        @block.gpsimd
        def _(pool):
            pool.memset(m.ident[:, :], 0.0)
            pool.memset(m.ones[:, :], 1.0)
            pool.memset(m.upto[:, :], 1.0)
            pool.memset(m.after[:, :], 1.0)
            pool.memset(m.before[:, :], 1.0)
            pool.memset(m.chunk_ones[:, :, :], 0.0)
            pool.memset(nowhere[:, :], NOWHERE)
            pool.drain()
            pool.affine_select(out=m.ident[:, :], in_=m.ident[:, :], compare_op=ALU.not_equal, fill=1.0, base=0,
                               pattern=[[-1, P]], channel_multiplier=1)
            pool.affine_select(out=m.upto[:, :], in_=m.upto[:, :], compare_op=ALU.is_ge, fill=0.0, base=0,
                               pattern=[[1, P]], channel_multiplier=-1)
            pool.affine_select(out=m.after[:, :], in_=m.after[:, :], compare_op=ALU.is_gt, fill=0.0, base=0,
                               pattern=[[-1, P]], channel_multiplier=1)
            pool.affine_select(out=m.before[:, :], in_=m.before[:, :], compare_op=ALU.is_gt, fill=0.0, base=0,
                               pattern=[[1, P]], channel_multiplier=-1)
            pool.drain()
            pool.memset(m.upto[0:CH, CH:P], 0.0)
            pool.drain()
            pool.memset(m.after[CH:P, 0:CH], 0.0)
            for c in range(2):
                pool.drain()
                pool.memset(m.chunk_ones[c * CH:(c + 1) * CH, c, :], 1.0)
            pool.drain()
            pool.memset(m.resets[:, :], 1.0)
            pool.drain()
            pool.memset(m.resets[:, :].rearrange("p (n c) -> p n c", c=CH)[:, :, 0:1], 0.0)
            pool.iota(m.expert_iota_i[:, :], pattern=[[1, EXPERTS]], base=0, channel_multiplier=0)
            pool.iota(m.codes_i[:, :], pattern=[[T, 2], [P, TT]], base=0, channel_multiplier=1)
            pool.iota(m.part_iota_i[:, :], pattern=[[0, 1]], base=0, channel_multiplier=1)
            pool.drain()
            pool.tensor_copy(m.expert_iota[:, :], m.expert_iota_i[:, :])
            pool.tensor_copy(m.part_iota[:, :], m.part_iota_i[:, :])
            pool.drain()
            pool.sem_inc(made, 1)
            pool.sem_inc(filled, 1)

        @block.tensor
        def _(pe):
            pe.wait_ge(made, 1)
            pe.wait_ge(rows_arrived, 16 * len(VEC))
            pe.transpose(ps[:, 0, 0:VROWS], vrows[:, :], m.ident[0:VROWS, 0:VROWS])
            pe.wait_ge(frows_arrived, 32)
            pe.transpose(ps[:, 1, 0:FSPLIT], frows[:, 0, :], m.ident[0:FSPLIT, 0:FSPLIT])
            pe.transpose(ps[:, 2, 0:FSPLIT], frows[:, 1, :], m.ident[0:FSPLIT, 0:FSPLIT]).then_inc(cast, 1)

        @block.vector
        def _(dve):
            dve.wait_ge(rel_arrived, 16)
            far = BAND + P - 1 - (NREL - 2)
            dve.memset(line[:, :], 0.0)
            dve.drain()
            dve.tensor_scalar(line[:, 0:far + 1], line[:, 0:far + 1], rel[:, NREL - 1:NREL], None, ALU.add)
            dve.drain()
            dve.tensor_copy(line[:, far:far + NREL - 2], rel[:, NREL - 2:0:-1]).then_inc(bias_rows, 1)
            dve.wait_ge(cast, 1)
            dve.tensor_copy(m.cols[:, :], ps[:, 0, 0:VROWS])
            dve.tensor_copy(m.conv_cols[:, 0:FSPLIT], ps[:, 1, 0:FSPLIT])
            dve.tensor_copy(m.conv_cols[:, FSPLIT:FROWS], ps[:, 2, 0:FSPLIT])
            dve.drain()



def modulation(nc, m, a):
    NB = 6 * D // HALF
    with ExitStack() as ctx:
        sem = lambda n: nc.alloc_semaphore(fresh(n))
        sb = lambda n, s, d=F32: ctx.enter_context(nc.sbuf_tensor(n, s, d))
        c_act = sb("c_act", [P, KT])
        c_wide = sb("c_wide", [P, KT, P])
        mod = m.big[:, 0:6 * D]
        w = [m.big[:, 6 * D + s * KT * HALF:6 * D + (s + 1) * KT * HALF].rearrange("p (k n) -> p k n", k=KT)
             for s in range(4)]
        b_row = sb("b_ada_row", [1, 6 * D])
        ps = ctx.enter_context(nc.psum_tensor("ps_mod", [P, 4, HALF], F32))
        pst = ctx.enter_context(nc.psum_tensor("ps_mod_t", [P, 4, HALF], F32))
        loaded = [sem(f"ada_loaded{s}") for s in range(4)]
        bias_row, activated, wide = sem("ada_bias"), sem("c_activated"), sem("c_widened")
        ps_ready, ps_free, turned = sem("mod_ready"), sem("mod_free"), sem("mod_turned")
        block = ctx.enter_context(nc.Block())

        @block.sync
        def _(sp):
            sp.dma_start(b_row[:, :], a["b_ada_2"]).then_inc(bias_row, 16)
            for b in range(NB):
                if b >= 4:
                    sp.wait_ge(ps_ready, b - 3)
                sp.dma_start(w[b % 4], a["w_ada_2"][0][:, b * HALF:(b + 1) * HALF]
                             .rearrange("(k p) n -> p k n", p=P)).then_inc(loaded[b % 4], 16)

        @block.scalar
        def _(act):
            row, n = VEC["c_2"]
            act.activation(c_act[:, :], m.cols[:, row:row + n], ACT.Silu).then_inc(activated, 1)

        @block.vector
        def _(dve):
            dve.wait_ge(activated, 1)
            dve.tensor_copy(c_wide[:, :, :], c_act[:, :, None].to_broadcast([P, KT, P])).then_inc(wide, 1)
            for b in range(NB):
                dve.wait_ge(ps_ready, b + 1)
                dve.tensor_copy(mod[:, b * HALF:(b + 1) * HALF], ps[:, b % 4, :]).then_inc(ps_free, 1)
            dve.drain()
            dve.tensor_copy(m.gate_mix[:, :], mod[:, 2 * D:3 * D])
            dve.tensor_copy(m.gate_ffn[:, :], mod[:, 5 * D:6 * D])
            for i, (dst, gain) in enumerate(((m.shift_mix, None), (m.scale_mix, "norm_mix_w_2"),
                                             (m.shift_ffn, None), (m.scale_ffn, "norm_ffn_w_2"))):
                for half in range(2):
                    n = 2 * i + half
                    dve.wait_ge(turned, n + 1)
                    src = pst[:, n % 4, :].rearrange("p (j c) -> p j c", j=4)[:, :, 0:1]
                    out = dst[:, 4 * half:4 * half + 4, None]
                    if gain is None:
                        dve.tensor_copy(out, src).then_inc(ps_free, 1)
                    else:
                        row = VEC[gain][0] + 4 * half
                        dve.tensor_scalar(out, src, 1.0, None, ALU.add).then_inc(ps_free, 1)
                        dve.drain()
                        dve.tensor_tensor(out, out, m.cols[:, row:row + 4, None], ALU.mult)
            dve.drain()

        @block.tensor
        def _(pe):
            pe.wait_ge(wide, 1)
            pe.wait_ge(bias_row, 16)
            for b in range(NB):
                pe.wait_ge(loaded[b % 4], 16 * (b // 4 + 1))
                if b >= 4:
                    pe.wait_ge(ps_free, b - 3)
                for k in range(KT):
                    pe.matmul(ps[:, b % 4, :], c_wide[:, k, :], w[b % 4][:, k, :], start=(k == 0), stop=False)
                pe.matmul(ps[:, b % 4, :], m.ones[0:1, :], b_row[:, b * HALF:(b + 1) * HALF],
                          start=False, stop=True).then_inc(ps_ready, 1)
            pe.wait_ge(ps_free, NB)
            for i, part in enumerate((0, 1, 3, 4)):
                for half in range(2):
                    n = 2 * i + half
                    if n >= 4:
                        pe.wait_ge(ps_free, NB + n - 3)
                    for j in range(4):
                        at = part * D + (4 * half + j) * P
                        last = pe.transpose(pst[:, n % 4, j * P:(j + 1) * P], mod[:, at:at + P], m.ident[:, :])
                    last.then_inc(turned, 1)



def gla_projections(nc, m, a):
    hT, qk, v, r = m.b1, m.b2, m.b3, m.b4
    with ExitStack() as ctx:
        sem = lambda n: nc.alloc_semaphore(fresh(n))
        sb = lambda n, s, d=F32: ctx.enter_context(nc.sbuf_tensor(n, s, d))
        w_lr = sb("w_low_rank", [P, KT, RANK])
        w_gate = sb("w_gate", [RANK, GH * GDK])
        lrT = sb("low_rankT", [RANK, T])
        mag = m.b3[:, 0:GH, :]
        gates = m.gates
        ps = ctx.enter_context(nc.psum_tensor("ps_gla_in", [P, 4, HALF], F32))
        ps_lr = ctx.enter_context(nc.psum_tensor("ps_low_rank", [P, 2, HALF], F32))
        small_loaded, ps_ready, ps_free = sem("gate_weights"), sem("proj_ready"), sem("proj_free")
        lr_ready, lr_sb, gate_ready, gate_free = sem("lr_ready"), sem("lr_in_sbuf"), sem("gate_ready"), sem("gate_free")
        biased, exped, logged, scanned = sem("biased"), sem("exped"), sem("logged"), sem("scanned")
        block = ctx.enter_context(nc.Block())
        a_col = 2 * GH * GDK + GH * GDV

        @block.sync
        def _(sp):
            with nc.allow_non_contiguous_dma(reason="sixteen columns of w_in"):
                sp.dma_start(w_lr[:, :, :], a["gla_w_in"][0][:, a_col:a_col + RANK]
                             .rearrange("(k p) n -> p k n", p=P)).then_inc(small_loaded, 16)
            sp.dma_start(w_gate[:, :], a["gla_w_gate"][0]).then_inc(small_loaded, 16)
            m.ring.issue(sp, 2, 8)

        @block.tensor
        def _(pe):
            pe.wait_ge(small_loaded, 32)
            for half in range(2):
                for k in range(KT):
                    last = pe.matmul(ps_lr[0:RANK, half, :], w_lr[:, k, :], hT[:, k, half * HALF:(half + 1) * HALF],
                                     start=(k == 0), stop=(k == KT - 1))
            last.then_inc(lr_ready, 1)
            pe.wait_ge(lr_sb, 1)
            for n in range(2 * GH):
                if n >= 2:
                    pe.wait_ge(gate_free, n - 1)
                pe.matmul(ps_lr[:, n % 2, :], w_gate[:, (n // 2) * P:(n // 2 + 1) * P],
                          lrT[:, (n % 2) * HALF:(n % 2 + 1) * HALF], start=True, stop=True).then_inc(gate_ready, 1)
            for b in range(2):
                pe.wait_ge(m.ring.loaded[b], m.ring.loads_before(b))
                gemm_channels(pe, m.ring, b, range(4), hT, ps, 8 * b, ps_ready, ps_free, 4)
            with pe.Fori(0, 2) as i:
                for s in range(2):
                    pe.wait_ge(m.ring.loaded[s], i * 16 + 16 * 2)
                    gemm_tokens(pe, m.ring, s, hT, ps, 16 + i * 16 + 8 * s, ps_ready, ps_free, 4)

        @block.vector
        def _(dve):
            dve.wait_ge(lr_ready, 1)
            dve.tensor_copy(lrT[:, :].rearrange("p (h n) -> p h n", h=2), ps_lr[0:RANK, :, :]).then_inc(lr_sb, 1)
            row = VEC["gla_b_gate"][0]
            for n in range(2 * GH):
                dve.wait_ge(gate_ready, n + 1)
                dve.tensor_scalar(gates[:, n // 2, (n % 2) * HALF:(n % 2 + 1) * HALF], ps_lr[:, n % 2, :],
                                  m.cols[:, row + n // 2:row + n // 2 + 1], None, ALU.add).then_inc(gate_free, 1)
            dve.drain()
            dve.tensor_scalar(mag[:, :, :], gates[:, :, :], -1.0, None, ALU.mult)
            dve.drain()
            dve.tensor_tensor(mag[:, :, :], mag[:, :, :], gates[:, :, :], ALU.max).then_inc(biased, 1)
            dve.wait_ge(logged, 1)
            dve.tensor_scalar(gates[:, :, :], gates[:, :, :], 0.0, None, ALU.min)
            dve.drain()
            dve.tensor_tensor(gates[:, :, :], gates[:, :, :], mag[:, :, :], ALU.subtract)
            dve.drain()
            dve.tensor_scalar(mag[:, :, :], gates[:, :, :], 1.0 / TAU, None, ALU.mult)
            dve.drain()
            for h in range(GH):
                dve.tensor_tensor_scan(gates[:, h, :], m.resets[:, :], mag[:, h, :], 0.0, ALU.mult, ALU.add)\
                    .then_inc(scanned, 1)
            dve.drain()

        @block.scalar
        def _(act):
            act.sem_inc(ps_free, 4)
            act.wait_ge(biased, 1)
            act.activation(mag[:, :, :], mag[:, :, :], ACT.Exp, scale=-1.0)
            act.drain()
            act.activation(mag[:, :, :], mag[:, :, :], ACT.Ln, bias=1.0).then_inc(logged, 1)
            for n in range(16):
                act.wait_ge(ps_ready, n + 1)
                c = n // 2
                out = qk[:, c, (n % 2) * HALF:(n % 2 + 1) * HALF]
                if c < GH:
                    act.mul(out, ps[:, n % 4, :], float(GDK) ** -0.5).then_inc(ps_free, 1)
                else:
                    act.copy(out, ps[:, n % 4, :]).then_inc(ps_free, 1)
                if n % 8 == 7:
                    m.ring.release(act)
            act.wait_ge(scanned, GH)
            with act.Fori(0, 2) as i:
                for j in range(16):
                    act.wait_ge(ps_ready, i * 16 + 17 + j)
                    act.copy(m.vr[:, i * TT + j % 8, (j // 8) * HALF:(j // 8 + 1) * HALF], ps[:, j % 4, :])\
                        .then_inc(ps_free, 1)
                    if j % 8 == 7:
                        m.ring.release(act)


def gla_chunks(nc, m, a):
    qk, v, gates = m.b2, m.b3, m.gates
    with ExitStack() as ctx:
        sem = lambda n: nc.alloc_semaphore(fresh(n))
        sb = lambda n, s, d=F32: ctx.enter_context(nc.sbuf_tensor(n, s, d))
        W = GH * P
        diff = [m.b1[:, 0:1, s * W:(s + 1) * W].rearrange("p o (h n) -> p (o h) n", h=GH) for s in range(2)]
        e = {n: m.b1[:, 1 + i // 2, (i % 2) * W:(i % 2 + 1) * W].rearrange("p (h n) -> p h n", h=GH)
             for i, n in enumerate(("up", "down", "full", "left"))}
        qi, ki, qn, ks = (m.b1[:, 3 + i // 2, (i % 2) * W:(i % 2 + 1) * W].rearrange("p (h n) -> p h n", h=GH)
                          for i in range(4))
        v_now = m.b1[:, 5, :]
        decay = sb("chunk_decay", [P, GH, 2])
        att = sb("att", [P, 2, P])
        kst = sb("k_state_tokens", [P, 2, P])
        S = sb("state", [P, GH, GDV])
        S_mid = sb("state_mid", [P, GH, GDV])
        psA = ctx.enter_context(nc.psum_tensor("ps_att", [P, 2, HALF], F32))
        psO = ctx.enter_context(nc.psum_tensor("ps_o", [P, 2, HALF], F32))
        psU = ctx.enter_context(nc.psum_tensor("ps_update", [P, 2, 2, HALF], F32))
        diffs, exps, scaled, v_copied = sem("diffs"), sem("exps"), sem("scaled"), sem("v_copied")
        att_ready, att_masked, kst_sb = sem("att_ready"), sem("att_masked"), sem("kst_sb")
        upd_ready, mid_ready, state_ready = sem("update_ready"), sem("mid_state"), sem("state_ready")
        o_ready, o_copied = sem("o_ready"), sem("o_copied")
        block = ctx.enter_context(nc.Block())

        @block.vector
        def _(dve):
            dve.memset(S[:, :, :], 0.0).then_inc(state_ready, GH)
            dve.memset(S_mid[:, :, :], 0.0)
            dve.drain()
            with dve.Fori(0, TT) as p:
                now = lambda buf, c0: buf[:, c0:c0 + GH, bass.ds(p * P, P)]
                g4 = now(gates, 0).rearrange("p h (c n) -> p h c n", c=2)
                d0 = diff[0].rearrange("p h (c n) -> p h c n", c=2)
                d1 = diff[1].rearrange("p h (c n) -> p h c n", c=2)
                for h in range(GH):
                    mid = g4[:, h, :, CH // 2:CH // 2 + 1].to_broadcast([P, 2, CH])
                    end = g4[:, h, :, CH - 1:CH].to_broadcast([P, 2, CH])
                    dve.tensor_tensor(d0[:, h], g4[:, h], mid, ALU.subtract)
                    last = dve.tensor_tensor(d1[:, h], end, g4[:, h], ALU.subtract)
                last.then_inc(diffs, 1)
                dve.wait_ge(exps, p + 1)
                dve.tensor_tensor(qi, now(qk, 0), e["up"], ALU.mult)
                dve.tensor_tensor(ki, now(qk, GH), e["down"], ALU.mult)
                dve.tensor_tensor(qn, now(qk, 0), e["full"], ALU.mult)
                dve.tensor_tensor(ks, now(qk, GH), e["left"], ALU.mult).then_inc(scaled, 1)
                for h in range(GH):
                    u = h % 2
                    dve.wait_ge(att_ready, p * GH + h + 1)
                    dve.tensor_tensor(att[:, u, :], psA[:, u, 0:P], m.upto[:, :], ALU.mult).then_inc(att_masked, 1)
                    dve.tensor_copy(kst[:, u, :], psA[:, u, P:2 * P]).then_inc(kst_sb, 1)
                    dve.wait_ge(upd_ready, p * GH + h + 1)
                    dve.scalar_tensor_tensor(S_mid[:, h, :], S[:, h, :], decay[:, h, 0:1], psU[:, u, 0, 0:GDV],
                                             ALU.mult, ALU.add).then_inc(mid_ready, 1)
                    dve.drain()
                    dve.wait_ge(o_ready, p * GH + h + 1)
                    dve.scalar_tensor_tensor(S[:, h, :], S_mid[:, h, :], decay[:, h, 1:2],
                                             psU[:, u, 1, 0:GDV], ALU.mult, ALU.add).then_inc(state_ready, 1)

        @block.scalar
        def _(act):
            act.sem_inc(o_copied, 2)
            with act.Fori(0, TT) as p:
                act.copy(v_now, v[:, p, :]).then_inc(v_copied, 1)
                act.wait_ge(diffs, p + 1)
                g_now = gates[:, :, bass.ds(p * P, P)]
                act.activation(e["up"], diff[0], ACT.Exp)
                act.activation(e["down"], diff[0], ACT.Exp, scale=-1.0)
                act.activation(e["full"], g_now, ACT.Exp)
                act.activation(e["left"], diff[1], ACT.Exp)
                act.activation(decay[:, :, :],
                               g_now.rearrange("p h (c n) -> p h c n", c=2)[:, :, :, CH - 1], ACT.Exp).then_inc(exps, 1)
                for h in range(GH):
                    act.wait_ge(o_ready, p * GH + h + 1)
                    carry(act, m)
                    act.copy(v[:, p, h * GDV:(h + 1) * GDV], psO[:, h % 2, 0:GDV]).then_inc(o_copied, 1)

        @block.tensor
        def _(pe):
            with pe.Fori(0, TT) as p:
                pe.wait_ge(scaled, p + 1)
                pe.wait_ge(v_copied, p + 1)
                for h in range(GH):
                    u = h % 2
                    vh = v_now[:, h * GDV:(h + 1) * GDV]
                    pe.matmul(psA[:, u, 0:P], ki[:, h, :], qi[:, h, :], start=True, stop=True)
                    pe.transpose(psA[:, u, P:2 * P], ks[:, h, :], m.ident[:, :]).then_inc(att_ready, 1)
                    pe.wait_ge(kst_sb, p * GH + h + 1)
                    pe.wait_ge(state_ready, p * GH + h + GH - 1)
                    for c in range(2):
                        last = pe.matmul(psU[:, u, c, 0:GDV], kst[c * CH:(c + 1) * CH, u, :],
                                         vh[c * CH:(c + 1) * CH, :], start=True, stop=True)
                    last.then_inc(upd_ready, 1)
                    pe.wait_ge(att_masked, p * GH + h + 1)
                    pe.wait_ge(o_copied, p * GH + h + 1)
                    pe.wait_ge(state_ready, p * GH + h + 1)
                    for c, state in enumerate((S, S_mid)):
                        part = slice(c * CH, (c + 1) * CH)
                        pe.matmul(psO[part, u, 0:GDV], att[:, u, part], vh, start=True, stop=False)
                        if c == 1:
                            pe.wait_ge(mid_ready, p * GH + h + 1)
                        last = pe.matmul(psO[part, u, 0:GDV], qn[:, h, part], state[:, h, :], start=False, stop=True)
                    last.then_inc(o_ready, 1)


def gla_output(nc, m, a):
    o, r, yT = m.b3, m.b4, m.b1
    with ExitStack() as ctx:
        sem = lambda n: nc.alloc_semaphore(fresh(n))
        sb = lambda n, s, d=F32: ctx.enter_context(nc.sbuf_tensor(n, s, d))
        ss, root, inv = sb("o_ss", [P, TT * GH]), sb("o_root", [P, TT * GH]), sb("o_inv", [P, TT * GH])
        junk = sb("o_squares", [P, GDV])
        gain = sb("out_norm", [P, GDV])
        ps = ctx.enter_context(nc.psum_tensor("ps_yT", [P, 4, HALF], F32))
        gain_arrived, summed, squares, roots, gated = (sem(n) for n in ("gain_arrived", "o_summed", "o_meaned", "o_rooted", "gated"))
        normed, ps_ready, ps_free = sem("o_normed"), sem("yT_ready"), sem("yT_free")
        block = ctx.enter_context(nc.Block())

        @block.sync
        def _(sp):
            sp.dma_start(gain[:, :], spread(a["gla_out_norm"])).then_inc(gain_arrived, 16)

        @block.scalar
        def _(act):
            for t in range(TT):
                for h in range(GH):
                    act.activation(junk[:, :], o[:, t, h * GDV:(h + 1) * GDV], ACT.Square,
                                   accum_out=ss[:, t * GH + h:t * GH + h + 1]).then_inc(summed, 1)
                    act.drain()
            inverse_rms(act, None, ss[:, :], root[:, :], None, GDV, squares, roots)
            for t in range(TT):
                act.activation(r[:, t, :], r[:, t, :], ACT.Silu).then_inc(gated, 1)

        @block.vector
        def _(dve):
            dve.wait_ge(summed, TT * GH)
            dve.tensor_scalar(ss[:, :], ss[:, :], 1.0 / GDV, EPS, ALU.mult, ALU.add).then_inc(squares, 1)
            inverse_rms(None, dve, None, root[:, :], inv[:, :], GDV, squares, roots)
            dve.wait_ge(gain_arrived, 16)
            for t in range(TT):
                for h in range(GH):
                    oh = o[:, t, h * GDV:(h + 1) * GDV]
                    dve.scalar_tensor_tensor(oh, oh, inv[:, t * GH + h:t * GH + h + 1], gain[:, :], ALU.mult, ALU.mult)
            dve.drain()
            for t in range(TT):
                dve.wait_ge(gated, t + 1)
                dve.tensor_tensor(o[:, t, :], o[:, t, :], r[:, t, :], ALU.mult).then_inc(normed, 1)
            transposes_out(dve, yT, lambda k: None, None, ps, ps_ready, ps_free)

        @block.tensor
        def _(pe):
            transposes(pe, m, o, lambda e: e.wait_ge(normed, TT), ps, ps_ready, ps_free)


def project_back(nc, m, actT, resid, resid_src, first, prefetch, gate=None):
    with ExitStack() as ctx:
        sem = lambda n: nc.alloc_semaphore(fresh(n))
        ps = ctx.enter_context(nc.psum_tensor(fresh("ps_back"), [P, 4, HALF], F32))
        temp = ctx.enter_context(nc.sbuf_tensor(fresh("gated"), [P, 2, HALF], F32))
        arrived = [sem(f"resid{t}") for t in range(TT)]
        ps_ready, ps_free = sem("back_ready"), sem("back_free")
        block = ctx.enter_context(nc.Block())

        @block.sync
        def _(sp):
            for t in range(TT):
                sp.dma_start(resid[:, t, :], resid_src[t * P:(t + 1) * P, :]).then_inc(arrived[t], 16)
            m.ring.issue(sp, *prefetch)

        @block.tensor
        def _(pe):
            for b in range(2):
                pe.wait_ge(m.ring.loaded[b], m.ring.loads_before(first + b))
                gemm_tokens(pe, m.ring, b, actT, ps, 8 * b, ps_ready, ps_free, 4)

        @block.vector
        def _(dve):
            dve.sem_inc(ps_free, 4)
            for n in range(2 * TT):
                t, cols = n % TT, slice((n // TT) * HALF, (n // TT + 1) * HALF)
                if n < TT:
                    dve.wait_ge(arrived[t], 16)
                dve.wait_ge(ps_ready, n + 1)
                if n % TT == TT - 1:
                    m.ring.release(dve)
                if gate is None:
                    dve.tensor_tensor(resid[:, t, cols], ps[:, n % 4, :], resid[:, t, cols], ALU.add).then_inc(ps_free, 1)
                else:
                    dve.tensor_tensor(temp[:, n % 2, :], ps[:, n % 4, :], gate[:, cols], ALU.mult).then_inc(ps_free, 1)
                    dve.drain()
                    dve.tensor_tensor(resid[:, t, cols], temp[:, n % 2, :], resid[:, t, cols], ALU.add)
            dve.drain()



UNROLL = 4


def load_expert(sp, m, a, e, u):
    for i, w in enumerate(("moe_w1", "moe_w3")):
        sp.dma_start(m.w13[u][:, i], a[w][0, e].rearrange("(k p) n -> p k n", p=P)).then_inc(m.w13_loaded[u], 16)
    sp.dma_start(m.w2[u], a["moe_w2"][0, e].rearrange("(k p) n -> p k n", p=P)).then_inc(m.w2_loaded[u], 16)


def router(nc, m, a):
    hT = m.b1
    NL = GROUPS + EXPERTS
    with ExitStack() as ctx:
        sem = lambda n: nc.alloc_semaphore(fresh(n))
        sb = lambda n, s, d=F32: ctx.enter_context(nc.sbuf_tensor(n, s, d))
        w = sb("w_router", [P, KT, NL])
        lg = sb("logits", [P, TT, NL])
        gmx, emx = sb("group_max", [P, TT, 8]), sb("expert_max", [P, TT, 8])
        gix, eix = sb("group_index", [P, TT, 8], U32), sb("expert_index", [P, TT, 8], U32)
        gid, eid = sb("group_id", [P, TT]), sb("expert_id", [P, 2, TT])
        in_group = sb("in_group", [P, TT, GROUPS])
        prod = sb("selected", [P, TT, GROUPS, PER_GROUP])
        el = sb("group_logits", [P, TT, PER_GROUP])
        gexp, gsum, ez, den = sb("group_exp", [P, TT, GROUPS]), sb("group_sum", [P, TT]), sb("second_exp", [P, TT]), sb("pair_sum", [P, TT])
        one = [sb(f"one_hot{k}", [P, TT, EXPERTS]) for k in range(2)]
        both = sb("assigned", [P, TT, EXPERTS])
        rank, dest = sb("rank", [P, 2, TT]), sb("slot_row", [P, 2 * TT], I32)
        cnt, extra, cum = sb("counts", [P, EXPERTS]), sb("extra_blocks", [P, EXPERTS]), sb("extra_cum", [P, EXPERTS])
        le, per_part, info_i = sb("passed", [P, EXPERTS]), sb("block_info", [P, 4]), sb("block_info_i", [P, 2], I32)
        ps = ctx.enter_context(nc.psum_tensor("ps_logits", [P, 2, HALF], F32))
        psp = ctx.enter_context(nc.psum_tensor("ps_rank", [P, TT, EXPERTS], F32))
        psc = ctx.enter_context(nc.psum_tensor("ps_counts", [P, EXPERTS], F32))
        w_arrived, logits_ready, shifted, exped = sem("router_w"), sem("logits_ready"), sem("shifted"), sem("exped")
        assigned, ranked, placed, scattered, tables = sem("assigned_s"), sem("ranked"), sem("placed"), sem("codes_scattered"), sem("tables")
        listed, info_stored, diffed = sem("listed"), sem("info_stored"), sem("diffed")
        block = ctx.enter_context(nc.Block())

        @block.sync
        def _(sp):
            sp.dma_start(w[:, :, 0:GROUPS], a["moe_w_group"][0].rearrange("(k p) n -> p k n", p=P)).then_inc(w_arrived, 16)
            sp.dma_start(w[:, :, GROUPS:NL], a["moe_w_expert"][0].rearrange("(k p) n -> p k n", p=P)).then_inc(w_arrived, 16)
            for e in range(2):
                load_expert(sp, m, a, e, e)
            sp.wait_ge(scattered, 16 * 2 * TT)
            sp.dma_start(m.scatter_idx[:, :], m.codes[0:SLOTS * EXPERTS, :].rearrange("(s e) o -> s (e o)", s=SLOTS))\
                .then_inc(tables, 16)
            sp.wait_ge(listed, 1)
            sp.dma_start(m.info_dram, info_i[:, :]).then_inc(info_stored, 16)
            sp.wait_ge(info_stored, 16)
            sp.dma_start(m.info_row[:, :], m.info_dram.rearrange("(o p) c -> o (p c)", o=1)).then_inc(info_stored, 16)
            sp.wait_ge(info_stored, 32)

        @block.tensor
        def _(pe):
            pe.wait_ge(w_arrived, 32)
            for t in range(TT):
                for k in range(KT):
                    last = pe.matmul(ps[:, t // 4, (t % 4) * NL:(t % 4 + 1) * NL], hT[:, k, t * P:(t + 1) * P], w[:, k, :],
                                     start=(k == 0), stop=(k == KT - 1))
            last.then_inc(logits_ready, 1)
            pe.wait_ge(assigned, 1)
            for t in range(TT):
                for s in range(t):
                    pe.matmul(psp[:, t, :], m.ones[:, :], both[:, s, :], start=(s == 0), stop=False)
                pe.matmul(psp[:, t, :], m.before[:, :], both[:, t, :], start=(t == 0), stop=True)
            for t in range(TT):
                last = pe.matmul(psc[:, :], m.ones[:, :], both[:, t, :], start=(t == 0), stop=(t == TT - 1))
            last.then_inc(ranked, 1)

        @block.scalar
        def _(act):
            act.wait_ge(shifted, 1)
            act.activation(gexp[:, :, :], gexp[:, :, :], ACT.Exp).then_inc(exped, 1)
            act.wait_ge(diffed, 1)
            act.activation(ez[:, :], ez[:, :], ACT.Exp).then_inc(exped, 1)

        @block.vector
        def _(dve):
            dve.wait_ge(logits_ready, 1)
            for h in range(2):
                dve.tensor_copy(lg[:, 4 * h:4 * h + 4, :], ps[:, h, 0:4 * NL].rearrange("p (t n) -> p t n", t=4))
            dve.drain()
            for t in range(TT):
                dve.max(gmx[:, t, :], lg[:, t, 0:GROUPS])
            dve.drain()
            for t in range(TT):
                dve.max_index(gix[:, t, :], gmx[:, t, :], lg[:, t, 0:GROUPS])
            dve.tensor_tensor(gexp[:, :, :], lg[:, :, 0:GROUPS], gmx[:, :, 0:1].to_broadcast([P, TT, GROUPS]),
                              ALU.subtract).then_inc(shifted, 1)
            dve.drain()
            dve.tensor_copy(gid[:, :], gix[:, :, 0])
            dve.drain()
            dve.tensor_tensor(in_group[:, :, :], m.expert_iota[:, None, 0:GROUPS].to_broadcast([P, TT, GROUPS]),
                              gid[:, :, None].to_broadcast([P, TT, GROUPS]), ALU.is_equal)
            dve.drain()
            dve.tensor_tensor(prod[:, :, :, :], lg[:, :, GROUPS:NL].rearrange("p t (g e) -> p t g e", g=GROUPS),
                              in_group[:, :, :, None].to_broadcast([P, TT, GROUPS, PER_GROUP]), ALU.mult)
            dve.drain()
            dve.reduce_sum(el[:, :, :], prod[:, :, :, :].rearrange("p t g e -> p t e g"), axis=AX.X)
            dve.drain()
            for t in range(TT):
                dve.max(emx[:, t, :], el[:, t, :])
            dve.drain()
            for t in range(TT):
                dve.max_index(eix[:, t, :], emx[:, t, :], el[:, t, :])
            dve.tensor_tensor(ez[:, :], emx[:, :, 1], emx[:, :, 0], ALU.subtract).then_inc(diffed, 1)
            dve.drain()
            for k in range(2):
                dve.tensor_copy(eid[:, k, :], eix[:, :, k])
            dve.drain()
            for k in range(2):
                dve.scalar_tensor_tensor(eid[:, k, :], gid[:, :], float(PER_GROUP), eid[:, k, :], ALU.mult, ALU.add)
            dve.drain()
            for k in range(2):
                dve.tensor_tensor(one[k][:, :, :], m.expert_iota[:, None, :].to_broadcast([P, TT, EXPERTS]),
                                  eid[:, k, :, None].to_broadcast([P, TT, EXPERTS]), ALU.is_equal)
            dve.drain()
            dve.tensor_tensor(both[:, :, :], one[0][:, :, :], one[1][:, :, :], ALU.add).then_inc(assigned, 1)
            dve.wait_ge(exped, 2)
            dve.reduce_sum(gsum[:, :], gexp[:, :, :], axis=AX.X)
            dve.tensor_scalar(den[:, :], ez[:, :], 1.0, None, ALU.add)
            dve.drain()
            dve.tensor_tensor(den[:, :], den[:, :], gsum[:, :], ALU.mult)
            dve.drain()
            dve.reciprocal(m.gates2[:, 0, :], den[:, :])
            dve.drain()
            dve.tensor_tensor(m.gates2[:, 1, :], m.gates2[:, 0, :], ez[:, :], ALU.mult)
            dve.wait_ge(ranked, 1)
            for k in range(2):
                dve.tensor_tensor(one[k][:, :, :], psp[:, :, :], one[k][:, :, :], ALU.mult)
            dve.drain()
            for k in range(2):
                dve.reduce_sum(rank[:, k, :], one[k][:, :, :], axis=AX.X)
            dve.drain()
            dve.scalar_tensor_tensor(dest[:, :].rearrange("p (k t) -> p k t", k=2), rank[:, :, :], float(EXPERTS),
                                     eid[:, :, :], ALU.mult, ALU.add).then_inc(placed, 1)
            dve.tensor_copy(cnt[:, :], psc[:, :])
            dve.memset(extra[:, :], 0.0)
            dve.drain()
            for j in range(1, T // SLOTS):
                dve.scalar_tensor_tensor(extra[:, :], cnt[:, :], float(SLOTS * j), extra[:, :], ALU.is_gt, ALU.add)
                dve.drain()
            dve.tensor_tensor_scan(cum[:, :], m.ones[:, 0:EXPERTS], extra[:, :], 0.0, ALU.mult, ALU.add)
            dve.drain()
            dve.tensor_scalar(le[:, :], cum[:, :], m.part_iota[:, 0:1], None, ALU.is_le)
            dve.tensor_copy(m.n_extra[:, :], cum[0:1, EXPERTS - 1:EXPERTS])
            dve.drain()
            dve.reduce_sum(per_part[:, 0:1], le[:, :], axis=AX.X)
            dve.tensor_tensor(extra[:, :], extra[:, :], le[:, :], ALU.mult)
            dve.drain()
            dve.reduce_sum(per_part[:, 1:2], extra[:, :], axis=AX.X)
            dve.drain()
            dve.tensor_tensor(per_part[:, 2:3], m.part_iota[:, 0:1], per_part[:, 1:2], ALU.subtract)
            dve.drain()
            dve.tensor_scalar(per_part[:, 3:4], per_part[:, 2:3], 1.0, float(SLOTS * EXPERTS), ALU.add, ALU.mult)
            dve.drain()
            dve.tensor_tensor(info_i[:, 1:2], per_part[:, 3:4], per_part[:, 0:1], ALU.add)
            dve.tensor_copy(info_i[:, 0:1], per_part[:, 0:1]).then_inc(listed, 1)
            dve.wait_ge(tables, 16)
            code_tokens(dve, m.gather_idx[:, :], m.scatter_idx[:, :])

        @block.gpsimd
        def _(pool):
            pool.wait_ge(placed, 1)
            for n in range(2 * TT):
                pool.indirect_dma_start(m.codes, bass.IndirectOffsetOnAxis(dest[:, n:n + 1], 0), m.codes_i[:, n:n + 1],
                                        None).then_inc(scattered, 16)


def code_tokens(dve, tokens, codes):
    dve.tensor_scalar(tokens, codes, float(T), -float(T), ALU.is_ge, ALU.mult)
    dve.drain()
    dve.tensor_tensor(tokens, tokens, codes, ALU.add)
    dve.drain()


class ExpertBuffers:

    def __init__(self, nc, ctx):
        sb = lambda n, s, d=F32: ctx.enter_context(nc.sbuf_tensor(fresh(n), s, d))
        self.xg = [sb("gathered", [SLOTS, D]) for _ in range(2)]
        self.y = [sb("expert_out", [SLOTS, D]) for _ in range(2)]
        self.xT = [sb("gatheredT", [P, KT, SLOTS]) for _ in range(2)]
        self.sil = [sb("silu", [P, 2, SLOTS]) for _ in range(2)]
        self.hid = [sb("hidden", [P, 2, SLOTS]) for _ in range(2)]
        self.gi = [sb("gather_now", [SLOTS, 1], I32) for _ in range(2)]
        self.si = [sb("scatter_now", [SLOTS, 1], I32) for _ in range(2)]
        pb = lambda n, s: ctx.enter_context(nc.psum_tensor(fresh(n), s, F32))
        self.psT, self.psH, self.psY = pb("ps_xT", [P, 2, HALF]), pb("ps_hid", [P, 2, HALF]), pb("ps_y", [P, 2, 2, HALF])


def expert_turn(pe, m, B, s):
    for k in range(KT):
        last = pe.transpose(B.psT[:, s, k * SLOTS:(k + 1) * SLOTS], B.xg[s][:, k * P:(k + 1) * P],
                            m.ident[0:SLOTS, 0:SLOTS])
    return last


def expert_up(pe, m, B, s, u):
    for f in range(4):
        for k in range(KT):
            last = pe.matmul(B.psH[:, s, f * SLOTS:(f + 1) * SLOTS], m.w13[u][:, f // 2, k, (f % 2) * P:(f % 2 + 1) * P],
                             B.xT[s][:, k, :], start=(k == 0), stop=(k == KT - 1))
    return last


def expert_down(pe, m, B, s, u):
    for h in range(2):
        for f in range(2):
            last = pe.matmul(B.psY[0:SLOTS, s, h, :], B.hid[s][:, f, :], m.w2[u][:, f, h * HALF:(h + 1) * HALF],
                             start=(f == 0), stop=(f == 1))
    return last


def expert_xT(dve, m, B, s):
    row = VEC["ffn_norm"][0]
    return dve.tensor_tensor(B.xT[s][:, :, :], B.psT[:, s, :].rearrange("p (k n) -> p k n", k=KT),
                             m.cols[:, row:row + KT, None].to_broadcast([P, KT, SLOTS]), ALU.mult)


def expert_silu(act, B, s):
    return act.activation(B.sil[s][:, :, :], B.psH[:, s, 0:2 * SLOTS].rearrange("p (f n) -> p f n", f=2), ACT.Silu)


def expert_hidden(dve, B, s):
    return dve.tensor_tensor(B.hid[s][:, :, :], B.psH[:, s, 2 * SLOTS:4 * SLOTS].rearrange("p (f n) -> p f n", f=2),
                             B.sil[s][:, :, :], ALU.mult)


def gather_tokens(pool, m, B, s):
    return pool.indirect_dma_start(B.xg[s][:, :], None, m.xn_dram, bass.IndirectOffsetOnAxis(B.gi[s][:, 0:1], 0),
                                   bounds_check=T - 1, oob_is_err=False)


def scatter_tokens(pool, m, B, s):
    return pool.indirect_dma_start(m.contrib, bass.IndirectOffsetOnAxis(B.si[s][:, 0:1], 0), B.y[s][:, :], None,
                                   bounds_check=2 * T - 1, oob_is_err=False)


def experts(nc, m, a):
    with ExitStack() as ctx:
        sem = lambda n: nc.alloc_semaphore(fresh(n))
        B = ExpertBuffers(nc, ctx)
        gathered = [sem(f"gathered{s}") for s in range(2)]
        scattered = [sem(f"scattered{s}") for s in range(2)]
        gi_ready, turned, xT_sb, up_done, silu_done, hid_done, down_done = (
            sem(n) for n in ("gather_index", "turned", "xT_in_sbuf", "up_done", "silu_done", "hid_done", "down_done"))
        y_sb = [sem(f"y_half{h}_in_sbuf") for h in range(2)]
        block = ctx.enter_context(nc.Block())
        ITERS = EXPERTS // UNROLL

        @block.sync
        def _(sp):
            for e in range(2, UNROLL):
                load_expert(sp, m, a, e, e)
            with sp.Fori(0, ITERS - 1) as i:
                for u in range(UNROLL):
                    e = i * UNROLL + (UNROLL + u)
                    sp.wait_ge(up_done, i * UNROLL + (u + 1))
                    for j, w in enumerate(("moe_w1", "moe_w3")):
                        sp.dma_start(m.w13[u][:, j], a[w][0, e].rearrange("(k p) n -> p k n", p=P)).then_inc(m.w13_loaded[u], 16)
                    sp.wait_ge(down_done, i * UNROLL + (u + 1))
                    sp.dma_start(m.w2[u], a["moe_w2"][0, e].rearrange("(k p) n -> p k n", p=P)).then_inc(m.w2_loaded[u], 16)

        def over_experts(engine, step):
            for u in range(UNROLL):
                step(u, 0, u, False)
            with engine.Fori(1, ITERS - 1) as i:
                for u in range(UNROLL):
                    step(i * UNROLL + u, i, u, False)
            for u in range(UNROLL):
                step((ITERS - 1) * UNROLL + u, ITERS - 1, u, True)

        def out_is_stored(engine, i, u):
            before = i * 2 + u // 2
            if not isinstance(before, int) or before > 0:
                engine.wait_ge(scattered[u % 2], before * 16)

        @block.gpsimd
        def _(pool):
            for s in range(2):
                pool.memset(B.xg[s][:, :], 0.0)
            pool.drain()
            for e in range(2):
                pool.wait_ge(gi_ready, e + 1)
                gather_tokens(pool, m, B, e).then_inc(gathered[e], 16)

            def step(e, i, u, tail):
                s = u % 2
                if not (tail and u >= UNROLL - 2):
                    pool.wait_ge(gi_ready, e + 3)
                    carry(pool, m)
                    gather_tokens(pool, m, B, s).then_inc(gathered[s], 16)
                pool.wait_ge(y_sb[0], e + 3)
                pool.wait_ge(y_sb[1], e + 3)
                carry(pool, m)
                scatter_tokens(pool, m, B, s).then_inc(scattered[s], 16)

            over_experts(pool, step)
            for s in range(2):
                pool.wait_ge(scattered[s], 16 * (EXPERTS // 2))

        @block.tensor
        def _(pe):
            pe.wait_ge(gathered[0], 16)
            expert_turn(pe, m, B, 0).then_inc(turned, 1)

            def step(e, i, u, tail):
                s = u % 2
                pe.wait_ge(xT_sb, e + 1)
                pe.wait_ge(m.w13_loaded[u], (i + 1) * 32)
                expert_up(pe, m, B, s, u).then_inc(up_done, 1)
                if not (tail and u == UNROLL - 1):
                    pe.wait_ge(gathered[1 - s], (i * 2 + ((u + 1) // 2 + 1)) * 16)
                    carry(pe, m)
                    expert_turn(pe, m, B, 1 - s).then_inc(turned, 1)
                pe.wait_ge(hid_done, e + 1)
                pe.wait_ge(m.w2_loaded[u], (i + 1) * 16)
                for h in range(2):
                    pe.wait_ge(y_sb[h], e + 1)
                expert_down(pe, m, B, s, u).then_inc(down_done, 1)

            over_experts(pe, step)

        @block.scalar
        def _(act):
            act.sem_inc(y_sb[1], 2)
            def step(e, i, u, tail):
                s = u % 2
                act.wait_ge(up_done, e + 1)
                expert_silu(act, B, s).then_inc(silu_done, 1)
                out_is_stored(act, i, u)
                act.wait_ge(down_done, e + 1)
                act.copy(B.y[s][:, HALF:D], B.psY[0:SLOTS, s, 1, :]).then_inc(y_sb[1], 1)

            over_experts(act, step)

        @block.vector
        def _(dve):
            dve.sem_inc(y_sb[0], 2)
            for e in range(2):
                dve.tensor_copy(B.gi[e][:, :], m.gather_idx[:, e:e + 1]).then_inc(gi_ready, 1)
            dve.wait_ge(turned, 1)
            expert_xT(dve, m, B, 0).then_inc(xT_sb, 1)
            dve.tensor_copy(B.gi[0][:, :], m.gather_idx[:, 2:3]).then_inc(gi_ready, 1)

            def step(e, i, u, tail):
                s = u % 2
                dve.wait_ge(silu_done, e + 1)
                expert_hidden(dve, B, s).then_inc(hid_done, 1)
                if not (tail and u == UNROLL - 1):
                    dve.wait_ge(turned, e + 2)
                    expert_xT(dve, m, B, 1 - s).then_inc(xT_sb, 1)
                if not (tail and u >= UNROLL - 3):
                    dve.tensor_copy(B.gi[1 - s][:, :], m.gather_idx[:, col(e + 3)]).then_inc(gi_ready, 1)
                out_is_stored(dve, i, u)
                carry(dve, m)
                dve.tensor_copy(B.si[s][:, :], m.scatter_idx[:, col(e)])
                dve.wait_ge(down_done, e + 1)
                dve.tensor_copy(B.y[s][:, 0:HALF], B.psY[0:SLOTS, s, 0, :])
                dve.drain()
                dve.sem_inc(y_sb[0], 1)

            over_experts(dve, step)


def more_blocks(nc, m, a):
    MOST = 2 * T // SLOTS
    with ExitStack() as ctx:
        sem = lambda n: nc.alloc_semaphore(fresh(n))
        B = ExpertBuffers(nc, ctx)
        weights, indices, tokens, gathered, turned, xT_sb, up_done, silu_done, hid_done, down_done, y_sb, scattered, free = (
            sem("more_" + n) for n in ("weights", "indices", "tokens", "gathered", "turned", "xT", "up", "silu",
                                       "hid", "down", "y", "scattered", "free"))
        block = ctx.enter_context(nc.Block())

        def over_blocks(engine, step):
            n = engine.value_load(m.n_extra[0:1, 0:1], min_val=0, max_val=MOST)
            with engine.If(n > 0):
                with engine.Fori(0, n) as b:
                    step(b)

        @block.sync
        def _(sp):
            def step(b):
                e = sp.value_load(m.info_row[0:1, bass.ds(b * 2, 1)], min_val=0, max_val=EXPERTS - 1)
                row = sp.value_load(m.info_row[0:1, bass.ds(b * 2 + 1, 1)], min_val=0, max_val=(T - SLOTS) * EXPERTS + EXPERTS - 1)
                sp.wait_ge(free, b + 1)
                for j, w in enumerate(("moe_w1", "moe_w3")):
                    sp.dma_start(m.w13[0][:, j], a[w][0, e].rearrange("(k p) n -> p k n", p=P)).then_inc(weights, 16)
                sp.dma_start(m.w2[0], a["moe_w2"][0, e].rearrange("(k p) n -> p k n", p=P)).then_inc(weights, 16)
                sp.dma_start(B.si[0][:, :], m.codes[bass.ds(row, SLOTS, EXPERTS), :])\
                    .then_inc(indices, 16)
            over_blocks(sp, step)

        @block.gpsimd
        def _(pool):
            pool.memset(B.xg[0][:, :], 0.0)
            pool.drain()
            pool.sem_inc(free, 1)
            def step(b):
                pool.wait_ge(tokens, b + 1)
                carry(pool, m)
                gather_tokens(pool, m, B, 0).then_inc(gathered, 16)
                pool.wait_ge(y_sb, b + 1)
                carry(pool, m)
                scatter_tokens(pool, m, B, 0).then_inc(scattered, 16)
                pool.wait_ge(scattered, (b + 1) * 16)
                pool.sem_inc(free, 1)
            over_blocks(pool, step)

        @block.tensor
        def _(pe):
            def step(b):
                pe.wait_ge(gathered, (b + 1) * 16)
                carry(pe, m)
                expert_turn(pe, m, B, 0).then_inc(turned, 1)
                pe.wait_ge(xT_sb, b + 1)
                pe.wait_ge(weights, (b + 1) * 48)
                expert_up(pe, m, B, 0, 0).then_inc(up_done, 1)
                pe.wait_ge(hid_done, b + 1)
                expert_down(pe, m, B, 0, 0).then_inc(down_done, 1)
            over_blocks(pe, step)

        @block.scalar
        def _(act):
            def step(b):
                act.wait_ge(up_done, b + 1)
                expert_silu(act, B, 0).then_inc(silu_done, 1)
            over_blocks(act, step)

        @block.vector
        def _(dve):
            def step(b):
                dve.wait_ge(indices, (b + 1) * 16)
                code_tokens(dve, B.gi[0][:, :], B.si[0][:, :])
                dve.sem_inc(tokens, 1)
                dve.wait_ge(turned, b + 1)
                expert_xT(dve, m, B, 0).then_inc(xT_sb, 1)
                dve.wait_ge(silu_done, b + 1)
                expert_hidden(dve, B, 0).then_inc(hid_done, 1)
                dve.wait_ge(down_done, b + 1)
                dve.tensor_copy(B.y[0][:, :].rearrange("p (h n) -> p h n", h=2), B.psY[0:SLOTS, 0, :, :]).then_inc(y_sb, 1)
            over_blocks(dve, step)


def combine(nc, m, a):
    x = m.b4
    parts = (m.b1, m.b2)
    with ExitStack() as ctx:
        sem = lambda n: nc.alloc_semaphore(fresh(n))
        sb = lambda n, s, d=F32: ctx.enter_context(nc.sbuf_tensor(n, s, d))
        gain = sb("final_norm_wide", [P, D])
        ss, root, inv, junk = sb("x2_ss", [P, TT]), sb("x2_root", [P, TT]), sb("x2_inv", [P, TT]), sb("x2_squares", [P, D])
        arrived = [sem(f"contrib_arrived{t}") for t in range(TT)]
        gain_arrived, added, summed, squares, roots, normed, stored = (
            sem(n) for n in ("final_gain", "contrib_added", "x2_summed", "x2_meaned", "x2_rooted", "x2_normed", "x2_stored"))
        block = ctx.enter_context(nc.Block())

        @block.sync
        def _(sp):
            sp.dma_start(gain[:, :], spread(a["final_norm"].rearrange("(o d) -> o d", o=1))).then_inc(gain_arrived, 16)
            for t in range(TT):
                for k in range(2):
                    sp.dma_start(parts[k][:, t, :], m.contrib[k * T + t * P:k * T + (t + 1) * P, :]).then_inc(arrived[t], 16)
            for t in range(TT):
                sp.wait_ge(normed, t + 1)
                sp.dma_start(m.x2_dram[t * P:(t + 1) * P, :], x[:, t, :]).then_inc(stored, 16)
            sp.wait_ge(stored, 16 * TT)

        @block.vector
        def _(dve):
            for t in range(TT):
                dve.wait_ge(arrived[t], 32)
                for k in range(2):
                    ins = dve.scalar_tensor_tensor(x[:, t, :], parts[k][:, t, :], m.gates2[:, k, t:t + 1], x[:, t, :],
                                                   ALU.mult, ALU.add)
                    if k == 0:
                        dve.drain()
                ins.then_inc(added, 1)
            dve.wait_ge(summed, TT)
            dve.tensor_scalar(ss[:, :], ss[:, :], 1.0 / D, EPS, ALU.mult, ALU.add).then_inc(squares, 1)
            inverse_rms(None, dve, None, root[:, :], inv[:, :], D, squares, roots)
            dve.wait_ge(gain_arrived, 16)
            for t in range(TT):
                dve.scalar_tensor_tensor(x[:, t, :], x[:, t, :], inv[:, t:t + 1], gain[:, :], ALU.mult, ALU.mult)\
                    .then_inc(normed, 1)

        @block.scalar
        def _(act):
            for t in range(TT):
                act.wait_ge(added, t + 1)
                act.activation(junk[:, :], x[:, t, :], ACT.Square, accum_out=ss[:, t:t + 1]).then_inc(summed, 1)
                act.drain()
            inverse_rms(act, None, ss[:, :], root[:, :], None, D, squares, roots)



def mixer_projections(nc, m, a):
    hT, raw, qk = m.b1, m.raw, m.b3
    with ExitStack() as ctx:
        sem = lambda n: nc.alloc_semaphore(fresh(n))
        sb = lambda n, s, d=F32: ctx.enter_context(nc.sbuf_tensor(n, s, d))
        w_dt = sb("w_dt", [P, KT, SH])
        dt_bias, a_log = sb("dt_bias_wide", [P, SH]), sb("a_log_wide", [P, SH])
        mag = sb("dt_magnitude", [P, TT, SH])
        conv = [sb(f"conv_sum{s}", [P, T]) for s in range(2)]
        ps = ctx.enter_context(nc.psum_tensor("ps_mix_in", [P, 4, HALF], F32))
        psd = ctx.enter_context(nc.psum_tensor("ps_dt", [P, TT, SH], F32))
        small, dt_ready, ps_ready, ps_free = sem("dt_weights"), sem("dt_ready"), sem("mix_ready"), sem("mix_free")
        dt_mag, dt_log, a_exp, padded, raw_sb, convolved, silued = (
            sem(n) for n in ("dt_mag", "dt_log", "a_exp", "padded", "raw_in_sbuf", "convolved", "conv_silu"))
        block = ctx.enter_context(nc.Block())
        BASE = 8

        @block.sync
        def _(sp):
            at = IN_AT["dt"]
            sp.dma_start(w_dt[:, :, :], a["w_in_2"][0][:, at:at + SH].rearrange("(k p) n -> p k n", p=P)).then_inc(small, 16)
            sp.dma_start(dt_bias[:, :], spread(a["dt_bias_2"])).then_inc(small, 16)
            sp.dma_start(a_log[:, :], spread(a["a_log_2"])).then_inc(small, 16)
            sp.dma_start(m.d_skip[:, :], spread(a["d_skip_2"])).then_inc(small, 16)
            m.ring.issue(sp, BASE + 2, BASE + 8)

        @block.tensor
        def _(pe):
            pe.wait_ge(small, 64)
            for t in range(TT):
                for k in range(KT):
                    last = pe.matmul(psd[:, t, :], hT[:, k, t * P:(t + 1) * P], w_dt[:, k, :], start=(k == 0), stop=(k == KT - 1))
            last.then_inc(dt_ready, 1)
            with pe.Fori(0, 2) as i:
                for s in range(2):
                    pe.wait_ge(m.ring.loaded[s], i * 16 + m.ring.loads_before(BASE + s))
                    gemm_channels(pe, m.ring, s, range(4), hT, ps, i * 16 + 8 * s, ps_ready, ps_free, 4)
            for s in range(2):
                pe.wait_ge(m.ring.loaded[s], m.ring.loads_before(BASE + 4 + s))
                gemm_tokens(pe, m.ring, s, hT, ps, 32 + 8 * s, ps_ready, ps_free, 4)

        @block.scalar
        def _(act):
            act.sem_inc(ps_free, 4)

            def silu(c):
                act.wait_ge(convolved, c + 1)
                act.activation(raw[:, c, TAPS - 1:], conv[c % 2][:, :], ACT.Silu).then_inc(silued, 1)

            act.wait_ge(small, 64)
            act.activation(a_log[:, :], a_log[:, :], ACT.Exp).then_inc(a_exp, 1)
            act.wait_ge(dt_mag, 1)
            act.activation(mag[:, :, :], mag[:, :, :], ACT.Exp, scale=-1.0)
            act.drain()
            act.activation(mag[:, :, :], mag[:, :, :], ACT.Ln, bias=1.0).then_inc(dt_log, 1)
            for n in range(48):
                act.wait_ge(ps_ready, n + 1)
                src, cols = ps[:, n % 4, :], slice((n % 2) * HALF, (n % 2 + 1) * HALF)
                if n < 16:
                    act.copy(raw[:, n // 2, TAPS - 1 + (n % 2) * HALF:TAPS - 1 + (n % 2 + 1) * HALF], src).then_inc(ps_free, 1)
                elif n < 24:
                    act.mul(qk[:, n // 2 - 8, cols], src, float(AHD) ** -0.5).then_inc(ps_free, 1)
                elif n < 32:
                    act.copy(qk[:, n // 2 - 8, cols], src).then_inc(ps_free, 1)
                else:
                    act.copy((m.z if n < 40 else m.v)[:, n % 8, :], src).then_inc(ps_free, 1)
                if n < 16:
                    act.drain()
                    act.sem_inc(raw_sb, 1)
                if n % 8 == 7:
                    m.ring.release(act)
                if n >= 16 and n % 2 == 0 and (n - 16) // 2 < KT:
                    silu((n - 16) // 2)
            for t in range(TT):
                act.activation(m.z[:, t, :], m.z[:, t, :], ACT.Silu)

        @block.vector
        def _(dve):
            dve.memset(raw[:, :, 0:TAPS - 1], 0.0)
            dve.wait_ge(dt_ready, 1)
            dve.tensor_tensor(m.dt[:, :, :], psd[:, :, :], dt_bias[:, None, :].to_broadcast([P, TT, SH]), ALU.add)
            dve.drain()
            dve.tensor_scalar(mag[:, :, :], m.dt[:, :, :], -1.0, None, ALU.mult)
            dve.drain()
            dve.tensor_tensor(mag[:, :, :], mag[:, :, :], m.dt[:, :, :], ALU.max).then_inc(dt_mag, 1)
            dve.wait_ge(dt_log, 1)
            dve.tensor_scalar(m.dt[:, :, :], m.dt[:, :, :], 0.0, None, ALU.max)
            dve.drain()
            dve.tensor_tensor(m.dt[:, :, :], m.dt[:, :, :], mag[:, :, :], ALU.add)
            dve.drain()
            dve.scalar_tensor_tensor(m.adt[:, :, :], m.dt[:, :, :], -1.0, a_log[:, None, :].to_broadcast([P, TT, SH]),
                                     ALU.mult, ALU.mult)
            row, bias = VEC["ssd_conv_w_2"][0], VEC["ssd_conv_b_2"][0]
            for c in range(KT):
                out = conv[c % 2][:, :]
                dve.wait_ge(raw_sb, 2 * c + 2)
                if c >= 2:
                    dve.wait_ge(silued, c - 1)
                w = lambda j: m.cols[:, row + j * KT + c:row + j * KT + c + 1]
                dve.tensor_scalar(out, raw[:, c, 0:T], w(0), m.cols[:, bias + c:bias + c + 1], ALU.mult, ALU.add)
                for j in range(1, TAPS):
                    dve.drain()
                    ins = dve.scalar_tensor_tensor(out, raw[:, c, j:j + T], w(j), out, ALU.mult, ALU.add)
                ins.then_inc(convolved, 1)
            dve.drain()


def state_space(nc, m, a):
    W = SH * SHD
    with ExitStack() as ctx:
        sem = lambda n: nc.alloc_semaphore(fresh(n))
        sb = lambda n, s, d=F32: ctx.enter_context(nc.sbuf_tensor(n, s, d))
        cur = m.b1[:, 4, :].rearrange("p (c n) -> p c n", c=KT)
        later = m.b1[:, 5, :].rearrange("p (h n) -> p h n", h=SH)
        dec = m.b1[:, 6, :].rearrange("p (h n) -> p h n", h=SH)
        M = m.b1[:, 7, :].rearrange("p (h n) -> p h n", h=SH)
        adt, dt, es = sb("adt_now", [P, SH]), sb("dt_now", [P, SH]), sb("decays", [P, 4, SH])
        X, XE, XD = sb("x_dt", [P, SH, SHD]), sb("x_to_end", [P, SH, SHD]), sb("x_skip", [P, SH, SHD])
        Bt, CB = sb("b_tokens", [P, SG, SN]), sb("cb", [P, SG, P])
        S, S_mid, tmp, y = sb("ssd_state", [P, SH, SHD]), sb("ssd_mid", [P, SH, SHD]), sb("ssd_tmp", [P, SH, SHD]), sb("ssd_y", [P, SH, SHD])
        psT = ctx.enter_context(nc.psum_tensor("ps_tokens", [P, 2, HALF], F32))
        psS = ctx.enter_context(nc.psum_tensor("ps_small", [P, 4, SH], F32))
        psG = ctx.enter_context(nc.psum_tensor("ps_seg", [P, SH, P], F32))
        psY = ctx.enter_context(nc.psum_tensor("ps_diag", [P, SH, SHD], F32))
        psZ = ctx.enter_context(nc.psum_tensor("ps_off", [P, SH, SHD], F32))
        (cur_ready, adt_ready, later_ready, small_ready, small_exp, T_ready, seg_ready, dec_ready, x_ready, M_ready,
         diag_ready, upd_ready, mid_ready, state_ready, off0_ready, off_ready) = (sem("s_" + n) for n in (
             "current", "adt", "later", "small", "small_exp", "tokens", "seg", "decay", "x", "M", "diag", "update", "mid",
             "state", "off0", "off"))
        block = ctx.enter_context(nc.Block())
        heads = lambda v: v[:, :, None].to_broadcast([P, SH, SHD])
        group = lambda g: slice(g * HPG, (g + 1) * HPG)

        @block.scalar
        def _(act):
            act.sem_inc(off_ready, 1)
            with act.Fori(0, TT) as p:
                act.wait_ge(off_ready, p + 1)
                carry(act, m)
                act.activation(cur, m.raw[:, :, bass.ds(p * P + (TAPS - 1), P)], ACT.Copy).then_inc(cur_ready, 1)
                act.wait_ge(small_ready, p + 1)
                act.activation(es[:, :, :], psS[:, :, :], ACT.Exp).then_inc(small_exp, 1)
                act.wait_ge(seg_ready, p + 1)
                act.activation(dec, psG[:, :, :], ACT.Exp).then_inc(dec_ready, 1)

        @block.tensor
        def _(pe):
            with pe.Fori(0, TT) as p:
                pe.wait_ge(adt_ready, p + 1)
                for i, mask in enumerate((m.upto[:, :], m.after[:, :], m.chunk_ones[:, 0, :], m.chunk_ones[:, 1, :])):
                    last = pe.matmul(psS[:, i, :], mask, adt[:, :], start=True, stop=True)
                last.then_inc(small_ready, 1)
                pe.wait_ge(later_ready, p + 1)
                for h in range(SH):
                    last = pe.matmul(psG[:, h, :], later[:, h, :], m.upto[:, :], start=True, stop=True)
                last.then_inc(seg_ready, 1)
                pe.wait_ge(cur_ready, p + 1)
                pe.wait_ge(state_ready, p + 1)
                for c in range(4):
                    pe.transpose(psT[:, 0, c * P:(c + 1) * P], cur[:, c, :], m.ident[:, :])
                for g in range(SG):
                    pe.transpose(psT[:, 1, g * P:(g + 1) * P], cur[:, 4 + g, :], m.ident[:, :])
                for g in range(SG):
                    last = pe.matmul(psT[:, 1, (2 + g) * P:(3 + g) * P], cur[:, 4 + g, :], cur[:, 6 + g, :], start=True, stop=True)
                last.then_inc(T_ready, 1)
                for g in range(SG):
                    last = pe.matmul(psZ[0:CH, group(g), :], cur[:, 6 + g, 0:CH], S[:, group(g), :], start=True, stop=True)
                last.then_inc(off0_ready, 1)
                pe.wait_ge(x_ready, p + 1)
                for c in range(2):
                    for g in range(SG):
                        last = pe.matmul(psT[:, c, g * 2 * P:(g + 1) * 2 * P], Bt[c * CH:(c + 1) * CH, g, :],
                                         XE[c * CH:(c + 1) * CH, group(g), :], start=True, stop=True)
                last.then_inc(upd_ready, 1)
                pe.wait_ge(M_ready, p + 1)
                for h in range(SH):
                    last = pe.matmul(psY[:, h, :], M[:, h, :], X[:, h, :], start=True, stop=True)
                last.then_inc(diag_ready, 1)
                pe.wait_ge(mid_ready, p + 1)
                for g in range(SG):
                    last = pe.matmul(psZ[CH:P, group(g), :], cur[:, 6 + g, CH:P], S_mid[:, group(g), :], start=True, stop=True)
                last.then_inc(off_ready, 1)

        @block.vector
        def _(dve):
            dve.memset(S[:, :, :], 0.0).then_inc(state_ready, 1)
            with dve.Fori(0, TT) as p:
                dve.tensor_copy(adt[:, :], m.adt[:, p, :])
                dve.tensor_copy(dt[:, :], m.dt[:, p, :])
                dve.drain()
                dve.sem_inc(adt_ready, 1)
                dve.tensor_tensor(later, m.after[:, None, :].to_broadcast([P, SH, P]),
                                  adt[:, :, None].to_broadcast([P, SH, P]), ALU.mult).then_inc(later_ready, 1)
                dve.wait_ge(T_ready, p + 1)
                xs = psT[:, 0, :].rearrange("p (h n) -> p h n", h=SH)
                dve.tensor_tensor(X[:, :, :], xs, heads(dt), ALU.mult)
                dve.tensor_tensor(XD[:, :, :], xs, heads(m.d_skip), ALU.mult)
                dve.tensor_copy(Bt[:, :, :], psT[:, 1, 0:2 * P].rearrange("p (g n) -> p g n", g=SG))
                dve.tensor_tensor(CB[:, :, :], psT[:, 1, 2 * P:4 * P].rearrange("p (g n) -> p g n", g=SG),
                                  m.upto[:, None, :].to_broadcast([P, SG, P]), ALU.mult)
                dve.drain()
                dve.wait_ge(small_exp, p + 1)
                dve.tensor_tensor(XE[:, :, :], X[:, :, :], heads(es[:, 1]), ALU.mult).then_inc(x_ready, 1)
                dve.wait_ge(dec_ready, p + 1)
                for g in range(SG):
                    ins = dve.tensor_tensor(M[:, group(g), :], dec[:, group(g), :],
                                            CB[:, g, None, :].to_broadcast([P, HPG, P]), ALU.mult)
                ins.then_inc(M_ready, 1)
                dve.tensor_tensor(tmp[:, :, :], S[:, :, :], heads(es[:, 2]), ALU.mult)
                dve.drain()
                dve.wait_ge(upd_ready, p + 1)
                dve.tensor_tensor(S_mid[:, :, :], psT[:, 0, :].rearrange("p (h n) -> p h n", h=SH), tmp[:, :, :],
                                  ALU.add).then_inc(mid_ready, 1)
                dve.drain()
                dve.tensor_tensor(tmp[:, :, :], S_mid[:, :, :], heads(es[:, 3]), ALU.mult)
                dve.drain()
                dve.wait_ge(off0_ready, p + 1)
                dve.tensor_tensor(S[:, :, :], psT[:, 1, :].rearrange("p (h n) -> p h n", h=SH), tmp[:, :, :],
                                  ALU.add).then_inc(state_ready, 1)
                dve.wait_ge(off_ready, p + 2)
                dve.tensor_tensor(y[:, :, :], psZ[:, :, :], heads(es[:, 0]), ALU.mult)
                dve.drain()
                dve.wait_ge(diag_ready, p + 1)
                dve.tensor_tensor(y[:, :, :], psY[:, :, :], y[:, :, :], ALU.add)
                dve.drain()
                dve.tensor_tensor(y[:, :, :], y[:, :, :], XD[:, :, :], ALU.add)
                dve.drain()
                z = m.z[:, p, :]
                dve.tensor_tensor(z, z, y[:, :, :].rearrange("p h n -> p (h n)"), ALU.mult)
                dve.drain()


def band_attention(nc, m, a):
    qk, v = m.b3, m.v
    with ExitStack() as ctx:
        sem = lambda n: nc.alloc_semaphore(fresh(n))
        sb = lambda n, s, d=F32: ctx.enter_context(nc.sbuf_tensor(n, s, d))
        q = m.raw[:, 0, 0:T]
        k = m.raw[:, 1, 0:T]
        bias = [m.raw[:, 2 + u, 0:BAND] for u in range(2)]
        sc = [m.raw[:, 4 + u, 0:BAND] for u in range(2)]
        pT = [m.raw[:, 6 + u, 0:BAND] for u in range(2)]
        nmx, rs, ri = sb("minus_max", [P, 4]), sb("prob_sum", [P, 4]), sb("prob_inv", [P, 4])
        psS = [ctx.enter_context(nc.psum_tensor(f"ps_scores{u}", [P, 2 * HALF], F32)) for u in range(2)]
        psT = [ctx.enter_context(nc.psum_tensor(f"ps_probsT{u}", [P, 2 * HALF], F32)) for u in range(2)]
        psO = [psT[u][:, HALF + P:HALF + P + AHD] for u in range(2)]
        bias_arrived = [sem(f"bias_arrived{u}") for u in range(2)]
        (copied, scores, read_s, maxed, exped, turned, pT_sb, out_ready, out_sb) = (sem("b_" + n) for n in (
            "qk_copied", "scores", "scores_read", "maxed", "exped", "turned", "probsT", "out", "out_in_sbuf"))
        block = ctx.enter_context(nc.Block())
        PAIRS = AH // 2
        WARM = 3
        UNITS = 2 * TT
        units = [(u, j) for j in range(TT) for u in range(2)]
        tiles = lambda n: min(units[n][1], BANDT - 1) + 1

        @block.sync
        def _(sp):
            for u in range(2):
                sp.dma_start(bias[u], shifted(m.bias_lines[u])).then_inc(bias_arrived[u], 16)
            with sp.Fori(1, PAIRS) as hp:
                for u in range(2):
                    sp.wait_ge(read_s, hp * UNITS + 2)
                    sp.dma_start(bias[u], shifted(m.bias_lines[hp * 2 + u])).then_inc(bias_arrived[u], 16)

        @block.scalar
        def _(act):
            act.sem_inc(out_ready, 1)
            with act.Fori(0, PAIRS) as hp:
                act.wait_ge(out_ready, hp * UNITS + 1)
                carry(act, m)
                act.activation(q, qk[:, hp, :], ACT.Copy)
                act.activation(k, qk[:, hp + PAIRS, :], ACT.Copy).then_inc(copied, 1)

                def exponentials(n):
                    w, i = tiles(n) * P, n % 4
                    act.wait_ge(maxed, hp * UNITS + (n + 1))
                    act.activation(sc[n % 2][:, 0:w], sc[n % 2][:, 0:w], ACT.Exp, bias=nmx[:, i:i + 1], accum_out=rs[:, i:i + 1])
                    act.drain()
                    act.sem_inc(exped, 1)

                exponentials(0)
                exponentials(1)
                for n in range(UNITS):
                    w = tiles(n) * P
                    act.wait_ge(turned, hp * UNITS + (n + 1))
                    if n >= 2:
                        act.wait_ge(out_ready, hp * UNITS + n)
                    act.activation(pT[n % 2][:, 0:w], psT[n % 2][:, 0:w], ACT.Copy).then_inc(pT_sb, 1)
                    if n + 2 < UNITS:
                        exponentials(n + 2)

        @block.tensor
        def _(pe):
            with pe.Fori(0, PAIRS) as hp:
                def score(n):
                    u, j = units[n]
                    first, w = j + 1 - tiles(n), tiles(n) * P
                    pe.wait_ge(read_s, hp * UNITS + (n + 1))
                    rows = slice(u * AHD, (u + 1) * AHD)
                    for c0 in range(0, w, HALF):
                        c1 = min(w, c0 + HALF)
                        last = pe.matmul(psS[u][:, c0:c1], q[rows, j * P:(j + 1) * P], k[rows, first * P + c0:first * P + c1],
                                         start=True, stop=True)
                    last.then_inc(scores, 1)

                def turn(n):
                    u = n % 2
                    pe.wait_ge(exped, hp * UNITS + (n + 1))
                    pe.wait_ge(out_sb, hp * UNITS + (n + 1))
                    for t in range(tiles(n)):
                        last = pe.transpose(psT[u][:, t * P:(t + 1) * P], sc[u][:, t * P:(t + 1) * P], m.ident[:, :])
                    last.then_inc(turned, 1)

                pe.wait_ge(copied, hp + 1)
                score(0)
                score(1)
                pe.wait_ge(out_sb, hp * UNITS + 1)
                for n in range(WARM):
                    pe.matmul(psT[0][:, 0:HALF], m.ident[:, :], k[:, 0:HALF], start=True, stop=True)
                turn(0)
                for n, (u, j) in enumerate(units):
                    if n + 2 < UNITS:
                        score(n + 2)
                    if n + 1 < UNITS:
                        turn(n + 1)
                    pe.wait_ge(pT_sb, hp * UNITS + (n + 1))
                    for t in range(tiles(n)):
                        last = pe.matmul(psO[u], pT[u][:, t * P:(t + 1) * P],
                                         v[:, j + 1 - tiles(n) + t, bass.ds(hp * 2 * AHD + u * AHD, AHD)],
                                         start=(t == 0), stop=(t == tiles(n) - 1))
                    last.then_inc(out_ready, 1)

        @block.vector
        def _(dve):
            dve.sem_inc(read_s, 2)
            dve.sem_inc(out_sb, 2)
            with dve.Fori(0, PAIRS) as hp:
                for u in range(2):
                    dve.wait_ge(bias_arrived[u], (hp + 1) * 16)
                    dve.memset(bias[u][0:CH, BAND - CH:BAND], MASKED)
                    dve.memset(bias[u][CH:P, 0:CH], MASKED)
                dve.drain()

                def biased(n):
                    u, w, i = n % 2, tiles(n) * P, n % 4
                    dve.wait_ge(scores, hp * UNITS + (n + 1))
                    if n >= 2:
                        dve.wait_ge(turned, hp * UNITS + (n - 1))
                    dve.tensor_tensor(sc[u][:, 0:w], psS[u][:, 0:w], bias[u][:, BAND - w:BAND], ALU.add).then_inc(read_s, 1)
                    dve.drain()
                    dve.reduce_max(nmx[:, i:i + 1], sc[u][:, 0:w], axis=AX.X, negate=True).then_inc(maxed, 1)

                biased(0)
                biased(1)
                for n, (u, j) in enumerate(units):
                    i = n % 4
                    if n + 2 < UNITS:
                        biased(n + 2)
                    dve.wait_ge(out_ready, hp * UNITS + (n + 2))
                    dve.reciprocal(ri[:, i:i + 1], rs[:, i:i + 1])
                    dve.drain()
                    dve.tensor_scalar(m.att[:, j, bass.ds(hp * 2 * AHD + u * AHD, AHD)], psO[u], ri[:, i:i + 1],
                                      None, ALU.mult).then_inc(out_sb, 1)
                dve.drain()


def shifted(lines):
    w = BAND + P
    flat = lines.rearrange("p n -> (p n)")
    return flat[P - 1:P - 1 + P * (w - 1)].rearrange("(p n) -> p n", n=w - 1)[:, 0:BAND]


def mixer_norm(nc, m, a):
    with ExitStack() as ctx:
        sem = lambda n: nc.alloc_semaphore(fresh(n))
        sb = lambda n, s, d=F32: ctx.enter_context(nc.sbuf_tensor(n, s, d))
        ss, root, inv, junk = sb("y_ss", [P, TT]), sb("y_root", [P, TT]), sb("y_inv", [P, TT]), sb("y_squares", [P, HALF])
        ps = ctx.enter_context(nc.psum_tensor("ps_catT", [P, 4, HALF], F32))
        summed, squares, roots, normed, ps_ready, ps_free = (
            sem(n) for n in ("y_summed", "y_meaned", "y_rooted", "y_normed", "catT_ready", "catT_free"))
        block = ctx.enter_context(nc.Block())
        y = m.z

        @block.scalar
        def _(act):
            for t in range(TT):
                act.activation(junk[:, :], y[:, t, :], ACT.Square, accum_out=ss[:, t:t + 1]).then_inc(summed, 1)
                act.drain()
            inverse_rms(act, None, ss[:, :], root[:, :], None, HALF, squares, roots)

        @block.vector
        def _(dve):
            dve.wait_ge(summed, TT)
            dve.tensor_scalar(ss[:, :], ss[:, :], 1.0 / (SH * SHD), EPS, ALU.mult, ALU.add).then_inc(squares, 1)
            inverse_rms(None, dve, None, root[:, :], inv[:, :], HALF, squares, roots)
            for t in range(TT):
                dve.tensor_scalar(y[:, t, :], y[:, t, :], inv[:, t:t + 1], None, ALU.mult).then_inc(normed, 1)
            row = VEC["ssd_norm_w_2"][0]
            transposes_out(dve, m.b2, lambda k: m.cols[:, row + k:row + k + 1] if k < 4 else None, None, ps, ps_ready, ps_free)

        @block.tensor
        def _(pe):
            pe.wait_ge(normed, TT)
            for n in range(2 * KT):
                k, half = n // 2, n % 2
                src = y if k < 4 else m.att
                if n >= 4:
                    pe.wait_ge(ps_free, n - 3)
                for j in range(4):
                    last = pe.transpose(ps[:, n % 4, j * P:(j + 1) * P], src[:, 4 * half + j, (k % 4) * P:(k % 4 + 1) * P],
                                        m.ident[:, :])
                last.then_inc(ps_ready, 1)



def ffn_up(nc, m, a):
    hT, uT = m.b1, m.uT
    BASE = 16
    PAD = FTAPS - 1
    with ExitStack() as ctx:
        sem = lambda n: nc.alloc_semaphore(fresh(n))
        sb = lambda n, s, d=F32: ctx.enter_context(nc.sbuf_tensor(n, s, d))
        raw = [[sb(f"up_raw{x}{s}", [P, T + PAD]) for x in range(2)] for s in range(2)]
        conv = [sb(f"up_conv{x}", [P, T]) for x in range(2)]
        ps = ctx.enter_context(nc.psum_tensor("ps_up", [P, 8, HALF], F32))
        ps_ready, ps_free, raw_sb, convolved, silued, made = (
            sem(n) for n in ("up_ready", "up_free", "up_raw_sb", "up_convolved", "up_silu", "up_made"))
        raw_free = sem("up_raw_free")
        block = ctx.enter_context(nc.Block())
        BLOCKS = FT // 2

        def over_blocks(engine, step):
            with engine.Fori(0, BLOCKS // 2) as i:
                for s in range(2):
                    step(i, s)
            step(BLOCKS // 2, 0)

        @block.sync
        def _(sp):
            m.ring.issue(sp, BASE + 2, BASE + BLOCKS)

        @block.tensor
        def _(pe):
            def step(i, s):
                pe.wait_ge(m.ring.loaded[s], i * 32 + m.ring.loads_before(BASE + s))
                gemm_channels(pe, m.ring, s, (0, 2, 1, 3), hT, ps, i * 16 + 8 * s, ps_ready, ps_free, 8)
            over_blocks(pe, step)

        @block.scalar
        def _(act):
            act.sem_inc(ps_free, 8)
            act.wait_ge(raw_free, 4)

            def step(i, s):
                for c in range(2):
                    n = i * 4 + (2 * s + c)
                    act.wait_ge(raw_free, n * 2 + 2)
                    carry(act, m)
                    for j in range(4):
                        act.wait_ge(ps_ready, i * 16 + (8 * s + 4 * c + j + 1))
                        act.copy(raw[c][j // 2][:, PAD + (j % 2) * HALF:PAD + (j % 2 + 1) * HALF], ps[:, 4 * c + j, :])\
                            .then_inc(ps_free, 1)
                    if c == 1:
                        m.ring.release(act)
                    act.drain()
                    act.sem_inc(raw_sb, 1)
                    act.wait_ge(convolved, n + 1)
                    act.activation(conv[0][:, :], conv[0][:, :], ACT.Silu).then_inc(silued, 1)
            over_blocks(act, step)

        @block.vector
        def _(dve):
            for s in range(2):
                for x in range(2):
                    dve.memset(raw[s][x][:, 0:PAD], 0.0).then_inc(raw_free, 1)

            def step(i, s):
                for c in range(2):
                    n = i * 4 + (2 * s + c)
                    dve.wait_ge(raw_sb, n + 1)
                    for x in (1, 0):
                        for j in range(FTAPS):
                            w = m.conv_cols[:, col(j * 2 * FT + x * FT + n)]
                            if j == 0:
                                dve.tensor_scalar(conv[x][:, :], raw[c][x][:, 0:T], w, None, ALU.mult)
                            else:
                                dve.drain()
                                ins = dve.scalar_tensor_tensor(conv[x][:, :], raw[c][x][:, j:j + T], w, conv[x][:, :],
                                                               ALU.mult, ALU.add)
                        if x == 0:
                            ins.then_inc(convolved, 1)
                            dve.sem_inc(raw_free, 2)
                    dve.wait_ge(silued, n + 1)
                    dve.tensor_tensor(uT[:, n, :], conv[0][:, :], conv[1][:, :], ALU.mult).then_inc(made, 1)
                    dve.drain()
            over_blocks(dve, step)


def col(n):
    return slice(n, n + 1) if isinstance(n, int) else bass.ds(n, 1)


def ffn_down(nc, m, a):
    uT = m.uT
    PARTS = ((0, 8), (8, 8), (16, 6))
    with ExitStack() as ctx:
        sem = lambda n: nc.alloc_semaphore(fresh(n))
        sb = lambda n, s, d=F32: ctx.enter_context(nc.sbuf_tensor(n, s, d))
        w = [m.ring.buf[:, 0], m.ring.buf[:, 1], m.b1[:, 0:3, :].rearrange("p a n -> p (a n)").rearrange("p (k n) -> p k n", n=HALF)]
        x3 = [sb(f"x3_part{s}", [P, HALF]) for s in range(2)]
        temp = sb("down_gated", [P, 2, HALF])
        ps = ctx.enter_context(nc.psum_tensor("ps_down", [P, 8, HALF], F32))
        loaded = [sem(f"down_loaded{i}") for i in range(3)]
        arrived = [sem(f"x3_arrived{s}") for s in range(2)]
        used, ps_ready, ps_free, added = sem("down_used"), sem("down_ready"), sem("down_free"), sem("down_added")
        block = ctx.enter_context(nc.Block())

        @block.sync
        def _(sp):
            def weights(h, i):
                k0, n = PARTS[i]
                if h:
                    sp.wait_ge(used, i + 1)
                sp.dma_start(w[i][:, 0:n, :], a["w_down_2"][0][k0 * P:(k0 + n) * P, h * HALF:(h + 1) * HALF]
                             .rearrange("(k p) n -> p k n", p=P)).then_inc(loaded[i], 16)
            for i in range(3):
                weights(0, i)
            for n in range(2 * TT):
                h, t = n // TT, n % TT
                if n >= 2:
                    sp.wait_ge(added, n - 1)
                sp.dma_start(x3[n % 2][:, :], m.x3_dram[t * P:(t + 1) * P, h * HALF:(h + 1) * HALF]).then_inc(arrived[n % 2], 16)
                if n == 1:
                    weights(1, 0)
                    weights(1, 1)
                if n == TT - 1:
                    weights(1, 2)

        @block.tensor
        def _(pe):
            for h in range(2):
                for i, (k0, n) in enumerate(PARTS):
                    pe.wait_ge(loaded[i], 16 * (h + 1))
                    for t in range(TT):
                        if h and i == 0:
                            pe.wait_ge(ps_free, t + 1)
                        for k in range(n):
                            last = pe.matmul(ps[:, t, :], uT[:, k0 + k, t * P:(t + 1) * P], w[i][:, k, :],
                                             start=(k0 + k == 0), stop=(k0 + k == FT - 1))
                        if i == 2:
                            last.then_inc(ps_ready, 1)
                    if i < 2:
                        last.then_inc(used, 1)

        @block.vector
        def _(dve):
            for n in range(2 * TT):
                h, t = n // TT, n % TT
                dve.wait_ge(ps_ready, n + 1)
                if n == TT - 1:
                    dve.sem_inc(used, 1)
                dve.tensor_tensor(temp[:, n % 2, :], ps[:, t, :], m.gate_ffn[:, h * HALF:(h + 1) * HALF], ALU.mult).then_inc(ps_free, 1)
                dve.drain()
                dve.wait_ge(arrived[n % 2], 16 * (n // 2 + 1))
                dve.tensor_tensor(m.xf[h][:, t, :], temp[:, n % 2, :], x3[n % 2][:, :], ALU.add).then_inc(added, 1)


def final_norm(nc, m, a, out):
    with ExitStack() as ctx:
        sem = lambda n: nc.alloc_semaphore(fresh(n))
        sb = lambda n, s, d=F32: ctx.enter_context(nc.sbuf_tensor(n, s, d))
        ss, root, inv, junk = sb("f_ss", [P, 2, TT]), sb("f_root", [P, TT]), sb("f_inv", [P, TT]), sb("f_squares", [P, HALF])
        gain = sb("final_norm_2_wide", [P, D])
        gain_arrived, summed, squares, roots, normed, stored = (
            sem(n) for n in ("f_gain", "f_summed", "f_meaned", "f_rooted", "f_normed", "out_stored"))
        block = ctx.enter_context(nc.Block())

        @block.sync
        def _(sp):
            sp.dma_start(gain[:, :], spread(a["final_norm_w_2"].rearrange("(o d) -> o d", o=1))).then_inc(gain_arrived, 16)
            for t in range(TT):
                for h in range(2):
                    sp.wait_ge(normed, 2 * t + h + 1)
                    sp.dma_start(out[0, t * P:(t + 1) * P, h * HALF:(h + 1) * HALF], m.xf[h][:, t, :]).then_inc(stored, 16)
            sp.wait_ge(stored, 16 * 2 * TT)

        @block.scalar
        def _(act):
            for t in range(TT):
                for h in range(2):
                    act.activation(junk[:, :], m.xf[h][:, t, :], ACT.Square, accum_out=ss[:, h, t:t + 1]).then_inc(summed, 1)
                    act.drain()
            inverse_rms(act, None, ss[:, 0, :], root[:, :], None, D, squares, roots)

        @block.vector
        def _(dve):
            dve.wait_ge(summed, 2 * TT)
            dve.tensor_tensor(ss[:, 0, :], ss[:, 0, :], ss[:, 1, :], ALU.add)
            dve.drain()
            dve.tensor_scalar(ss[:, 0, :], ss[:, 0, :], 1.0 / D, EPS, ALU.mult, ALU.add).then_inc(squares, 1)
            inverse_rms(None, dve, None, root[:, :], inv[:, :], D, squares, roots)
            dve.wait_ge(gain_arrived, 16)
            for t in range(TT):
                for h in range(2):
                    x = m.xf[h][:, t, :]
                    dve.scalar_tensor_tensor(x, x, inv[:, t:t + 1], gain[:, h * HALF:(h + 1) * HALF], ALU.mult, ALU.mult)\
                        .then_inc(normed, 1)



def program(nc, a, out):
    _names.clear()
    with ExitStack() as ctx:
        ctx.enter_context(nc.allow_non_contiguous_dma(reason="columns and broadcasts"))
        sb = lambda n, s, d=F32: ctx.enter_context(nc.sbuf_tensor(n, s, d))
        dram = lambda n, s, d=F32: nc.dram_tensor(n, s, d).ap()
        m = Parts()
        PAD = TAPS - 1
        size2 = KT * (T + PAD)
        m.big = sb("big", [P, 3 * 8 * D + size2])
        cut = lambda at, w=D: m.big[:, at:at + 8 * w].rearrange("p (t n) -> p t n", t=8)
        m.b1, m.b3, m.b4 = cut(0), cut(8 * D), cut(16 * D)
        m.vr = m.big[:, 8 * D:24 * D].rearrange("p (t n) -> p t n", t=16)
        m.b2, m.raw = cut(24 * D), cut(24 * D, T + PAD)
        m.uT = m.big[:, 8 * D:(8 + FT) * D].rearrange("p (t n) -> p t n", t=FT)
        m.ident, m.ones = sb("ident", [P, P]), sb("ones", [P, P])
        m.upto, m.after, m.before = sb("upto", [P, P]), sb("after", [P, P]), sb("before", [P, P])
        m.chunk_ones = sb("chunk_ones", [P, 2, P])
        m.expert_iota_i, m.expert_iota = sb("expert_iota_i", [P, EXPERTS], I32), sb("expert_iota", [P, EXPERTS])
        m.part_iota_i, m.part_iota = sb("part_iota_i", [P, 1], I32), sb("part_iota", [P, 1])
        m.codes_i = sb("codes_i", [P, 2 * TT], I32)
        m.cols, m.conv_cols = sb("vector_cols", [P, VROWS]), sb("conv_cols", [P, FROWS])
        m.gate_mix, m.gate_ffn = sb("gate_mix", [P, D]), sb("gate_ffn", [P, D])
        m.shift_mix, m.scale_mix = sb("shift_mix", [P, KT]), sb("scale_mix", [P, KT])
        m.shift_ffn, m.scale_ffn = sb("shift_ffn", [P, KT]), sb("scale_ffn", [P, KT])
        m.w13 = [b[:, 4 * j:4 * j + 4, :].rearrange("p a n -> p (a n)").rearrange("p (w k n) -> p w k n", w=2, k=KT)
                 for b in (m.b3, m.b1) for j in range(2)]
        m.w2 = [m.b2[:, 2 * j:2 * j + 2, :] for j in range(4)]
        m.w13_loaded = [ctx.enter_context(nc.semaphore(f"w13_loaded{u}")) for u in range(4)]
        m.w2_loaded = [ctx.enter_context(nc.semaphore(f"w2_loaded{u}")) for u in range(4)]
        m.scatter_idx, m.gather_idx = sb("scatter_idx", [SLOTS, EXPERTS], I32), sb("gather_idx", [SLOTS, EXPERTS], I32)
        m.gates2 = sb("expert_gates", [P, 2, TT])
        m.info_row, m.n_extra = sb("info_row", [1, 2 * P], I32), sb("n_extra", [1, 1], I32)
        m.info_dram = dram("block_info_d", (P, 2), I32)
        words = lambda b, t: b[:, t:t + 4, :].rearrange("p a n -> p (a n)").rearrange("p (t n) -> p t n", n=HALF)
        m.z, m.v, m.att = words(m.b4, 0), words(m.b4, 4), words(m.b1, 0)
        m.xf = [words(m.b1, 4), words(m.b3, 0)]
        m.dt, m.adt, m.d_skip = sb("dt", [P, TT, SH]), sb("adt", [P, TT, SH]), sb("d_skip_wide", [P, SH])
        m.codes = dram("slot_codes", (T * EXPERTS, 1), I32)
        m.bias_lines = dram("bias_lines", (AH, P, BAND + P))
        m.xn_dram = dram("normed_tokens", (T, D))
        m.contrib = dram("contributions", (2 * T, D))
        m.x2_dram = dram("x2", (T, D))
        m.x3_dram = dram("x3", (T, D))

        w1 = a["gla_w_in"][0]
        w2 = a["w_in_2"][0]
        c = lambda w, at, n=HALF: w[:, at:at + n]
        sources = [[c(w1, b * HALF)] for b in range(4)] + [[c(w1, 2064 + b * HALF)] for b in range(2)]
        sources += [[c(a["gla_w_o"][0], b * HALF)] for b in range(2)]
        sources += [[c(w2, at)] for at in (IN_AT["xbc"], IN_AT["xbc"] + HALF, IN_AT["q"], IN_AT["k"], IN_AT["z"], IN_AT["v"])]
        sources += [[c(a["w_out_2"][0], b * HALF)] for b in range(2)]
        sources += [[c(a["w_up_2"][0], f * 256, 256), c(a["w_up_2"][0], FDIM + f * 256, 256)] for f in range(FT // 2)]
        m.ring = Ring(nc, ctx, sources)

        x = a["x"][0]
        m.carried = ctx.enter_context(nc.semaphore("waits_carried"))
        col = lambda name: (lambda k: m.cols[:, VEC[name][0] + k:VEC[name][0] + k + 1])

        m.resets = sb("resets", [P, T])
        with nc.cleanup_on_exit():
            constants(nc, m, a)
            modulation(nc, m, a)
            rms_to_channels(nc, m, m.b2, m.b2, m.b1, col("attn_norm"), None, loads=x)
            with nc.sbuf_tensor("log_gates", [P, GH, T], F32) as m.gates:
                gla_projections(nc, m, a)
                gla_chunks(nc, m, a)
            gla_output(nc, m, a)
            project_back(nc, m, m.b1, m.b4, x, 6, (8, 10))
        with nc.cleanup_on_exit():
            rms_to_channels(nc, m, m.b4, m.b3, m.b1, col("ffn_norm"), None, to_dram=m.xn_dram)
            router(nc, m, a)
            experts(nc, m, a)
            more_blocks(nc, m, a)
            combine(nc, m, a)
        with nc.cleanup_on_exit():
            rms_to_channels(nc, m, m.b4, m.b3, m.b1, lambda k: m.scale_mix[:, k:k + 1], lambda k: m.shift_mix[:, k:k + 1])
            mixer_projections(nc, m, a)
            state_space(nc, m, a)
            band_attention(nc, m, a)
            mixer_norm(nc, m, a)
            project_back(nc, m, m.b2, m.b3, m.x2_dram, 14, (16, 18), gate=m.gate_mix)
            rms_to_channels(nc, m, m.b3, m.b4, m.b1, lambda k: m.scale_ffn[:, k:k + 1], lambda k: m.shift_ffn[:, k:k + 1],
                            spill=m.x3_dram)
            ffn_up(nc, m, a)
            ffn_down(nc, m, a)
            final_norm(nc, m, a, out)


INPUTS = ("a_log_2", "attn_norm", "b_ada_2", "c_2", "d_skip_2", "dt_bias_2", "ffn_conv_w_2", "ffn_norm",
          "final_norm", "final_norm_w_2", "gla_b_gate", "gla_out_norm", "gla_w_gate", "gla_w_in", "gla_w_o",
          "moe_w1", "moe_w2", "moe_w3", "moe_w_expert", "moe_w_group", "norm_ffn_w_2", "norm_mix_w_2",
          "rel_bias_2", "ssd_conv_b_2", "ssd_conv_w_2", "ssd_norm_w_2", "w_ada_2", "w_down_2", "w_in_2",
          "w_out_2", "w_up_2", "x")


def kernel(**inputs):
    import numpy as np
    import concourse.bacc as bacc
    from concourse import mybir
    from concourse.bass_utils import run_bass_kernel_spmd

    nc = bacc.Bacc("TRN2", target_bir_lowering=False, num_devices=1)
    arrays, aps = {}, {}
    for name in INPUTS:
        array = np.ascontiguousarray(inputs[name])
        arrays[f"in_{name}_dram"] = array
        aps[name] = nc.dram_tensor(f"in_{name}_dram", array.shape, mybir.dt.from_np(array.dtype), kind="ExternalInput").ap()
    out = nc.dram_tensor("out_0_dram", (1, T, D), mybir.dt.float32, kind="ExternalOutput").ap()
    program(nc, aps, out)
    result = run_bass_kernel_spmd(nc, [arrays], core_ids=[0])
    return result.results[0]["out_0_dram"]
```

```python
import numpy as np
import concourse.bass as bass
from concourse import mybir
from contextlib import ExitStack

F32 = mybir.dt.float32
F32R = mybir.dt.float32r
I32 = mybir.dt.int32
U32 = mybir.dt.uint32
ALU = mybir.AluOpType
ACT = mybir.ActivationFunctionType
AX = mybir.AxisListType

P = 128
T = 1024
D = 1024
TT = T // P
KT = D // P
HALF = 512
EPS = 1e-6
CH = 64

GH, GDK, GDV, RANK, TAU = 4, 128, 256, 16, 16.0
GROUPS, PER_GROUP, EXPERTS, FF = 8, 8, 64, 256
SLOTS = 64
NOWHERE = 8192
SH, SHD, SG, SN = 8, 64, 2, 128
HPG = SH // SG
TAPS = 4
AH, AHD = 8, 64
BANDT = 5
BAND = BANDT * P
NREL, MAXREL = 257, 128
MASKED = -1e30
FDIM = 2816
FT = FDIM // P
FTAPS = 3

IN_AT = {"z": 0, "xbc": 512, "dt": 1536, "q": 1544, "k": 2056, "v": 2568}

VEC = {}
_row = 0
for _name, _n in (("attn_norm", KT), ("ffn_norm", KT), ("gla_b_gate", GH), ("norm_mix_w_2", KT), ("norm_ffn_w_2", KT),
                  ("ssd_norm_w_2", 4), ("ssd_conv_b_2", KT), ("ssd_conv_w_2", TAPS * KT), ("c_2", KT)):
    VEC[_name] = (_row, _n)
    _row += _n
VROWS = _row
FROWS = FTAPS * 2 * FT
FSPLIT = FROWS // 2


_names = {}


def fresh(name):
    _names[name] = _names.get(name, 0) + 1
    return f"{name}_{_names[name]}"


def rows_of(ap):
    return ap.rearrange("(r c) -> r c", c=P)


def spread(ap, n=P):
    return ap.to_broadcast([n, ap.shape[1]])


class Parts:
    pass


def carry(engine, m):
    engine.sem_inc(m.carried, 1)


_rounded = {}


def both_kinds(nc, ctx, name, shape, parts=1, part=None):
    start = -(-nc.sbuf_base // 32) * 32
    t = ctx.enter_context(nc.sbuf_tensor(name, shape, F32))
    words = int(np.prod(shape[1:]))
    assert nc.sbuf_base == start + 4 * words
    part = part or words
    _rounded[t.name] = (part, [nc.alloc_sbuf_tensor_at(f"{name}_rounded{i}", [P, part], F32R, offset=start + 4 * part * i)
                               for i in range(parts)])
    return t


def R(ap):
    part, tensors = _rounded[ap.tensor.name]
    return bass.AP(tensor=tensors[ap.offset // part], offset=ap.offset % part, ap=[[part, P]] + list(ap.ap)[1:])


def rounded(ap):
    return R(ap).bitcast(F32)


def by_tile(buf):
    return lambda k: buf[:, k, :]



def transposes(pe, m, src, tiles_ready, ps, ps_ready, ps_free):
    for n in range(2 * KT):
        k, half = n // 2, n % 2
        if n == 0:
            tiles_ready(pe)
        if n >= 4:
            pe.wait_ge(ps_free, n - 3)
        for j in range(4):
            last = pe.transpose(ps[:, n % 4, j * P:(j + 1) * P], src[:, 4 * half + j, k * P:(k + 1) * P],
                                m.ident[:, :])
        last.then_inc(ps_ready, 1)


def transposes_out(dve, dst, gain, bias, ps, ps_ready, ps_free, high=None, high_made=None):
    def low_part(k):
        dve.wait_ge(high_made, k + 1)
        dve.tensor_tensor(R(dst(k)), dst(k), rounded(high(k)), ALU.subtract)

    for n in range(2 * KT):
        k, half = n // 2, n % 2
        dve.wait_ge(ps_ready, n + 1)
        out = dst(k)[:, half * HALF:(half + 1) * HALF]
        g = gain(k)
        if g is None:
            ins = dve.tensor_copy(out, ps[:, n % 4, :])
        elif bias is None:
            ins = dve.tensor_scalar(out, ps[:, n % 4, :], g, None, ALU.mult)
        else:
            ins = dve.tensor_scalar(out, ps[:, n % 4, :], g, bias(k), ALU.mult, ALU.add)
        ins.then_inc(ps_free, 1)
        if high is not None and n % 2 == 1 and k > 0:
            low_part(k - 1)
    if high is not None:
        low_part(KT - 1)


def high_parts(act, src, high, ps_free, high_made):
    for k in range(KT):
        act.wait_ge(ps_free, 2 * k + 2)
        act.activation(R(high(k)), src(k), ACT.Copy).then_inc(high_made, 1)


def inverse_rms(act, dve, ss, root, inv, width, squares, roots):
    if act is not None:
        act.wait_ge(squares, 1)
        act.activation(root, ss, ACT.Sqrt).then_inc(roots, 1)
    if dve is not None:
        dve.wait_ge(roots, 1)
        dve.reciprocal(inv, root)
        dve.drain()


def rms_to_channels(nc, m, src, xn, dst, gain, bias, high=None, loads=None, to_dram=None, spill=None):
    with ExitStack() as ctx:
        sem = lambda n: nc.alloc_semaphore(fresh(n))
        arrived = [sem(f"x_tile_arrived{t}") for t in range(TT)] if loads is not None else None
        squares, roots, scaled = sem("squares_summed"), sem("roots_taken"), sem("tiles_scaled")
        ps_ready, ps_free, stored = sem("transposed"), sem("transposed_out"), sem("normed_stored")
        ss = ctx.enter_context(nc.sbuf_tensor(fresh("sum_sq"), [P, TT], F32))
        root = ctx.enter_context(nc.sbuf_tensor(fresh("root"), [P, TT], F32))
        inv = ctx.enter_context(nc.sbuf_tensor(fresh("inv_rms"), [P, TT], F32))
        junk = ctx.enter_context(nc.sbuf_tensor(fresh("squares"), [P, D], F32))
        sums, high_made = sem("act_sums"), sem("high_made")
        ps = ctx.enter_context(nc.psum_tensor(fresh("ps_transposed"), [P, 4, HALF], F32))
        block = ctx.enter_context(nc.Block())

        @block.sync
        def _(sp):
            if loads is not None:
                for t in range(TT):
                    sp.dma_start(src[:, t, :], loads[t * P:(t + 1) * P, :]).then_inc(arrived[t], 16)
            if spill is not None:
                sp.dma_start(spill.rearrange("(t p) d -> p t d", p=P), src).then_inc(stored, 16)
                sp.wait_ge(stored, 16)
            if to_dram is not None:
                sp.wait_ge(scaled, TT)
                sp.dma_start(to_dram.rearrange("(t p) d -> p t d", p=P), xn).then_inc(stored, 16)
                sp.wait_ge(stored, 16)

        @block.scalar
        def _(act):
            for t in range(TT):
                if arrived:
                    act.wait_ge(arrived[t], 16)
                act.activation(junk[:, :], src[:, t, :], ACT.Square, accum_out=ss[:, t:t + 1]).then_inc(sums, 1)
                act.drain()
            inverse_rms(act, None, ss[:, :], root[:, :], None, D, squares, roots)
            if high is not None:
                high_parts(act, by_tile(dst), by_tile(high), ps_free, high_made)

        @block.vector
        def _(dve):
            dve.wait_ge(sums, TT)
            dve.tensor_scalar(ss[:, :], ss[:, :], 1.0 / D, EPS, ALU.mult, ALU.add).then_inc(squares, 1)
            inverse_rms(None, dve, None, root[:, :], inv[:, :], D, squares, roots)
            for t in range(TT):
                dve.tensor_scalar(xn[:, t, :], src[:, t, :], inv[:, t:t + 1], None, ALU.mult).then_inc(scaled, 1)
            transposes_out(dve, by_tile(dst), gain, bias, ps, ps_ready, ps_free, None if high is None else by_tile(high), high_made)

        @block.tensor
        def _(pe):
            transposes(pe, m, xn, lambda e: e.wait_ge(scaled, TT), ps, ps_ready, ps_free)


class Ring:

    def __init__(self, nc, ctx, sources):
        self.buf = both_kinds(nc, ctx, "weight_ring", [P, 4, KT // 2, HALF])
        self.low = [self.buf[:, s] for s in range(2)]
        self.high = [self.buf[:, 2 + s] for s in range(2)]
        self.loaded = [ctx.enter_context(nc.semaphore(f"weights_loaded{s}")) for s in range(2)]
        self.used = ctx.enter_context(nc.semaphore("weights_used"))
        self.high_made = ctx.enter_context(nc.semaphore("weights_high"))
        self.split = ctx.enter_context(nc.semaphore("weights_split"))
        self.sources, self.issued = sources, 0

    def issue(self, sp, end):
        for i in range(self.issued, end):
            if i >= 2:
                sp.wait_ge(self.used, i - 1)
            at, h = 0, i % 2
            for src in self.sources[i // 2]:
                n = src.shape[1]
                sp.dma_start(self.low[h][:, :, at:at + n],
                             src[h * D // 2:(h + 1) * D // 2, :].rearrange("(k p) n -> p k n", p=P)).then_inc(self.loaded[h], 16)
                at += n
        self.issued = end

    def loads_before(self, b):
        return 16 * sum(len(self.sources[c]) for c in range(b + 1))

    def make_high(self, act, i):
        act.wait_ge(self.loaded[i % 2], self.loads_before(i // 2))
        act.activation(R(self.high[i % 2]), self.low[i % 2], ACT.Copy).then_inc(self.high_made, 1)

    def make_low(self, dve, i):
        dve.wait_ge(self.high_made, i + 1)
        dve.tensor_tensor(R(self.low[i % 2]), self.low[i % 2], rounded(self.high[i % 2]), ALU.subtract).then_inc(self.split, 1)

    def release(self, engine):
        engine.sem_inc(self.used, 1)


def evacuate_split(act, m, blocks, evacuate, before_last=None):
    first, end = blocks
    for i in range(2):
        m.ring.make_high(act, 2 * first + i)
    if before_last is not None:
        before_last()
    for b in range(first, end):
        for j in range(8):
            evacuate((b - first) * 8 + j, j == 7)
            if j == 2 and b + 1 < end:
                m.ring.make_high(act, 2 * b + 2)
        if b + 1 < end:
            m.ring.make_high(act, 2 * b + 3)


def gemm(pe, m, acts, weights_ready, n0, ps, ps_ready, ps_free, tokens, tiles=range(4)):
    for h in range(2):
        weights_ready(h)
        weights = (m.ring.high[h], m.ring.low[h]) if len(acts) == 2 else (m.ring.low[h],)
        pairs = ((0, 0), (0, 1), (1, 0)) if len(acts) == 2 else ((0, 0),)
        view = R if len(acts) == 2 else (lambda ap: ap)
        for n in range(8):
            if h == 0:
                pe.wait_ge(ps_free, n0 + n + 1)
            for k in range(4):
                for i, j in pairs:
                    first, final = h == k == i == j == 0, h == 1 and k == 3 and (i, j) == pairs[-1]
                    if tokens:
                        left, right = acts[i](4 * h + k)[:, n * P:(n + 1) * P], weights[j][:, k, :]
                    else:
                        c, half = tiles[n // 2], n % 2
                        left, right = weights[i][:, k, c * P:(c + 1) * P], acts[j](4 * h + k)[:, half * HALF:(half + 1) * HALF]
                    last = pe.matmul(ps[:, n, :], view(left), view(right), start=first, stop=final)
            if h == 1:
                last.then_inc(ps_ready, 1)
            elif n == 7:
                last.then_inc(m.ring.used, 1)


def store_stage(act, sp_free, n):
    if n >= 4:
        act.wait_ge(sp_free[n % 4], 16 * (n // 4))



def constants(nc, m, a):
    with ExitStack() as ctx:
        sem = lambda n: nc.alloc_semaphore(fresh(n))
        sb = lambda n, s, d=F32: ctx.enter_context(nc.sbuf_tensor(n, s, d))
        rows_arrived, rel_arrived, made, cast = sem("rows_arrived"), sem("rel_arrived"), sem("masks_made"), sem("columns")
        frows_arrived, bias_rows, bias_stored, filled = sem("conv_rows"), sem("bias_rows"), sem("bias_stored"), sem("filled")
        vrows = sb("vector_rows", [VROWS, P])
        frows = sb("conv_rows", [FSPLIT, 2, P])
        rel = sb("rel_bias_rows", [AH, NREL])
        line = sb("bias_line", [AH, BAND + P])
        nowhere = sb("nowhere", [P, T * EXPERTS // P], I32)
        ps = ctx.enter_context(nc.psum_tensor("ps_columns", [P, 3, HALF], F32))
        block = ctx.enter_context(nc.Block())

        @block.sync
        def _(sp):
            for name, (row, n) in VEC.items():
                src = a[name]
                if name == "ssd_conv_w_2":
                    src = src[0].rearrange("k (r c) -> (k r) c", c=P)
                else:
                    src = rows_of(src[0] if len(src.shape) == 2 else src)
                sp.dma_start(vrows[row:row + n, :], src).then_inc(rows_arrived, 16)
            conv = a["ffn_conv_w_2"][0].rearrange("k (r c) -> (k r) c", c=P)
            for s in range(2):
                sp.dma_start(frows[:, s, :], conv[s * FSPLIT:(s + 1) * FSPLIT, :]).then_inc(frows_arrived, 16)
            sp.dma_start(rel[:, :], a["rel_bias_2"][0]).then_inc(rel_arrived, 16)
            m.ring.issue(sp, 2)
            sp.wait_ge(filled, 1)
            sp.dma_start(m.codes.rearrange("(p n) o -> p (n o)", p=P), nowhere[:, :]).then_inc(bias_stored, 16)
            sp.wait_ge(bias_rows, 1)
            for h in range(AH):
                sp.dma_start(m.bias_lines[h], line[h:h + 1, None, :].to_broadcast([1, P, BAND + P])).then_inc(bias_stored, 16)
            sp.wait_ge(bias_stored, 16 * (AH + 1))

        @block.gpsimd
        def _(pool):
            pool.memset(m.ident[:, :], 0.0)
            pool.memset(m.ones[:, :], 1.0)
            pool.memset(m.upto[:, :], 1.0)
            pool.memset(m.after[:, :], 1.0)
            pool.memset(m.before[:, :], 1.0)
            pool.memset(m.chunk_ones[:, :, :], 0.0)
            pool.memset(nowhere[:, :], NOWHERE)
            pool.drain()
            pool.affine_select(out=m.ident[:, :], in_=m.ident[:, :], compare_op=ALU.not_equal, fill=1.0, base=0,
                               pattern=[[-1, P]], channel_multiplier=1)
            pool.affine_select(out=m.upto[:, :], in_=m.upto[:, :], compare_op=ALU.is_ge, fill=0.0, base=0,
                               pattern=[[1, P]], channel_multiplier=-1)
            pool.affine_select(out=m.after[:, :], in_=m.after[:, :], compare_op=ALU.is_gt, fill=0.0, base=0,
                               pattern=[[-1, P]], channel_multiplier=1)
            pool.affine_select(out=m.before[:, :], in_=m.before[:, :], compare_op=ALU.is_gt, fill=0.0, base=0,
                               pattern=[[1, P]], channel_multiplier=-1)
            pool.drain()
            pool.memset(m.upto[0:CH, CH:P], 0.0)
            pool.drain()
            pool.memset(m.after[CH:P, 0:CH], 0.0)
            for c in range(2):
                pool.drain()
                pool.memset(m.chunk_ones[c * CH:(c + 1) * CH, c, :], 1.0)
            pool.drain()
            pool.memset(m.resets[:, :], 1.0)
            pool.drain()
            pool.memset(m.resets[:, :].rearrange("p (n c) -> p n c", c=CH)[:, :, 0:1], 0.0)
            pool.iota(m.expert_iota_i[:, :], pattern=[[1, EXPERTS]], base=0, channel_multiplier=0)
            pool.iota(m.codes_i[:, :], pattern=[[T, 2], [P, TT]], base=0, channel_multiplier=1)
            pool.iota(m.part_iota_i[:, :], pattern=[[0, 1]], base=0, channel_multiplier=1)
            pool.drain()
            pool.tensor_copy(m.expert_iota[:, :], m.expert_iota_i[:, :])
            pool.tensor_copy(m.part_iota[:, :], m.part_iota_i[:, :])
            pool.drain()
            pool.sem_inc(made, 1)
            pool.sem_inc(filled, 1)

        @block.tensor
        def _(pe):
            pe.wait_ge(made, 1)
            pe.wait_ge(rows_arrived, 16 * len(VEC))
            pe.transpose(ps[:, 0, 0:VROWS], vrows[:, :], m.ident[0:VROWS, 0:VROWS])
            pe.wait_ge(frows_arrived, 32)
            pe.transpose(ps[:, 1, 0:FSPLIT], frows[:, 0, :], m.ident[0:FSPLIT, 0:FSPLIT])
            pe.transpose(ps[:, 2, 0:FSPLIT], frows[:, 1, :], m.ident[0:FSPLIT, 0:FSPLIT]).then_inc(cast, 1)

        @block.vector
        def _(dve):
            dve.wait_ge(rel_arrived, 16)
            far = BAND + P - 1 - (NREL - 2)
            dve.memset(line[:, :], 0.0)
            dve.drain()
            dve.tensor_scalar(line[:, 0:far + 1], line[:, 0:far + 1], rel[:, NREL - 1:NREL], None, ALU.add)
            dve.drain()
            dve.tensor_copy(line[:, far:far + NREL - 2], rel[:, NREL - 2:0:-1]).then_inc(bias_rows, 1)
            dve.wait_ge(cast, 1)
            dve.tensor_copy(m.cols[:, :], ps[:, 0, 0:VROWS])
            dve.tensor_copy(m.conv_cols[:, 0:FSPLIT], ps[:, 1, 0:FSPLIT])
            dve.tensor_copy(m.conv_cols[:, FSPLIT:FROWS], ps[:, 2, 0:FSPLIT])
            dve.drain()



def modulation(nc, m, a):
    NB = 6 * D // HALF
    with ExitStack() as ctx:
        sem = lambda n: nc.alloc_semaphore(fresh(n))
        sb = lambda n, s, d=F32: ctx.enter_context(nc.sbuf_tensor(n, s, d))
        c_act = sb("c_act", [P, KT])
        c_wide = sb("c_wide", [P, KT, P])
        mod = m.big[:, 0:6 * D]
        w = [m.big[:, 6 * D + s * KT * HALF:6 * D + (s + 1) * KT * HALF].rearrange("p (k n) -> p k n", k=KT)
             for s in range(4)]
        b_row = sb("b_ada_row", [1, 6 * D])
        ps = ctx.enter_context(nc.psum_tensor("ps_mod", [P, 4, HALF], F32))
        pst = ctx.enter_context(nc.psum_tensor("ps_mod_t", [P, 4, HALF], F32))
        loaded = [sem(f"ada_loaded{s}") for s in range(4)]
        bias_row, activated, wide = sem("ada_bias"), sem("c_activated"), sem("c_widened")
        ps_ready, ps_free, turned = sem("mod_ready"), sem("mod_free"), sem("mod_turned")
        block = ctx.enter_context(nc.Block())

        @block.sync
        def _(sp):
            sp.dma_start(b_row[:, :], a["b_ada_2"]).then_inc(bias_row, 16)
            for b in range(NB):
                if b >= 4:
                    sp.wait_ge(ps_ready, b - 3)
                sp.dma_start(w[b % 4], a["w_ada_2"][0][:, b * HALF:(b + 1) * HALF]
                             .rearrange("(k p) n -> p k n", p=P)).then_inc(loaded[b % 4], 16)

        @block.scalar
        def _(act):
            row, n = VEC["c_2"]
            act.activation(c_act[:, :], m.cols[:, row:row + n], ACT.Silu).then_inc(activated, 1)

        @block.vector
        def _(dve):
            dve.wait_ge(activated, 1)
            dve.tensor_copy(c_wide[:, :, :], c_act[:, :, None].to_broadcast([P, KT, P])).then_inc(wide, 1)
            for b in range(NB):
                dve.wait_ge(ps_ready, b + 1)
                dve.tensor_copy(mod[:, b * HALF:(b + 1) * HALF], ps[:, b % 4, :]).then_inc(ps_free, 1)
            dve.drain()
            dve.tensor_copy(m.gate_mix[:, :], mod[:, 2 * D:3 * D])
            dve.tensor_copy(m.gate_ffn[:, :], mod[:, 5 * D:6 * D])
            for i, (dst, gain) in enumerate(((m.shift_mix, None), (m.scale_mix, "norm_mix_w_2"),
                                             (m.shift_ffn, None), (m.scale_ffn, "norm_ffn_w_2"))):
                for half in range(2):
                    n = 2 * i + half
                    dve.wait_ge(turned, n + 1)
                    src = pst[:, n % 4, :].rearrange("p (j c) -> p j c", j=4)[:, :, 0:1]
                    out = dst[:, 4 * half:4 * half + 4, None]
                    if gain is None:
                        dve.tensor_copy(out, src).then_inc(ps_free, 1)
                    else:
                        row = VEC[gain][0] + 4 * half
                        dve.tensor_scalar(out, src, 1.0, None, ALU.add).then_inc(ps_free, 1)
                        dve.drain()
                        dve.tensor_tensor(out, out, m.cols[:, row:row + 4, None], ALU.mult)
            dve.drain()

        @block.tensor
        def _(pe):
            pe.wait_ge(wide, 1)
            pe.wait_ge(bias_row, 16)
            for b in range(NB):
                pe.wait_ge(loaded[b % 4], 16 * (b // 4 + 1))
                if b >= 4:
                    pe.wait_ge(ps_free, b - 3)
                for k in range(KT):
                    pe.matmul(ps[:, b % 4, :], c_wide[:, k, :], w[b % 4][:, k, :], start=(k == 0), stop=False)
                pe.matmul(ps[:, b % 4, :], m.ones[0:1, :], b_row[:, b * HALF:(b + 1) * HALF],
                          start=False, stop=True).then_inc(ps_ready, 1)
            pe.wait_ge(ps_free, NB)
            for i, part in enumerate((0, 1, 3, 4)):
                for half in range(2):
                    n = 2 * i + half
                    if n >= 4:
                        pe.wait_ge(ps_free, NB + n - 3)
                    for j in range(4):
                        at = part * D + (4 * half + j) * P
                        last = pe.transpose(pst[:, n % 4, j * P:(j + 1) * P], mod[:, at:at + P], m.ident[:, :])
                    last.then_inc(turned, 1)



def gla_projections(nc, m, a):
    acts = (by_tile(m.b1), by_tile(m.b4))
    qk, v = m.b2, m.b3
    with ExitStack() as ctx:
        sem = lambda n: nc.alloc_semaphore(fresh(n))
        sb = lambda n, s, d=F32: ctx.enter_context(nc.sbuf_tensor(n, s, d))
        w_lr = [both_kinds(nc, ctx, f"w_low_rank{i}", [P, KT, RANK]) for i in range(2)]
        mag = m.b3[:, 0:GH, :]
        lrT = m.b3[0:RANK, GH, :]
        w_gate = m.b3[0:RANK, GH + 1, 0:GH * GDK]
        stage = sb("r_stage", [P, 4, HALF])
        gates = m.gates
        ps = ctx.enter_context(nc.psum_tensor("ps_gla_in", [P, 8, HALF], F32))
        ps_lr = ps[:, 6:8, :]
        small_loaded, ps_ready, ps_free = sem("gate_weights"), sem("proj_ready"), sem("proj_free")
        lr_high, lr_split, staged = sem("lr_high"), sem("lr_split"), sem("r_staged")
        stored = [sem(f"r_stored{s}") for s in range(4)]
        lr_ready, lr_sb, gate_ready, gate_free = sem("lr_ready"), sem("lr_in_sbuf"), sem("gate_ready"), sem("gate_free")
        biased, logged, scanned = sem("biased"), sem("logged"), sem("scanned")
        block = ctx.enter_context(nc.Block())
        a_col = 2 * GH * GDK + GH * GDV

        @block.sync
        def _(sp):
            with nc.allow_non_contiguous_dma(reason="sixteen columns of w_in"):
                sp.dma_start(w_lr[1][:, :, :], a["gla_w_in"][0][:, a_col:a_col + RANK]
                             .rearrange("(k p) n -> p k n", p=P)).then_inc(small_loaded, 16)
            sp.dma_start(w_gate, a["gla_w_gate"][0]).then_inc(small_loaded, 16)
            for b in (4, 5):
                m.ring.issue(sp, 2 * b + 3)
                for t in range(TT):
                    n = (b - 4) * TT + t
                    sp.wait_ge(staged, n + 1)
                    sp.dma_start(m.r_dram[t * P:(t + 1) * P, (b - 4) * HALF:(b - 3) * HALF], stage[:, n % 4, :])\
                        .then_inc(stored[n % 4], 16)
                m.ring.issue(sp, 2 * b + 4)
            for s in range(4):
                sp.wait_ge(stored[s], 16 * 4)

        @block.tensor
        def _(pe):
            pe.wait_ge(lr_split, 1)
            for half in range(2):
                for k in range(KT):
                    for i, j in ((0, 0), (0, 1), (1, 0)):
                        last = pe.matmul(ps_lr[0:RANK, half, :], R(w_lr[i][:, k, :]), R(acts[j](k)[:, half * HALF:(half + 1) * HALF]),
                                         start=(k == i == j == 0), stop=(k == KT - 1 and i == 1))
            last.then_inc(lr_ready, 1)
            pe.wait_ge(small_loaded, 32)
            pe.wait_ge(lr_sb, 1)
            for n in range(2 * GH):
                if n >= 2:
                    pe.wait_ge(gate_free, n - 1)
                pe.matmul(ps_lr[:, n % 2, :], w_gate[:, (n // 2) * P:(n // 2 + 1) * P],
                          lrT[:, (n % 2) * HALF:(n % 2 + 1) * HALF], start=True, stop=True).then_inc(gate_ready, 1)
            pe.wait_ge(gate_free, 2 * GH)
            for first, tokens in ((0, False), (2, True)):
                with pe.Fori(0, 2 if first == 0 else 4) as i:
                    gemm(pe, m, acts, lambda h: pe.wait_ge(m.ring.split, i * 2 + (2 * first + h + 1)), i * 8 + 8 * first,
                         ps, ps_ready, ps_free, tokens)

        @block.vector
        def _(dve):
            dve.wait_ge(lr_high, 1)
            dve.tensor_tensor(R(w_lr[1][:, :, :]), w_lr[1][:, :, :], rounded(w_lr[0][:, :, :]), ALU.subtract).then_inc(lr_split, 1)
            for i in range(2):
                m.ring.make_low(dve, i)
            dve.wait_ge(lr_ready, 1)
            dve.tensor_copy(lrT[:, :].rearrange("p (h n) -> p h n", h=2), ps_lr[0:RANK, :, :]).then_inc(lr_sb, 1)
            row = VEC["gla_b_gate"][0]
            for n in range(2 * GH):
                dve.wait_ge(gate_ready, n + 1)
                dve.tensor_scalar(gates[:, n // 2, (n % 2) * HALF:(n % 2 + 1) * HALF], ps_lr[:, n % 2, :],
                                  m.cols[:, row + n // 2:row + n // 2 + 1], None, ALU.add).then_inc(gate_free, 1)
            dve.drain()
            dve.tensor_scalar(mag[:, :, :], gates[:, :, :], -1.0, None, ALU.mult)
            dve.drain()
            dve.tensor_tensor(mag[:, :, :], mag[:, :, :], gates[:, :, :], ALU.max).then_inc(biased, 1)
            dve.wait_ge(logged, 1)
            dve.tensor_scalar(gates[:, :, :], gates[:, :, :], 0.0, None, ALU.min)
            dve.drain()
            dve.tensor_tensor(gates[:, :, :], gates[:, :, :], mag[:, :, :], ALU.subtract)
            dve.drain()
            dve.tensor_scalar(mag[:, :, :], gates[:, :, :], 1.0 / TAU, None, ALU.mult)
            dve.drain()
            for h in range(GH):
                dve.tensor_tensor_scan(gates[:, h, :], m.resets[:, :], mag[:, h, :], 0.0, ALU.mult, ALU.add)\
                    .then_inc(scanned, 1)
            for i in range(2, 12):
                m.ring.make_low(dve, i)

        @block.scalar
        def _(act):
            act.wait_ge(small_loaded, 32)
            act.activation(R(w_lr[0][:, :, :]), w_lr[1][:, :, :], ACT.Copy).then_inc(lr_high, 1)
            act.sem_inc(ps_free, 8)

            def magnitudes():
                act.wait_ge(biased, 1)
                act.activation(mag[:, :, :], mag[:, :, :], ACT.Exp, scale=-1.0)
                act.drain()
                act.activation(mag[:, :, :], mag[:, :, :], ACT.Ln, bias=1.0).then_inc(logged, 1)

            def evacuate(n, last):
                act.wait_ge(ps_ready, n + 1)
                if last:
                    m.ring.release(act)
                src, t, cols = ps[:, n % 8, :], n % 8, slice((n // 8 % 2) * HALF, (n // 8 % 2 + 1) * HALF)
                if n < 16:
                    out = qk[:, n // 2, (n % 2) * HALF:(n % 2 + 1) * HALF]
                    if n // 2 < GH:
                        act.mul(out, src, float(GDK) ** -0.5).then_inc(ps_free, 1)
                    else:
                        act.copy(out, src).then_inc(ps_free, 1)
                elif n < 32:
                    if n == 16:
                        act.wait_ge(scanned, GH)
                    act.copy(v[:, t, cols], src).then_inc(ps_free, 1)
                else:
                    store_stage(act, stored, n - 32)
                    act.copy(stage[:, n % 4, :], src)
                    act.drain()
                    act.sem_inc(staged, 1)
                    act.sem_inc(ps_free, 1)

            evacuate_split(act, m, (0, 6), evacuate, magnitudes)


def gla_chunks(nc, m, a):
    qk, v, gates = m.b2, m.b3, m.gates
    with ExitStack() as ctx:
        sem = lambda n: nc.alloc_semaphore(fresh(n))
        sb = lambda n, s, d=F32: ctx.enter_context(nc.sbuf_tensor(n, s, d))
        W = GH * P
        diff = [m.b1[:, 0:1, s * W:(s + 1) * W].rearrange("p o (h n) -> p (o h) n", h=GH) for s in range(2)]
        e = {n: m.b1[:, 1 + i // 2, (i % 2) * W:(i % 2 + 1) * W].rearrange("p (h n) -> p h n", h=GH)
             for i, n in enumerate(("up", "down", "full", "left"))}
        qi, ki, qn, ks = (m.b1[:, 3 + i // 2, (i % 2) * W:(i % 2 + 1) * W].rearrange("p (h n) -> p h n", h=GH)
                          for i in range(4))
        v_now = m.b1[:, 5, :]
        decay = sb("chunk_decay", [P, GH, 2])
        att = sb("att", [P, 2, P])
        kst = sb("k_state_tokens", [P, 2, P])
        S = sb("state", [P, GH, GDV])
        S_mid = sb("state_mid", [P, GH, GDV])
        psA = ctx.enter_context(nc.psum_tensor("ps_att", [P, 2, HALF], F32))
        psO = ctx.enter_context(nc.psum_tensor("ps_o", [P, 2, HALF], F32))
        psU = ctx.enter_context(nc.psum_tensor("ps_update", [P, 2, 2, HALF], F32))
        diffs, exps, scaled, v_copied = sem("diffs"), sem("exps"), sem("scaled"), sem("v_copied")
        att_ready, att_masked, kst_sb = sem("att_ready"), sem("att_masked"), sem("kst_sb")
        upd_ready, mid_ready, state_ready = sem("update_ready"), sem("mid_state"), sem("state_ready")
        o_ready, o_copied = sem("o_ready"), sem("o_copied")
        block = ctx.enter_context(nc.Block())

        @block.vector
        def _(dve):
            dve.memset(S[:, :, :], 0.0).then_inc(state_ready, GH)
            dve.memset(S_mid[:, :, :], 0.0)
            dve.drain()
            with dve.Fori(0, TT) as p:
                now = lambda buf, c0: buf[:, c0:c0 + GH, bass.ds(p * P, P)]
                g4 = now(gates, 0).rearrange("p h (c n) -> p h c n", c=2)
                d0 = diff[0].rearrange("p h (c n) -> p h c n", c=2)
                d1 = diff[1].rearrange("p h (c n) -> p h c n", c=2)
                for h in range(GH):
                    mid = g4[:, h, :, CH // 2:CH // 2 + 1].to_broadcast([P, 2, CH])
                    end = g4[:, h, :, CH - 1:CH].to_broadcast([P, 2, CH])
                    dve.tensor_tensor(d0[:, h], g4[:, h], mid, ALU.subtract)
                    last = dve.tensor_tensor(d1[:, h], end, g4[:, h], ALU.subtract)
                last.then_inc(diffs, 1)
                dve.wait_ge(exps, p + 1)
                dve.tensor_tensor(qi, now(qk, 0), e["up"], ALU.mult)
                dve.tensor_tensor(ki, now(qk, GH), e["down"], ALU.mult)
                dve.tensor_tensor(qn, now(qk, 0), e["full"], ALU.mult)
                dve.tensor_tensor(ks, now(qk, GH), e["left"], ALU.mult).then_inc(scaled, 1)
                for h in range(GH):
                    u = h % 2
                    dve.wait_ge(att_ready, p * GH + h + 1)
                    dve.tensor_tensor(att[:, u, :], psA[:, u, 0:P], m.upto[:, :], ALU.mult).then_inc(att_masked, 1)
                    dve.tensor_copy(kst[:, u, :], psA[:, u, P:2 * P]).then_inc(kst_sb, 1)
                    dve.wait_ge(upd_ready, p * GH + h + 1)
                    dve.scalar_tensor_tensor(S_mid[:, h, :], S[:, h, :], decay[:, h, 0:1], psU[:, u, 0, 0:GDV],
                                             ALU.mult, ALU.add).then_inc(mid_ready, 1)
                    dve.drain()
                    dve.wait_ge(o_ready, p * GH + h + 1)
                    dve.scalar_tensor_tensor(S[:, h, :], S_mid[:, h, :], decay[:, h, 1:2],
                                             psU[:, u, 1, 0:GDV], ALU.mult, ALU.add).then_inc(state_ready, 1)

        @block.scalar
        def _(act):
            act.sem_inc(o_copied, 2)
            with act.Fori(0, TT) as p:
                act.copy(v_now, v[:, p, :]).then_inc(v_copied, 1)
                act.wait_ge(diffs, p + 1)
                g_now = gates[:, :, bass.ds(p * P, P)]
                act.activation(e["up"], diff[0], ACT.Exp)
                act.activation(e["down"], diff[0], ACT.Exp, scale=-1.0)
                act.activation(e["full"], g_now, ACT.Exp)
                act.activation(e["left"], diff[1], ACT.Exp)
                act.activation(decay[:, :, :],
                               g_now.rearrange("p h (c n) -> p h c n", c=2)[:, :, :, CH - 1], ACT.Exp).then_inc(exps, 1)
                for h in range(GH):
                    act.wait_ge(o_ready, p * GH + h + 1)
                    carry(act, m)
                    act.copy(v[:, p, h * GDV:(h + 1) * GDV], psO[:, h % 2, 0:GDV]).then_inc(o_copied, 1)

        @block.tensor
        def _(pe):
            with pe.Fori(0, TT) as p:
                pe.wait_ge(scaled, p + 1)
                pe.wait_ge(v_copied, p + 1)
                for h in range(GH):
                    u = h % 2
                    vh = v_now[:, h * GDV:(h + 1) * GDV]
                    pe.matmul(psA[:, u, 0:P], ki[:, h, :], qi[:, h, :], start=True, stop=True)
                    pe.transpose(psA[:, u, P:2 * P], ks[:, h, :], m.ident[:, :]).then_inc(att_ready, 1)
                    pe.wait_ge(kst_sb, p * GH + h + 1)
                    pe.wait_ge(state_ready, p * GH + h + GH - 1)
                    for c in range(2):
                        last = pe.matmul(psU[:, u, c, 0:GDV], kst[c * CH:(c + 1) * CH, u, :],
                                         vh[c * CH:(c + 1) * CH, :], start=True, stop=True)
                    last.then_inc(upd_ready, 1)
                    pe.wait_ge(att_masked, p * GH + h + 1)
                    pe.wait_ge(o_copied, p * GH + h + 1)
                    pe.wait_ge(state_ready, p * GH + h + 1)
                    for c, state in enumerate((S, S_mid)):
                        part = slice(c * CH, (c + 1) * CH)
                        pe.matmul(psO[part, u, 0:GDV], att[:, u, part], vh, start=True, stop=False)
                        if c == 1:
                            pe.wait_ge(mid_ready, p * GH + h + 1)
                        last = pe.matmul(psO[part, u, 0:GDV], qn[:, h, part], state[:, h, :], start=False, stop=True)
                    last.then_inc(o_ready, 1)


def gla_output(nc, m, a):
    o, r, yT = m.b3, m.b4, (by_tile(m.b1), by_tile(m.b2))
    with ExitStack() as ctx:
        sem = lambda n: nc.alloc_semaphore(fresh(n))
        sb = lambda n, s, d=F32: ctx.enter_context(nc.sbuf_tensor(n, s, d))
        ss, root, inv = sb("o_ss", [P, TT * GH]), sb("o_root", [P, TT * GH]), sb("o_inv", [P, TT * GH])
        junk = sb("o_squares", [P, GDV])
        gain = sb("out_norm", [P, GDV])
        ps = ctx.enter_context(nc.psum_tensor("ps_yT", [P, 4, HALF], F32))
        gain_arrived, summed, squares, roots, gated = (sem(n) for n in ("gain_arrived", "o_summed", "o_meaned", "o_rooted", "gated"))
        normed, ps_ready, ps_free, high_made = sem("o_normed"), sem("yT_ready"), sem("yT_free"), sem("yT_high")
        r_arrived = [sem(f"r_arrived{t}") for t in range(TT)]
        block = ctx.enter_context(nc.Block())

        @block.sync
        def _(sp):
            sp.dma_start(gain[:, :], spread(a["gla_out_norm"])).then_inc(gain_arrived, 16)
            for t in range(TT):
                sp.dma_start(r[:, t, :], m.r_dram[t * P:(t + 1) * P, :]).then_inc(r_arrived[t], 16)

        @block.scalar
        def _(act):
            for t in range(TT):
                for h in range(GH):
                    act.activation(junk[:, :], o[:, t, h * GDV:(h + 1) * GDV], ACT.Square,
                                   accum_out=ss[:, t * GH + h:t * GH + h + 1]).then_inc(summed, 1)
                    act.drain()
            inverse_rms(act, None, ss[:, :], root[:, :], None, GDV, squares, roots)
            for t in range(TT):
                act.wait_ge(r_arrived[t], 16)
                act.activation(r[:, t, :], r[:, t, :], ACT.Silu).then_inc(gated, 1)
            high_parts(act, yT[1], yT[0], ps_free, high_made)

        @block.vector
        def _(dve):
            dve.wait_ge(summed, TT * GH)
            dve.tensor_scalar(ss[:, :], ss[:, :], 1.0 / GDV, EPS, ALU.mult, ALU.add).then_inc(squares, 1)
            inverse_rms(None, dve, None, root[:, :], inv[:, :], GDV, squares, roots)
            dve.wait_ge(gain_arrived, 16)
            for t in range(TT):
                for h in range(GH):
                    oh = o[:, t, h * GDV:(h + 1) * GDV]
                    dve.scalar_tensor_tensor(oh, oh, inv[:, t * GH + h:t * GH + h + 1], gain[:, :], ALU.mult, ALU.mult)
            dve.drain()
            for t in range(TT):
                dve.wait_ge(gated, t + 1)
                dve.tensor_tensor(o[:, t, :], o[:, t, :], r[:, t, :], ALU.mult).then_inc(normed, 1)
            transposes_out(dve, yT[1], lambda k: None, None, ps, ps_ready, ps_free, yT[0], high_made)

        @block.tensor
        def _(pe):
            transposes(pe, m, o, lambda e: e.wait_ge(normed, TT), ps, ps_ready, ps_free)


def project_back(nc, m, acts, resid, resid_src, first, gate=None):
    with ExitStack() as ctx:
        sem = lambda n: nc.alloc_semaphore(fresh(n))
        ps = ctx.enter_context(nc.psum_tensor(fresh("ps_back"), [P, 8, HALF], F32))
        got = ctx.enter_context(nc.sbuf_tensor(fresh("product"), [P, 4, HALF], F32))
        arrived = [sem(f"resid{t}") for t in range(TT)]
        ps_ready, ps_free, got_sb, added = sem("back_ready"), sem("back_free"), sem("product_in_sbuf"), sem("back_added")
        block = ctx.enter_context(nc.Block())

        @block.sync
        def _(sp):
            for t in range(TT):
                sp.dma_start(resid[:, t, :], resid_src[t * P:(t + 1) * P, :]).then_inc(arrived[t], 16)
            m.ring.issue(sp, 2 * first + 6)

        @block.tensor
        def _(pe):
            with pe.Fori(0, 2) as i:
                gemm(pe, m, acts, lambda h: pe.wait_ge(m.ring.split, i * 2 + (2 * first + h + 1)), i * 8,
                     ps, ps_ready, ps_free, True)

        @block.scalar
        def _(act):
            act.sem_inc(ps_free, 8)

            def evacuate(n, last):
                act.wait_ge(ps_ready, n + 1)
                if last:
                    m.ring.release(act)
                if n >= 4:
                    act.wait_ge(added, n - 3)
                act.copy(got[:, n % 4, :], ps[:, n % 8, :])
                act.drain()
                act.sem_inc(got_sb, 1)
                act.sem_inc(ps_free, 1)

            evacuate_split(act, m, (first, first + 2), evacuate)

        @block.vector
        def _(dve):
            for i in range(2):
                m.ring.make_low(dve, 2 * first + i)
            for n in range(2 * TT):
                t, cols, x = n % TT, slice((n // TT) * HALF, (n // TT + 1) * HALF), got[:, n % 4, :]
                if n < TT:
                    dve.wait_ge(arrived[t], 16)
                dve.wait_ge(got_sb, n + 1)
                if gate is not None:
                    dve.tensor_tensor(x, x, gate[:, cols], ALU.mult)
                    dve.drain()
                dve.tensor_tensor(resid[:, t, cols], x, resid[:, t, cols], ALU.add).then_inc(added, 1)
                if n == 4:
                    m.ring.make_low(dve, 2 * first + 2)
                if n == 7:
                    m.ring.make_low(dve, 2 * first + 3)



UNROLL = 4


def load_expert(sp, m, a, e, u):
    for i, w in enumerate(("moe_w1", "moe_w3")):
        sp.dma_start(m.w13[u][:, i], a[w][0, e].rearrange("(k p) n -> p k n", p=P)).then_inc(m.w13_loaded[u], 16)
    sp.dma_start(m.w2[u], a["moe_w2"][0, e].rearrange("(k p) n -> p k n", p=P)).then_inc(m.w2_loaded[u], 16)


def router(nc, m, a):
    hT = m.b1
    NL = GROUPS + EXPERTS
    with ExitStack() as ctx:
        sem = lambda n: nc.alloc_semaphore(fresh(n))
        sb = lambda n, s, d=F32: ctx.enter_context(nc.sbuf_tensor(n, s, d))
        w = sb("w_router", [P, KT, NL])
        lg = sb("logits", [P, TT, NL])
        gmx, emx = sb("group_max", [P, TT, 8]), sb("expert_max", [P, TT, 8])
        gix, eix = sb("group_index", [P, TT, 8], U32), sb("expert_index", [P, TT, 8], U32)
        gid, eid = sb("group_id", [P, TT]), sb("expert_id", [P, 2, TT])
        in_group = sb("in_group", [P, TT, GROUPS])
        prod = sb("selected", [P, TT, GROUPS, PER_GROUP])
        el = sb("group_logits", [P, TT, PER_GROUP])
        gexp, gsum, ez, den = sb("group_exp", [P, TT, GROUPS]), sb("group_sum", [P, TT]), sb("second_exp", [P, TT]), sb("pair_sum", [P, TT])
        one = [sb(f"one_hot{k}", [P, TT, EXPERTS]) for k in range(2)]
        both = sb("assigned", [P, TT, EXPERTS])
        rank, dest = sb("rank", [P, 2, TT]), sb("slot_row", [P, 2 * TT], I32)
        cnt, extra, cum = sb("counts", [P, EXPERTS]), sb("extra_blocks", [P, EXPERTS]), sb("extra_cum", [P, EXPERTS])
        le, per_part, info_i = sb("passed", [P, EXPERTS]), sb("block_info", [P, 4]), sb("block_info_i", [P, 2], I32)
        ps = ctx.enter_context(nc.psum_tensor("ps_logits", [P, 2, HALF], F32))
        psp = ctx.enter_context(nc.psum_tensor("ps_rank", [P, TT, EXPERTS], F32))
        psc = ctx.enter_context(nc.psum_tensor("ps_counts", [P, EXPERTS], F32))
        w_arrived, logits_ready, shifted, exped = sem("router_w"), sem("logits_ready"), sem("shifted"), sem("exped")
        assigned, ranked, placed, scattered, tables = sem("assigned_s"), sem("ranked"), sem("placed"), sem("codes_scattered"), sem("tables")
        listed, info_stored, diffed = sem("listed"), sem("info_stored"), sem("diffed")
        block = ctx.enter_context(nc.Block())

        @block.sync
        def _(sp):
            sp.dma_start(w[:, :, 0:GROUPS], a["moe_w_group"][0].rearrange("(k p) n -> p k n", p=P)).then_inc(w_arrived, 16)
            sp.dma_start(w[:, :, GROUPS:NL], a["moe_w_expert"][0].rearrange("(k p) n -> p k n", p=P)).then_inc(w_arrived, 16)
            for e in range(2):
                load_expert(sp, m, a, e, e)
            sp.wait_ge(scattered, 16 * 2 * TT)
            sp.dma_start(m.scatter_idx[:, :], m.codes[0:SLOTS * EXPERTS, :].rearrange("(s e) o -> s (e o)", s=SLOTS))\
                .then_inc(tables, 16)
            sp.wait_ge(listed, 1)
            sp.dma_start(m.info_dram, info_i[:, :]).then_inc(info_stored, 16)
            sp.wait_ge(info_stored, 16)
            sp.dma_start(m.info_row[:, :], m.info_dram.rearrange("(o p) c -> o (p c)", o=1)).then_inc(info_stored, 16)
            sp.wait_ge(info_stored, 32)

        @block.tensor
        def _(pe):
            pe.wait_ge(w_arrived, 32)
            for t in range(TT):
                for k in range(KT):
                    last = pe.matmul(ps[:, t // 4, (t % 4) * NL:(t % 4 + 1) * NL], hT[:, k, t * P:(t + 1) * P], w[:, k, :],
                                     start=(k == 0), stop=(k == KT - 1))
            last.then_inc(logits_ready, 1)
            pe.wait_ge(assigned, 1)
            for t in range(TT):
                for s in range(t):
                    pe.matmul(psp[:, t, :], m.ones[:, :], both[:, s, :], start=(s == 0), stop=False)
                pe.matmul(psp[:, t, :], m.before[:, :], both[:, t, :], start=(t == 0), stop=True)
            for t in range(TT):
                last = pe.matmul(psc[:, :], m.ones[:, :], both[:, t, :], start=(t == 0), stop=(t == TT - 1))
            last.then_inc(ranked, 1)

        @block.scalar
        def _(act):
            act.wait_ge(shifted, 1)
            act.activation(gexp[:, :, :], gexp[:, :, :], ACT.Exp).then_inc(exped, 1)
            act.wait_ge(diffed, 1)
            act.activation(ez[:, :], ez[:, :], ACT.Exp).then_inc(exped, 1)

        @block.vector
        def _(dve):
            dve.wait_ge(logits_ready, 1)
            for h in range(2):
                dve.tensor_copy(lg[:, 4 * h:4 * h + 4, :], ps[:, h, 0:4 * NL].rearrange("p (t n) -> p t n", t=4))
            dve.drain()
            for t in range(TT):
                dve.max(gmx[:, t, :], lg[:, t, 0:GROUPS])
            dve.drain()
            for t in range(TT):
                dve.max_index(gix[:, t, :], gmx[:, t, :], lg[:, t, 0:GROUPS])
            dve.tensor_tensor(gexp[:, :, :], lg[:, :, 0:GROUPS], gmx[:, :, 0:1].to_broadcast([P, TT, GROUPS]),
                              ALU.subtract).then_inc(shifted, 1)
            dve.drain()
            dve.tensor_copy(gid[:, :], gix[:, :, 0])
            dve.drain()
            dve.tensor_tensor(in_group[:, :, :], m.expert_iota[:, None, 0:GROUPS].to_broadcast([P, TT, GROUPS]),
                              gid[:, :, None].to_broadcast([P, TT, GROUPS]), ALU.is_equal)
            dve.drain()
            dve.tensor_tensor(prod[:, :, :, :], lg[:, :, GROUPS:NL].rearrange("p t (g e) -> p t g e", g=GROUPS),
                              in_group[:, :, :, None].to_broadcast([P, TT, GROUPS, PER_GROUP]), ALU.mult)
            dve.drain()
            dve.reduce_sum(el[:, :, :], prod[:, :, :, :].rearrange("p t g e -> p t e g"), axis=AX.X)
            dve.drain()
            for t in range(TT):
                dve.max(emx[:, t, :], el[:, t, :])
            dve.drain()
            for t in range(TT):
                dve.max_index(eix[:, t, :], emx[:, t, :], el[:, t, :])
            dve.tensor_tensor(ez[:, :], emx[:, :, 1], emx[:, :, 0], ALU.subtract).then_inc(diffed, 1)
            dve.drain()
            for k in range(2):
                dve.tensor_copy(eid[:, k, :], eix[:, :, k])
            dve.drain()
            for k in range(2):
                dve.scalar_tensor_tensor(eid[:, k, :], gid[:, :], float(PER_GROUP), eid[:, k, :], ALU.mult, ALU.add)
            dve.drain()
            for k in range(2):
                dve.tensor_tensor(one[k][:, :, :], m.expert_iota[:, None, :].to_broadcast([P, TT, EXPERTS]),
                                  eid[:, k, :, None].to_broadcast([P, TT, EXPERTS]), ALU.is_equal)
            dve.drain()
            dve.tensor_tensor(both[:, :, :], one[0][:, :, :], one[1][:, :, :], ALU.add).then_inc(assigned, 1)
            dve.wait_ge(exped, 2)
            dve.reduce_sum(gsum[:, :], gexp[:, :, :], axis=AX.X)
            dve.tensor_scalar(den[:, :], ez[:, :], 1.0, None, ALU.add)
            dve.drain()
            dve.tensor_tensor(den[:, :], den[:, :], gsum[:, :], ALU.mult)
            dve.drain()
            dve.reciprocal(m.gates2[:, 0, :], den[:, :])
            dve.drain()
            dve.tensor_tensor(m.gates2[:, 1, :], m.gates2[:, 0, :], ez[:, :], ALU.mult)
            dve.wait_ge(ranked, 1)
            for k in range(2):
                dve.tensor_tensor(one[k][:, :, :], psp[:, :, :], one[k][:, :, :], ALU.mult)
            dve.drain()
            for k in range(2):
                dve.reduce_sum(rank[:, k, :], one[k][:, :, :], axis=AX.X)
            dve.drain()
            dve.scalar_tensor_tensor(dest[:, :].rearrange("p (k t) -> p k t", k=2), rank[:, :, :], float(EXPERTS),
                                     eid[:, :, :], ALU.mult, ALU.add).then_inc(placed, 1)
            dve.tensor_copy(cnt[:, :], psc[:, :])
            dve.memset(extra[:, :], 0.0)
            dve.drain()
            for j in range(1, T // SLOTS):
                dve.scalar_tensor_tensor(extra[:, :], cnt[:, :], float(SLOTS * j), extra[:, :], ALU.is_gt, ALU.add)
                dve.drain()
            dve.tensor_tensor_scan(cum[:, :], m.ones[:, 0:EXPERTS], extra[:, :], 0.0, ALU.mult, ALU.add)
            dve.drain()
            dve.tensor_scalar(le[:, :], cum[:, :], m.part_iota[:, 0:1], None, ALU.is_le)
            dve.tensor_copy(m.n_extra[:, :], cum[0:1, EXPERTS - 1:EXPERTS])
            dve.drain()
            dve.reduce_sum(per_part[:, 0:1], le[:, :], axis=AX.X)
            dve.tensor_tensor(extra[:, :], extra[:, :], le[:, :], ALU.mult)
            dve.drain()
            dve.reduce_sum(per_part[:, 1:2], extra[:, :], axis=AX.X)
            dve.drain()
            dve.tensor_tensor(per_part[:, 2:3], m.part_iota[:, 0:1], per_part[:, 1:2], ALU.subtract)
            dve.drain()
            dve.tensor_scalar(per_part[:, 3:4], per_part[:, 2:3], 1.0, float(SLOTS * EXPERTS), ALU.add, ALU.mult)
            dve.drain()
            dve.tensor_tensor(info_i[:, 1:2], per_part[:, 3:4], per_part[:, 0:1], ALU.add)
            dve.tensor_copy(info_i[:, 0:1], per_part[:, 0:1]).then_inc(listed, 1)
            dve.wait_ge(tables, 16)
            code_tokens(dve, m.gather_idx[:, :], m.scatter_idx[:, :])

        @block.gpsimd
        def _(pool):
            pool.wait_ge(placed, 1)
            for n in range(2 * TT):
                pool.indirect_dma_start(m.codes, bass.IndirectOffsetOnAxis(dest[:, n:n + 1], 0), m.codes_i[:, n:n + 1],
                                        None).then_inc(scattered, 16)


def code_tokens(dve, tokens, codes):
    dve.tensor_scalar(tokens, codes, float(T), -float(T), ALU.is_ge, ALU.mult)
    dve.drain()
    dve.tensor_tensor(tokens, tokens, codes, ALU.add)
    dve.drain()


class ExpertBuffers:

    def __init__(self, nc, ctx):
        sb = lambda n, s, d=F32: ctx.enter_context(nc.sbuf_tensor(fresh(n), s, d))
        self.xg = [sb("gathered", [SLOTS, D]) for _ in range(2)]
        self.y = [sb("expert_out", [SLOTS, D]) for _ in range(2)]
        self.xT = [sb("gatheredT", [P, KT, SLOTS]) for _ in range(2)]
        self.sil = [sb("silu", [P, 2, SLOTS]) for _ in range(2)]
        self.hid = [sb("hidden", [P, 2, SLOTS]) for _ in range(2)]
        self.gi = [sb("gather_now", [SLOTS, 1], I32) for _ in range(2)]
        self.si = [sb("scatter_now", [SLOTS, 1], I32) for _ in range(2)]
        pb = lambda n, s: ctx.enter_context(nc.psum_tensor(fresh(n), s, F32))
        self.psT, self.psH, self.psY = pb("ps_xT", [P, 2, HALF]), pb("ps_hid", [P, 2, HALF]), pb("ps_y", [P, 2, 2, HALF])


def expert_turn(pe, m, B, s):
    for k in range(KT):
        last = pe.transpose(B.psT[:, s, k * SLOTS:(k + 1) * SLOTS], B.xg[s][:, k * P:(k + 1) * P],
                            m.ident[0:SLOTS, 0:SLOTS])
    return last


def expert_up(pe, m, B, s, u):
    for f in range(4):
        for k in range(KT):
            last = pe.matmul(B.psH[:, s, f * SLOTS:(f + 1) * SLOTS], m.w13[u][:, f // 2, k, (f % 2) * P:(f % 2 + 1) * P],
                             B.xT[s][:, k, :], start=(k == 0), stop=(k == KT - 1))
    return last


def expert_down(pe, m, B, s, u):
    for h in range(2):
        for f in range(2):
            last = pe.matmul(B.psY[0:SLOTS, s, h, :], B.hid[s][:, f, :], m.w2[u][:, f, h * HALF:(h + 1) * HALF],
                             start=(f == 0), stop=(f == 1))
    return last


def expert_xT(dve, m, B, s):
    row = VEC["ffn_norm"][0]
    return dve.tensor_tensor(B.xT[s][:, :, :], B.psT[:, s, :].rearrange("p (k n) -> p k n", k=KT),
                             m.cols[:, row:row + KT, None].to_broadcast([P, KT, SLOTS]), ALU.mult)


def expert_silu(act, B, s):
    return act.activation(B.sil[s][:, :, :], B.psH[:, s, 0:2 * SLOTS].rearrange("p (f n) -> p f n", f=2), ACT.Silu)


def expert_hidden(dve, B, s):
    return dve.tensor_tensor(B.hid[s][:, :, :], B.psH[:, s, 2 * SLOTS:4 * SLOTS].rearrange("p (f n) -> p f n", f=2),
                             B.sil[s][:, :, :], ALU.mult)


def gather_tokens(pool, m, B, s):
    return pool.indirect_dma_start(B.xg[s][:, :], None, m.xn_dram, bass.IndirectOffsetOnAxis(B.gi[s][:, 0:1], 0),
                                   bounds_check=T - 1, oob_is_err=False)


def scatter_tokens(pool, m, B, s):
    return pool.indirect_dma_start(m.contrib, bass.IndirectOffsetOnAxis(B.si[s][:, 0:1], 0), B.y[s][:, :], None,
                                   bounds_check=2 * T - 1, oob_is_err=False)


def experts(nc, m, a):
    with ExitStack() as ctx:
        sem = lambda n: nc.alloc_semaphore(fresh(n))
        B = ExpertBuffers(nc, ctx)
        gathered = [sem(f"gathered{s}") for s in range(2)]
        scattered = [sem(f"scattered{s}") for s in range(2)]
        gi_ready, turned, xT_sb, up_done, silu_done, hid_done, down_done = (
            sem(n) for n in ("gather_index", "turned", "xT_in_sbuf", "up_done", "silu_done", "hid_done", "down_done"))
        y_sb = [sem(f"y_half{h}_in_sbuf") for h in range(2)]
        block = ctx.enter_context(nc.Block())
        ITERS = EXPERTS // UNROLL

        @block.sync
        def _(sp):
            for e in range(2, UNROLL):
                load_expert(sp, m, a, e, e)
            with sp.Fori(0, ITERS - 1) as i:
                for u in range(UNROLL):
                    e = i * UNROLL + (UNROLL + u)
                    sp.wait_ge(up_done, i * UNROLL + (u + 1))
                    for j, w in enumerate(("moe_w1", "moe_w3")):
                        sp.dma_start(m.w13[u][:, j], a[w][0, e].rearrange("(k p) n -> p k n", p=P)).then_inc(m.w13_loaded[u], 16)
                    sp.wait_ge(down_done, i * UNROLL + (u + 1))
                    sp.dma_start(m.w2[u], a["moe_w2"][0, e].rearrange("(k p) n -> p k n", p=P)).then_inc(m.w2_loaded[u], 16)

        def over_experts(engine, step):
            for u in range(UNROLL):
                step(u, 0, u, False)
            with engine.Fori(1, ITERS - 1) as i:
                for u in range(UNROLL):
                    step(i * UNROLL + u, i, u, False)
            for u in range(UNROLL):
                step((ITERS - 1) * UNROLL + u, ITERS - 1, u, True)

        def out_is_stored(engine, i, u):
            before = i * 2 + u // 2
            if not isinstance(before, int) or before > 0:
                engine.wait_ge(scattered[u % 2], before * 16)

        @block.gpsimd
        def _(pool):
            for s in range(2):
                pool.memset(B.xg[s][:, :], 0.0)
            pool.drain()
            for e in range(2):
                pool.wait_ge(gi_ready, e + 1)
                gather_tokens(pool, m, B, e).then_inc(gathered[e], 16)

            def step(e, i, u, tail):
                s = u % 2
                if not (tail and u >= UNROLL - 2):
                    pool.wait_ge(gi_ready, e + 3)
                    carry(pool, m)
                    gather_tokens(pool, m, B, s).then_inc(gathered[s], 16)
                pool.wait_ge(y_sb[0], e + 3)
                pool.wait_ge(y_sb[1], e + 3)
                carry(pool, m)
                scatter_tokens(pool, m, B, s).then_inc(scattered[s], 16)

            over_experts(pool, step)
            for s in range(2):
                pool.wait_ge(scattered[s], 16 * (EXPERTS // 2))

        @block.tensor
        def _(pe):
            pe.wait_ge(gathered[0], 16)
            expert_turn(pe, m, B, 0).then_inc(turned, 1)

            def step(e, i, u, tail):
                s = u % 2
                pe.wait_ge(xT_sb, e + 1)
                pe.wait_ge(m.w13_loaded[u], (i + 1) * 32)
                expert_up(pe, m, B, s, u).then_inc(up_done, 1)
                if not (tail and u == UNROLL - 1):
                    pe.wait_ge(gathered[1 - s], (i * 2 + ((u + 1) // 2 + 1)) * 16)
                    carry(pe, m)
                    expert_turn(pe, m, B, 1 - s).then_inc(turned, 1)
                pe.wait_ge(hid_done, e + 1)
                pe.wait_ge(m.w2_loaded[u], (i + 1) * 16)
                for h in range(2):
                    pe.wait_ge(y_sb[h], e + 1)
                expert_down(pe, m, B, s, u).then_inc(down_done, 1)

            over_experts(pe, step)

        @block.scalar
        def _(act):
            act.sem_inc(y_sb[1], 2)
            def step(e, i, u, tail):
                s = u % 2
                act.wait_ge(up_done, e + 1)
                expert_silu(act, B, s).then_inc(silu_done, 1)
                out_is_stored(act, i, u)
                act.wait_ge(down_done, e + 1)
                act.copy(B.y[s][:, HALF:D], B.psY[0:SLOTS, s, 1, :]).then_inc(y_sb[1], 1)

            over_experts(act, step)

        @block.vector
        def _(dve):
            dve.sem_inc(y_sb[0], 2)
            for e in range(2):
                dve.tensor_copy(B.gi[e][:, :], m.gather_idx[:, e:e + 1]).then_inc(gi_ready, 1)
            dve.wait_ge(turned, 1)
            expert_xT(dve, m, B, 0).then_inc(xT_sb, 1)
            dve.tensor_copy(B.gi[0][:, :], m.gather_idx[:, 2:3]).then_inc(gi_ready, 1)

            def step(e, i, u, tail):
                s = u % 2
                dve.wait_ge(silu_done, e + 1)
                expert_hidden(dve, B, s).then_inc(hid_done, 1)
                if not (tail and u == UNROLL - 1):
                    dve.wait_ge(turned, e + 2)
                    expert_xT(dve, m, B, 1 - s).then_inc(xT_sb, 1)
                if not (tail and u >= UNROLL - 3):
                    dve.tensor_copy(B.gi[1 - s][:, :], m.gather_idx[:, col(e + 3)]).then_inc(gi_ready, 1)
                out_is_stored(dve, i, u)
                carry(dve, m)
                dve.tensor_copy(B.si[s][:, :], m.scatter_idx[:, col(e)])
                dve.wait_ge(down_done, e + 1)
                dve.tensor_copy(B.y[s][:, 0:HALF], B.psY[0:SLOTS, s, 0, :])
                dve.drain()
                dve.sem_inc(y_sb[0], 1)

            over_experts(dve, step)


def more_blocks(nc, m, a):
    MOST = 2 * T // SLOTS
    with ExitStack() as ctx:
        sem = lambda n: nc.alloc_semaphore(fresh(n))
        B = ExpertBuffers(nc, ctx)
        weights, indices, tokens, gathered, turned, xT_sb, up_done, silu_done, hid_done, down_done, y_sb, scattered, free = (
            sem("more_" + n) for n in ("weights", "indices", "tokens", "gathered", "turned", "xT", "up", "silu",
                                       "hid", "down", "y", "scattered", "free"))
        block = ctx.enter_context(nc.Block())

        def over_blocks(engine, step):
            n = engine.value_load(m.n_extra[0:1, 0:1], min_val=0, max_val=MOST)
            with engine.If(n > 0):
                with engine.Fori(0, n) as b:
                    step(b)

        @block.sync
        def _(sp):
            def step(b):
                e = sp.value_load(m.info_row[0:1, bass.ds(b * 2, 1)], min_val=0, max_val=EXPERTS - 1)
                row = sp.value_load(m.info_row[0:1, bass.ds(b * 2 + 1, 1)], min_val=0, max_val=(T - SLOTS) * EXPERTS + EXPERTS - 1)
                sp.wait_ge(free, b + 1)
                for j, w in enumerate(("moe_w1", "moe_w3")):
                    sp.dma_start(m.w13[0][:, j], a[w][0, e].rearrange("(k p) n -> p k n", p=P)).then_inc(weights, 16)
                sp.dma_start(m.w2[0], a["moe_w2"][0, e].rearrange("(k p) n -> p k n", p=P)).then_inc(weights, 16)
                sp.dma_start(B.si[0][:, :], m.codes[bass.ds(row, SLOTS, EXPERTS), :])\
                    .then_inc(indices, 16)
            over_blocks(sp, step)

        @block.gpsimd
        def _(pool):
            pool.memset(B.xg[0][:, :], 0.0)
            pool.drain()
            pool.sem_inc(free, 1)
            def step(b):
                pool.wait_ge(tokens, b + 1)
                carry(pool, m)
                gather_tokens(pool, m, B, 0).then_inc(gathered, 16)
                pool.wait_ge(y_sb, b + 1)
                carry(pool, m)
                scatter_tokens(pool, m, B, 0).then_inc(scattered, 16)
                pool.wait_ge(scattered, (b + 1) * 16)
                pool.sem_inc(free, 1)
            over_blocks(pool, step)

        @block.tensor
        def _(pe):
            def step(b):
                pe.wait_ge(gathered, (b + 1) * 16)
                carry(pe, m)
                expert_turn(pe, m, B, 0).then_inc(turned, 1)
                pe.wait_ge(xT_sb, b + 1)
                pe.wait_ge(weights, (b + 1) * 48)
                expert_up(pe, m, B, 0, 0).then_inc(up_done, 1)
                pe.wait_ge(hid_done, b + 1)
                expert_down(pe, m, B, 0, 0).then_inc(down_done, 1)
            over_blocks(pe, step)

        @block.scalar
        def _(act):
            def step(b):
                act.wait_ge(up_done, b + 1)
                expert_silu(act, B, 0).then_inc(silu_done, 1)
            over_blocks(act, step)

        @block.vector
        def _(dve):
            def step(b):
                dve.wait_ge(indices, (b + 1) * 16)
                code_tokens(dve, B.gi[0][:, :], B.si[0][:, :])
                dve.sem_inc(tokens, 1)
                dve.wait_ge(turned, b + 1)
                expert_xT(dve, m, B, 0).then_inc(xT_sb, 1)
                dve.wait_ge(silu_done, b + 1)
                expert_hidden(dve, B, 0).then_inc(hid_done, 1)
                dve.wait_ge(down_done, b + 1)
                dve.tensor_copy(B.y[0][:, :].rearrange("p (h n) -> p h n", h=2), B.psY[0:SLOTS, 0, :, :]).then_inc(y_sb, 1)
            over_blocks(dve, step)


def combine(nc, m, a):
    x = m.b4
    parts = (m.b1, m.b2)
    with ExitStack() as ctx:
        sem = lambda n: nc.alloc_semaphore(fresh(n))
        sb = lambda n, s, d=F32: ctx.enter_context(nc.sbuf_tensor(n, s, d))
        gain = sb("final_norm_wide", [P, D])
        ss, root, inv, junk = sb("x2_ss", [P, TT]), sb("x2_root", [P, TT]), sb("x2_inv", [P, TT]), sb("x2_squares", [P, D])
        arrived = [sem(f"contrib_arrived{t}") for t in range(TT)]
        gain_arrived, added, summed, squares, roots, normed, stored = (
            sem(n) for n in ("final_gain", "contrib_added", "x2_summed", "x2_meaned", "x2_rooted", "x2_normed", "x2_stored"))
        block = ctx.enter_context(nc.Block())

        @block.sync
        def _(sp):
            sp.dma_start(gain[:, :], spread(a["final_norm"].rearrange("(o d) -> o d", o=1))).then_inc(gain_arrived, 16)
            for t in range(TT):
                for k in range(2):
                    sp.dma_start(parts[k][:, t, :], m.contrib[k * T + t * P:k * T + (t + 1) * P, :]).then_inc(arrived[t], 16)
            for t in range(TT):
                sp.wait_ge(normed, t + 1)
                sp.dma_start(m.x2_dram[t * P:(t + 1) * P, :], x[:, t, :]).then_inc(stored, 16)
            sp.wait_ge(stored, 16 * TT)

        @block.vector
        def _(dve):
            for t in range(TT):
                dve.wait_ge(arrived[t], 32)
                for k in range(2):
                    ins = dve.scalar_tensor_tensor(x[:, t, :], parts[k][:, t, :], m.gates2[:, k, t:t + 1], x[:, t, :],
                                                   ALU.mult, ALU.add)
                    if k == 0:
                        dve.drain()
                ins.then_inc(added, 1)
            dve.wait_ge(summed, TT)
            dve.tensor_scalar(ss[:, :], ss[:, :], 1.0 / D, EPS, ALU.mult, ALU.add).then_inc(squares, 1)
            inverse_rms(None, dve, None, root[:, :], inv[:, :], D, squares, roots)
            dve.wait_ge(gain_arrived, 16)
            for t in range(TT):
                dve.scalar_tensor_tensor(x[:, t, :], x[:, t, :], inv[:, t:t + 1], gain[:, :], ALU.mult, ALU.mult)\
                    .then_inc(normed, 1)

        @block.scalar
        def _(act):
            for t in range(TT):
                act.wait_ge(added, t + 1)
                act.activation(junk[:, :], x[:, t, :], ACT.Square, accum_out=ss[:, t:t + 1]).then_inc(summed, 1)
                act.drain()
            inverse_rms(act, None, ss[:, :], root[:, :], None, D, squares, roots)



def mixer_projections(nc, m, a):
    acts = (by_tile(m.b1), by_tile(m.b4))
    raw, qk = m.raw, m.b3
    FIRST = 8
    with ExitStack() as ctx:
        sem = lambda n: nc.alloc_semaphore(fresh(n))
        sb = lambda n, s, d=F32: ctx.enter_context(nc.sbuf_tensor(n, s, d))
        w_dt = [both_kinds(nc, ctx, f"w_dt{i}", [P, KT, SH]) for i in range(2)]
        dt_bias, a_log = sb("dt_bias_wide", [P, SH]), sb("a_log_wide", [P, SH])
        mag = sb("dt_magnitude", [P, TT, SH])
        conv = [sb(f"conv_sum{s}", [P, T]) for s in range(2)]
        stage = sb("zv_stage", [P, 4, HALF])
        ps = ctx.enter_context(nc.psum_tensor("ps_mix_in", [P, 8, HALF], F32))
        psd = ps[:, 7, 0:TT * SH].rearrange("p (t n) -> p t n", t=TT)
        small, dt_ready, dt_read, ps_ready, ps_free = sem("dt_weights"), sem("dt_ready"), sem("dt_read"), sem("mix_ready"), sem("mix_free")
        dt_high, dt_split, staged = sem("dt_high"), sem("dt_split"), sem("zv_staged")
        stored = [sem(f"zv_stored{s}") for s in range(4)]
        dt_mag, dt_log, a_exp, raw_sb, convolved, silued = (
            sem(n) for n in ("dt_mag", "dt_log", "a_exp", "raw_in_sbuf", "convolved", "conv_silu"))
        block = ctx.enter_context(nc.Block())

        @block.sync
        def _(sp):
            at = IN_AT["dt"]
            sp.dma_start(w_dt[1][:, :, :], a["w_in_2"][0][:, at:at + SH].rearrange("(k p) n -> p k n", p=P)).then_inc(small, 16)
            sp.dma_start(dt_bias[:, :], spread(a["dt_bias_2"])).then_inc(small, 16)
            sp.dma_start(a_log[:, :], spread(a["a_log_2"])).then_inc(small, 16)
            sp.dma_start(m.d_skip[:, :], spread(a["d_skip_2"])).then_inc(small, 16)
            for i, dst in enumerate((m.z_dram, m.v_dram)):
                b = FIRST + 4 + i
                m.ring.issue(sp, 2 * b + 3)
                for t in range(TT):
                    n = i * TT + t
                    sp.wait_ge(staged, n + 1)
                    sp.dma_start(dst[t * P:(t + 1) * P, :], stage[:, n % 4, :]).then_inc(stored[n % 4], 16)
                m.ring.issue(sp, 2 * b + 4)
            for s in range(4):
                sp.wait_ge(stored[s], 16 * 4)

        @block.tensor
        def _(pe):
            pe.wait_ge(dt_split, 1)
            for t in range(TT):
                for k in range(KT):
                    for i, j in ((0, 0), (0, 1), (1, 0)):
                        last = pe.matmul(psd[:, t, :], R(acts[i](k)[:, t * P:(t + 1) * P]), R(w_dt[j][:, k, :]),
                                         start=(k == i == j == 0), stop=(k == KT - 1 and i == 1))
            last.then_inc(dt_ready, 1)
            pe.wait_ge(dt_read, 1)
            for first, tokens in ((0, False), (4, True)):
                with pe.Fori(0, 2 if tokens else 4) as i:
                    gemm(pe, m, acts, lambda h: pe.wait_ge(m.ring.split, i * 2 + (2 * (FIRST + first) + h + 1)), i * 8 + 8 * first,
                         ps, ps_ready, ps_free, tokens)

        @block.scalar
        def _(act):
            act.sem_inc(ps_free, 8)
            act.wait_ge(small, 64)
            act.activation(R(w_dt[0][:, :, :]), w_dt[1][:, :, :], ACT.Copy).then_inc(dt_high, 1)
            act.activation(a_log[:, :], a_log[:, :], ACT.Exp).then_inc(a_exp, 1)

            def silu(c):
                act.wait_ge(convolved, c + 1)
                act.activation(raw[:, c, TAPS - 1:], conv[c % 2][:, :], ACT.Silu).then_inc(silued, 1)

            def softplus():
                act.wait_ge(dt_mag, 1)
                act.activation(mag[:, :, :], mag[:, :, :], ACT.Exp, scale=-1.0)
                act.drain()
                act.activation(mag[:, :, :], mag[:, :, :], ACT.Ln, bias=1.0).then_inc(dt_log, 1)

            def evacuate(n, last):
                act.wait_ge(ps_ready, n + 1)
                if last:
                    m.ring.release(act)
                src, cols = ps[:, n % 8, :], slice((n % 2) * HALF, (n % 2 + 1) * HALF)
                if n < 16:
                    act.copy(raw[:, n // 2, TAPS - 1 + (n % 2) * HALF:TAPS - 1 + (n % 2 + 1) * HALF], src).then_inc(ps_free, 1)
                    act.drain()
                    act.sem_inc(raw_sb, 1)
                    if n % 8 in (4, 6):
                        silu(n // 8 * 4 + (n % 8 - 4) // 2)
                elif n < 24:
                    act.mul(qk[:, n // 2 - 8, cols], src, float(AHD) ** -0.5).then_inc(ps_free, 1)
                elif n < 32:
                    act.copy(qk[:, n // 2 - 8, cols], src).then_inc(ps_free, 1)
                else:
                    store_stage(act, stored, n - 32)
                    act.activation(stage[:, n % 4, :], src, ACT.Silu if n < 40 else ACT.Copy)
                    act.drain()
                    act.sem_inc(staged, 1)
                    act.sem_inc(ps_free, 1)
                if n in (8, 16):
                    silu(n // 2 - 2)
                    silu(n // 2 - 1)

            evacuate_split(act, m, (FIRST, FIRST + 6), evacuate, softplus)

        @block.vector
        def _(dve):
            dve.memset(raw[:, :, 0:TAPS - 1], 0.0)
            dve.wait_ge(dt_high, 1)
            dve.tensor_tensor(R(w_dt[1][:, :, :]), w_dt[1][:, :, :], rounded(w_dt[0][:, :, :]), ALU.subtract).then_inc(dt_split, 1)
            for i in range(2):
                m.ring.make_low(dve, 2 * FIRST + i)
            dve.wait_ge(dt_ready, 1)
            dve.tensor_tensor(m.dt[:, :, :], psd, dt_bias[:, None, :].to_broadcast([P, TT, SH]), ALU.add).then_inc(dt_read, 1)
            dve.drain()
            dve.tensor_scalar(mag[:, :, :], m.dt[:, :, :], -1.0, None, ALU.mult)
            dve.drain()
            dve.tensor_tensor(mag[:, :, :], mag[:, :, :], m.dt[:, :, :], ALU.max).then_inc(dt_mag, 1)
            dve.wait_ge(dt_log, 1)
            dve.tensor_scalar(m.dt[:, :, :], m.dt[:, :, :], 0.0, None, ALU.max)
            dve.drain()
            dve.tensor_tensor(m.dt[:, :, :], m.dt[:, :, :], mag[:, :, :], ALU.add)
            dve.drain()
            dve.scalar_tensor_tensor(m.adt[:, :, :], m.dt[:, :, :], -1.0, a_log[:, None, :].to_broadcast([P, TT, SH]),
                                     ALU.mult, ALU.mult)
            row, bias = VEC["ssd_conv_w_2"][0], VEC["ssd_conv_b_2"][0]
            for c in range(KT):
                out = conv[c % 2][:, :]
                dve.wait_ge(raw_sb, 2 * c + 2)
                if c >= 2:
                    dve.wait_ge(silued, c - 1)
                w = lambda j: m.cols[:, row + j * KT + c:row + j * KT + c + 1]
                dve.tensor_scalar(out, raw[:, c, 0:T], w(0), m.cols[:, bias + c:bias + c + 1], ALU.mult, ALU.add)
                for j in range(1, TAPS):
                    dve.drain()
                    ins = dve.scalar_tensor_tensor(out, raw[:, c, j:j + T], w(j), out, ALU.mult, ALU.add)
                ins.then_inc(convolved, 1)
                if c % 4 == 0:
                    m.ring.make_low(dve, 2 * FIRST + c // 2 + 2)
                if c % 4 == 3:
                    m.ring.make_low(dve, 2 * FIRST + c // 2 + 2)
            for i in range(6, 12):
                m.ring.make_low(dve, 2 * FIRST + i)


def state_space(nc, m, a):
    W = SH * SHD
    with ExitStack() as ctx:
        sem = lambda n: nc.alloc_semaphore(fresh(n))
        sb = lambda n, s, d=F32: ctx.enter_context(nc.sbuf_tensor(n, s, d))
        cur = m.b1[:, 4, :].rearrange("p (c n) -> p c n", c=KT)
        later = m.b1[:, 5, :].rearrange("p (h n) -> p h n", h=SH)
        dec = m.b1[:, 6, :].rearrange("p (h n) -> p h n", h=SH)
        M = m.b1[:, 7, :].rearrange("p (h n) -> p h n", h=SH)
        adt, dt, es = sb("adt_now", [P, SH]), sb("dt_now", [P, SH]), sb("decays", [P, 4, SH])
        X, XE, XD = sb("x_dt", [P, SH, SHD]), sb("x_to_end", [P, SH, SHD]), sb("x_skip", [P, SH, SHD])
        Bt, CB = sb("b_tokens", [P, SG, SN]), sb("cb", [P, SG, P])
        S, S_mid, tmp, y = sb("ssd_state", [P, SH, SHD]), sb("ssd_mid", [P, SH, SHD]), sb("ssd_tmp", [P, SH, SHD]), sb("ssd_y", [P, SH, SHD])
        psT = ctx.enter_context(nc.psum_tensor("ps_tokens", [P, 2, HALF], F32))
        psS = ctx.enter_context(nc.psum_tensor("ps_small", [P, 4, SH], F32))
        psG = ctx.enter_context(nc.psum_tensor("ps_seg", [P, SH, P], F32))
        psY = ctx.enter_context(nc.psum_tensor("ps_diag", [P, SH, SHD], F32))
        psZ = ctx.enter_context(nc.psum_tensor("ps_off", [P, SH, SHD], F32))
        (cur_ready, adt_ready, later_ready, small_ready, small_exp, T_ready, seg_ready, dec_ready, x_ready, M_ready,
         diag_ready, upd_ready, mid_ready, state_ready, off0_ready, off_ready) = (sem("s_" + n) for n in (
             "current", "adt", "later", "small", "small_exp", "tokens", "seg", "decay", "x", "M", "diag", "update", "mid",
             "state", "off0", "off"))
        zv_arrived = sem("zv_arrived")
        block = ctx.enter_context(nc.Block())
        heads = lambda v: v[:, :, None].to_broadcast([P, SH, SHD])
        group = lambda g: slice(g * HPG, (g + 1) * HPG)

        @block.sync
        def _(sp):
            for dst, src in ((m.z, m.z_dram), (m.v, m.v_dram)):
                sp.dma_start(dst, src.rearrange("(t p) n -> p t n", p=P)).then_inc(zv_arrived, 16)
            sp.wait_ge(zv_arrived, 32)

        @block.scalar
        def _(act):
            act.sem_inc(off_ready, 1)
            with act.Fori(0, TT) as p:
                act.wait_ge(off_ready, p + 1)
                carry(act, m)
                act.activation(cur, m.raw[:, :, bass.ds(p * P + (TAPS - 1), P)], ACT.Copy).then_inc(cur_ready, 1)
                act.wait_ge(small_ready, p + 1)
                act.activation(es[:, :, :], psS[:, :, :], ACT.Exp).then_inc(small_exp, 1)
                act.wait_ge(seg_ready, p + 1)
                act.activation(dec, psG[:, :, :], ACT.Exp).then_inc(dec_ready, 1)

        @block.tensor
        def _(pe):
            with pe.Fori(0, TT) as p:
                pe.wait_ge(adt_ready, p + 1)
                for i, mask in enumerate((m.upto[:, :], m.after[:, :], m.chunk_ones[:, 0, :], m.chunk_ones[:, 1, :])):
                    last = pe.matmul(psS[:, i, :], mask, adt[:, :], start=True, stop=True)
                last.then_inc(small_ready, 1)
                pe.wait_ge(later_ready, p + 1)
                for h in range(SH):
                    last = pe.matmul(psG[:, h, :], later[:, h, :], m.upto[:, :], start=True, stop=True)
                last.then_inc(seg_ready, 1)
                pe.wait_ge(cur_ready, p + 1)
                pe.wait_ge(state_ready, p + 1)
                for c in range(4):
                    pe.transpose(psT[:, 0, c * P:(c + 1) * P], cur[:, c, :], m.ident[:, :])
                for g in range(SG):
                    pe.transpose(psT[:, 1, g * P:(g + 1) * P], cur[:, 4 + g, :], m.ident[:, :])
                for g in range(SG):
                    last = pe.matmul(psT[:, 1, (2 + g) * P:(3 + g) * P], cur[:, 4 + g, :], cur[:, 6 + g, :], start=True, stop=True)
                last.then_inc(T_ready, 1)
                for g in range(SG):
                    last = pe.matmul(psZ[0:CH, group(g), :], cur[:, 6 + g, 0:CH], S[:, group(g), :], start=True, stop=True)
                last.then_inc(off0_ready, 1)
                pe.wait_ge(x_ready, p + 1)
                for c in range(2):
                    for g in range(SG):
                        last = pe.matmul(psT[:, c, g * 2 * P:(g + 1) * 2 * P], Bt[c * CH:(c + 1) * CH, g, :],
                                         XE[c * CH:(c + 1) * CH, group(g), :], start=True, stop=True)
                last.then_inc(upd_ready, 1)
                pe.wait_ge(M_ready, p + 1)
                for h in range(SH):
                    last = pe.matmul(psY[:, h, :], M[:, h, :], X[:, h, :], start=True, stop=True)
                last.then_inc(diag_ready, 1)
                pe.wait_ge(mid_ready, p + 1)
                for g in range(SG):
                    last = pe.matmul(psZ[CH:P, group(g), :], cur[:, 6 + g, CH:P], S_mid[:, group(g), :], start=True, stop=True)
                last.then_inc(off_ready, 1)

        @block.vector
        def _(dve):
            dve.memset(S[:, :, :], 0.0).then_inc(state_ready, 1)
            dve.wait_ge(zv_arrived, 32)
            with dve.Fori(0, TT) as p:
                dve.tensor_copy(adt[:, :], m.adt[:, p, :])
                dve.tensor_copy(dt[:, :], m.dt[:, p, :])
                dve.drain()
                dve.sem_inc(adt_ready, 1)
                dve.tensor_tensor(later, m.after[:, None, :].to_broadcast([P, SH, P]),
                                  adt[:, :, None].to_broadcast([P, SH, P]), ALU.mult).then_inc(later_ready, 1)
                dve.wait_ge(T_ready, p + 1)
                xs = psT[:, 0, :].rearrange("p (h n) -> p h n", h=SH)
                dve.tensor_tensor(X[:, :, :], xs, heads(dt), ALU.mult)
                dve.tensor_tensor(XD[:, :, :], xs, heads(m.d_skip), ALU.mult)
                dve.tensor_copy(Bt[:, :, :], psT[:, 1, 0:2 * P].rearrange("p (g n) -> p g n", g=SG))
                dve.tensor_tensor(CB[:, :, :], psT[:, 1, 2 * P:4 * P].rearrange("p (g n) -> p g n", g=SG),
                                  m.upto[:, None, :].to_broadcast([P, SG, P]), ALU.mult)
                dve.drain()
                dve.wait_ge(small_exp, p + 1)
                dve.tensor_tensor(XE[:, :, :], X[:, :, :], heads(es[:, 1]), ALU.mult).then_inc(x_ready, 1)
                dve.wait_ge(dec_ready, p + 1)
                for g in range(SG):
                    ins = dve.tensor_tensor(M[:, group(g), :], dec[:, group(g), :],
                                            CB[:, g, None, :].to_broadcast([P, HPG, P]), ALU.mult)
                ins.then_inc(M_ready, 1)
                dve.tensor_tensor(tmp[:, :, :], S[:, :, :], heads(es[:, 2]), ALU.mult)
                dve.drain()
                dve.wait_ge(upd_ready, p + 1)
                dve.tensor_tensor(S_mid[:, :, :], psT[:, 0, :].rearrange("p (h n) -> p h n", h=SH), tmp[:, :, :],
                                  ALU.add).then_inc(mid_ready, 1)
                dve.drain()
                dve.tensor_tensor(tmp[:, :, :], S_mid[:, :, :], heads(es[:, 3]), ALU.mult)
                dve.drain()
                dve.wait_ge(off0_ready, p + 1)
                dve.tensor_tensor(S[:, :, :], psT[:, 1, :].rearrange("p (h n) -> p h n", h=SH), tmp[:, :, :],
                                  ALU.add).then_inc(state_ready, 1)
                dve.wait_ge(off_ready, p + 2)
                dve.tensor_tensor(y[:, :, :], psZ[:, :, :], heads(es[:, 0]), ALU.mult)
                dve.drain()
                dve.wait_ge(diag_ready, p + 1)
                dve.tensor_tensor(y[:, :, :], psY[:, :, :], y[:, :, :], ALU.add)
                dve.drain()
                dve.tensor_tensor(y[:, :, :], y[:, :, :], XD[:, :, :], ALU.add)
                dve.drain()
                z = m.z[:, p, :]
                dve.tensor_tensor(z, z, y[:, :, :].rearrange("p h n -> p (h n)"), ALU.mult)
                dve.drain()


def band_attention(nc, m, a):
    qk, v = m.b3, m.v
    with ExitStack() as ctx:
        sem = lambda n: nc.alloc_semaphore(fresh(n))
        sb = lambda n, s, d=F32: ctx.enter_context(nc.sbuf_tensor(n, s, d))
        q = m.raw[:, 0, 0:T]
        k = m.raw[:, 1, 0:T]
        bias = [m.raw[:, 2 + u, 0:BAND] for u in range(2)]
        sc = [m.raw[:, 4 + u, 0:BAND] for u in range(2)]
        pT = [m.raw[:, 6 + u, 0:BAND] for u in range(2)]
        nmx, rs, ri = sb("minus_max", [P, 4]), sb("prob_sum", [P, 4]), sb("prob_inv", [P, 4])
        psS = [ctx.enter_context(nc.psum_tensor(f"ps_scores{u}", [P, 2 * HALF], F32)) for u in range(2)]
        psT = [ctx.enter_context(nc.psum_tensor(f"ps_probsT{u}", [P, 2 * HALF], F32)) for u in range(2)]
        psO = [psT[u][:, HALF + P:HALF + P + AHD] for u in range(2)]
        bias_arrived = [sem(f"bias_arrived{u}") for u in range(2)]
        (copied, scores, read_s, maxed, exped, turned, pT_sb, out_ready, out_sb) = (sem("b_" + n) for n in (
            "qk_copied", "scores", "scores_read", "maxed", "exped", "turned", "probsT", "out", "out_in_sbuf"))
        block = ctx.enter_context(nc.Block())
        PAIRS = AH // 2
        WARM = 2
        UNITS = 2 * TT
        units = [(u, j) for j in range(TT) for u in range(2)]
        tiles = lambda n: min(units[n][1], BANDT - 1) + 1

        @block.sync
        def _(sp):
            for u in range(2):
                sp.dma_start(bias[u], shifted(m.bias_lines[u])).then_inc(bias_arrived[u], 16)
            with sp.Fori(1, PAIRS) as hp:
                for u in range(2):
                    sp.wait_ge(read_s, hp * UNITS + 2)
                    sp.dma_start(bias[u], shifted(m.bias_lines[hp * 2 + u])).then_inc(bias_arrived[u], 16)

        @block.scalar
        def _(act):
            act.sem_inc(out_ready, 1)
            with act.Fori(0, PAIRS) as hp:
                act.wait_ge(out_ready, hp * UNITS + 1)
                carry(act, m)
                act.activation(q, qk[:, hp, :], ACT.Copy)
                act.activation(k, qk[:, hp + PAIRS, :], ACT.Copy).then_inc(copied, 1)

                def exponentials(n):
                    w, i = tiles(n) * P, n % 4
                    act.wait_ge(maxed, hp * UNITS + (n + 1))
                    act.activation(sc[n % 2][:, 0:w], sc[n % 2][:, 0:w], ACT.Exp, bias=nmx[:, i:i + 1], accum_out=rs[:, i:i + 1])
                    act.drain()
                    act.sem_inc(exped, 1)

                exponentials(0)
                exponentials(1)
                for n in range(UNITS):
                    w = tiles(n) * P
                    act.wait_ge(turned, hp * UNITS + (n + 1))
                    if n >= 2:
                        act.wait_ge(out_ready, hp * UNITS + n)
                    act.activation(pT[n % 2][:, 0:w], psT[n % 2][:, 0:w], ACT.Copy).then_inc(pT_sb, 1)
                    if n + 2 < UNITS:
                        exponentials(n + 2)

        @block.tensor
        def _(pe):
            with pe.Fori(0, PAIRS) as hp:
                def score(n):
                    u, j = units[n]
                    first, w = j + 1 - tiles(n), tiles(n) * P
                    pe.wait_ge(read_s, hp * UNITS + (n + 1))
                    rows = slice(u * AHD, (u + 1) * AHD)
                    for c0 in range(0, w, HALF):
                        c1 = min(w, c0 + HALF)
                        last = pe.matmul(psS[u][:, c0:c1], q[rows, j * P:(j + 1) * P], k[rows, first * P + c0:first * P + c1],
                                         start=True, stop=True)
                    last.then_inc(scores, 1)

                def turn(n):
                    u = n % 2
                    pe.wait_ge(exped, hp * UNITS + (n + 1))
                    pe.wait_ge(out_sb, hp * UNITS + (n + 1))
                    for t in range(tiles(n)):
                        last = pe.transpose(psT[u][:, t * P:(t + 1) * P], sc[u][:, t * P:(t + 1) * P], m.ident[:, :])
                    last.then_inc(turned, 1)

                pe.wait_ge(copied, hp + 1)
                score(0)
                score(1)
                pe.wait_ge(out_sb, hp * UNITS + 1)
                for n in range(WARM):
                    pe.matmul(psT[0][:, 0:HALF], m.ident[:, :], k[:, 0:HALF], start=True, stop=True)
                turn(0)
                for n, (u, j) in enumerate(units):
                    if n + 2 < UNITS:
                        score(n + 2)
                    if n + 1 < UNITS:
                        turn(n + 1)
                    pe.wait_ge(pT_sb, hp * UNITS + (n + 1))
                    for t in range(tiles(n)):
                        last = pe.matmul(psO[u], pT[u][:, t * P:(t + 1) * P],
                                         v[:, j + 1 - tiles(n) + t, bass.ds(hp * 2 * AHD + u * AHD, AHD)],
                                         start=(t == 0), stop=(t == tiles(n) - 1))
                    last.then_inc(out_ready, 1)

        @block.vector
        def _(dve):
            dve.sem_inc(read_s, 2)
            dve.sem_inc(out_sb, 2)
            with dve.Fori(0, PAIRS) as hp:
                for u in range(2):
                    dve.wait_ge(bias_arrived[u], (hp + 1) * 16)
                    dve.memset(bias[u][0:CH, BAND - CH:BAND], MASKED)
                    dve.memset(bias[u][CH:P, 0:CH], MASKED)
                dve.drain()

                def biased(n):
                    u, w, i = n % 2, tiles(n) * P, n % 4
                    dve.wait_ge(scores, hp * UNITS + (n + 1))
                    if n >= 2:
                        dve.wait_ge(turned, hp * UNITS + (n - 1))
                    dve.tensor_tensor(sc[u][:, 0:w], psS[u][:, 0:w], bias[u][:, BAND - w:BAND], ALU.add).then_inc(read_s, 1)
                    dve.drain()
                    dve.reduce_max(nmx[:, i:i + 1], sc[u][:, 0:w], axis=AX.X, negate=True).then_inc(maxed, 1)

                biased(0)
                biased(1)
                for n, (u, j) in enumerate(units):
                    i = n % 4
                    if n + 2 < UNITS:
                        biased(n + 2)
                    dve.wait_ge(out_ready, hp * UNITS + (n + 2))
                    dve.reciprocal(ri[:, i:i + 1], rs[:, i:i + 1])
                    dve.drain()
                    dve.tensor_scalar(m.att[:, j, bass.ds(hp * 2 * AHD + u * AHD, AHD)], psO[u], ri[:, i:i + 1],
                                      None, ALU.mult).then_inc(out_sb, 1)
                dve.drain()


def shifted(lines):
    w = BAND + P
    flat = lines.rearrange("p n -> (p n)")
    return flat[P - 1:P - 1 + P * (w - 1)].rearrange("(p n) -> p n", n=w - 1)[:, 0:BAND]


def mixer_norm(nc, m, a):
    with ExitStack() as ctx:
        sem = lambda n: nc.alloc_semaphore(fresh(n))
        sb = lambda n, s, d=F32: ctx.enter_context(nc.sbuf_tensor(n, s, d))
        ss, root, inv, junk = sb("y_ss", [P, TT]), sb("y_root", [P, TT]), sb("y_inv", [P, TT]), sb("y_squares", [P, HALF])
        ps = ctx.enter_context(nc.psum_tensor("ps_catT", [P, 4, HALF], F32))
        summed, squares, roots, normed, ps_ready, ps_free, high_made = (
            sem(n) for n in ("y_summed", "y_meaned", "y_rooted", "y_normed", "catT_ready", "catT_free", "catT_high"))
        block = ctx.enter_context(nc.Block())
        y = m.z

        @block.scalar
        def _(act):
            for t in range(TT):
                act.activation(junk[:, :], y[:, t, :], ACT.Square, accum_out=ss[:, t:t + 1]).then_inc(summed, 1)
                act.drain()
            inverse_rms(act, None, ss[:, :], root[:, :], None, HALF, squares, roots)
            high_parts(act, m.cat[1], m.cat[0], ps_free, high_made)

        @block.vector
        def _(dve):
            dve.wait_ge(summed, TT)
            dve.tensor_scalar(ss[:, :], ss[:, :], 1.0 / (SH * SHD), EPS, ALU.mult, ALU.add).then_inc(squares, 1)
            inverse_rms(None, dve, None, root[:, :], inv[:, :], HALF, squares, roots)
            for t in range(TT):
                dve.tensor_scalar(y[:, t, :], y[:, t, :], inv[:, t:t + 1], None, ALU.mult).then_inc(normed, 1)
            row = VEC["ssd_norm_w_2"][0]
            transposes_out(dve, m.cat[1], lambda k: m.cols[:, row + k:row + k + 1] if k < 4 else None, None, ps, ps_ready, ps_free,
                           m.cat[0], high_made)

        @block.tensor
        def _(pe):
            pe.wait_ge(normed, TT)
            for n in range(2 * KT):
                k, half = n // 2, n % 2
                src = y if k < 4 else m.att
                if n >= 4:
                    pe.wait_ge(ps_free, n - 3)
                for j in range(4):
                    last = pe.transpose(ps[:, n % 4, j * P:(j + 1) * P], src[:, 4 * half + j, (k % 4) * P:(k % 4 + 1) * P],
                                        m.ident[:, :])
                last.then_inc(ps_ready, 1)



def ffn_up(nc, m, a):
    hT, uT = m.b1, m.uT
    BASE = 16
    PAD = FTAPS - 1
    with ExitStack() as ctx:
        sem = lambda n: nc.alloc_semaphore(fresh(n))
        sb = lambda n, s, d=F32: ctx.enter_context(nc.sbuf_tensor(n, s, d))
        raw = [[sb(f"up_raw{x}{s}", [P, T + PAD]) for x in range(2)] for s in range(2)]
        conv = [sb(f"up_conv{x}", [P, T]) for x in range(2)]
        ps = ctx.enter_context(nc.psum_tensor("ps_up", [P, 8, HALF], F32))
        ps_ready, ps_free, raw_sb, convolved, silued, made = (
            sem(n) for n in ("up_ready", "up_free", "up_raw_sb", "up_convolved", "up_silu", "up_made"))
        raw_free = sem("up_raw_free")
        block = ctx.enter_context(nc.Block())
        BLOCKS = FT // 2

        @block.sync
        def _(sp):
            m.ring.issue(sp, 2 * (BASE + BLOCKS))

        @block.tensor
        def _(pe):
            with pe.Fori(0, BLOCKS) as i:
                gemm(pe, m, (by_tile(hT),), lambda h: pe.wait_ge(m.ring.loaded[h], i * 32 + m.ring.loads_before(BASE)), i * 8,
                     ps, ps_ready, ps_free, False, (0, 2, 1, 3))

        @block.scalar
        def _(act):
            act.sem_inc(ps_free, 8)
            act.wait_ge(raw_free, 4)

            with act.Fori(0, BLOCKS) as i:
                for c in range(2):
                    n = i * 2 + c
                    act.wait_ge(raw_free, n * 2 + 2)
                    carry(act, m)
                    for j in range(4):
                        act.wait_ge(ps_ready, i * 8 + (4 * c + j + 1))
                        if c == 1 and j == 3:
                            m.ring.release(act)
                        act.copy(raw[c][j // 2][:, PAD + (j % 2) * HALF:PAD + (j % 2 + 1) * HALF], ps[:, 4 * c + j, :])\
                            .then_inc(ps_free, 1)
                    act.drain()
                    act.sem_inc(raw_sb, 1)
                    act.wait_ge(convolved, n + 1)
                    act.activation(conv[0][:, :], conv[0][:, :], ACT.Silu).then_inc(silued, 1)

        @block.vector
        def _(dve):
            for s in range(2):
                for x in range(2):
                    dve.memset(raw[s][x][:, 0:PAD], 0.0).then_inc(raw_free, 1)

            with dve.Fori(0, BLOCKS) as i:
                for c in range(2):
                    n = i * 2 + c
                    dve.wait_ge(raw_sb, n + 1)
                    for x in (1, 0):
                        for j in range(FTAPS):
                            w = m.conv_cols[:, col(j * 2 * FT + x * FT + n)]
                            if j == 0:
                                dve.tensor_scalar(conv[x][:, :], raw[c][x][:, 0:T], w, None, ALU.mult)
                            else:
                                dve.drain()
                                ins = dve.scalar_tensor_tensor(conv[x][:, :], raw[c][x][:, j:j + T], w, conv[x][:, :],
                                                               ALU.mult, ALU.add)
                        if x == 0:
                            ins.then_inc(convolved, 1)
                            dve.sem_inc(raw_free, 2)
                    dve.wait_ge(silued, n + 1)
                    dve.tensor_tensor(uT[:, n, :], conv[0][:, :], conv[1][:, :], ALU.mult).then_inc(made, 1)
                    dve.drain()


def col(n):
    return slice(n, n + 1) if isinstance(n, int) else bass.ds(n, 1)


def ffn_down(nc, m, a):
    uT = m.uT
    PARTS = ((0, 8), (8, 8), (16, 6))
    with ExitStack() as ctx:
        sem = lambda n: nc.alloc_semaphore(fresh(n))
        sb = lambda n, s, d=F32: ctx.enter_context(nc.sbuf_tensor(n, s, d))
        w = [m.ring.buf[:, 2 * i:2 * i + 2].rearrange("p s k n -> p (s k) n") for i in range(2)] + [m.b1[:, 0:3, :].rearrange("p a n -> p (a n)").rearrange("p (k n) -> p k n", n=HALF)]
        x3 = [sb(f"x3_part{s}", [P, HALF]) for s in range(2)]
        temp = sb("down_gated", [P, 2, HALF])
        ps = ctx.enter_context(nc.psum_tensor("ps_down", [P, 8, HALF], F32))
        loaded = [sem(f"down_loaded{i}") for i in range(3)]
        arrived = [sem(f"x3_arrived{s}") for s in range(2)]
        used, ps_ready, ps_free, added = sem("down_used"), sem("down_ready"), sem("down_free"), sem("down_added")
        block = ctx.enter_context(nc.Block())

        @block.sync
        def _(sp):
            def weights(h, i):
                k0, n = PARTS[i]
                if h:
                    sp.wait_ge(used, i + 1)
                sp.dma_start(w[i][:, 0:n, :], a["w_down_2"][0][k0 * P:(k0 + n) * P, h * HALF:(h + 1) * HALF]
                             .rearrange("(k p) n -> p k n", p=P)).then_inc(loaded[i], 16)
            for i in range(3):
                weights(0, i)
            for n in range(2 * TT):
                h, t = n // TT, n % TT
                if n >= 2:
                    sp.wait_ge(added, n - 1)
                sp.dma_start(x3[n % 2][:, :], m.x3_dram[t * P:(t + 1) * P, h * HALF:(h + 1) * HALF]).then_inc(arrived[n % 2], 16)
                if n == 1:
                    weights(1, 0)
                    weights(1, 1)
                if n == TT - 1:
                    weights(1, 2)

        @block.tensor
        def _(pe):
            for h in range(2):
                for i, (k0, n) in enumerate(PARTS):
                    pe.wait_ge(loaded[i], 16 * (h + 1))
                    for t in range(TT):
                        if h and i == 0:
                            pe.wait_ge(ps_free, t + 1)
                        for k in range(n):
                            last = pe.matmul(ps[:, t, :], uT[:, k0 + k, t * P:(t + 1) * P], w[i][:, k, :],
                                             start=(k0 + k == 0), stop=(k0 + k == FT - 1))
                        if i == 2:
                            last.then_inc(ps_ready, 1)
                    if i < 2:
                        last.then_inc(used, 1)

        @block.vector
        def _(dve):
            for n in range(2 * TT):
                h, t = n // TT, n % TT
                dve.wait_ge(ps_ready, n + 1)
                if n == TT - 1:
                    dve.sem_inc(used, 1)
                dve.tensor_tensor(temp[:, n % 2, :], ps[:, t, :], m.gate_ffn[:, h * HALF:(h + 1) * HALF], ALU.mult).then_inc(ps_free, 1)
                dve.drain()
                dve.wait_ge(arrived[n % 2], 16 * (n // 2 + 1))
                dve.tensor_tensor(m.xf[h][:, t, :], temp[:, n % 2, :], x3[n % 2][:, :], ALU.add).then_inc(added, 1)


def final_norm(nc, m, a, out):
    with ExitStack() as ctx:
        sem = lambda n: nc.alloc_semaphore(fresh(n))
        sb = lambda n, s, d=F32: ctx.enter_context(nc.sbuf_tensor(n, s, d))
        ss, root, inv, junk = sb("f_ss", [P, 2, TT]), sb("f_root", [P, TT]), sb("f_inv", [P, TT]), sb("f_squares", [P, HALF])
        gain = sb("final_norm_2_wide", [P, D])
        gain_arrived, summed, squares, roots, normed, stored = (
            sem(n) for n in ("f_gain", "f_summed", "f_meaned", "f_rooted", "f_normed", "out_stored"))
        block = ctx.enter_context(nc.Block())

        @block.sync
        def _(sp):
            sp.dma_start(gain[:, :], spread(a["final_norm_w_2"].rearrange("(o d) -> o d", o=1))).then_inc(gain_arrived, 16)
            for t in range(TT):
                for h in range(2):
                    sp.wait_ge(normed, 2 * t + h + 1)
                    sp.dma_start(out[0, t * P:(t + 1) * P, h * HALF:(h + 1) * HALF], m.xf[h][:, t, :]).then_inc(stored, 16)
            sp.wait_ge(stored, 16 * 2 * TT)

        @block.scalar
        def _(act):
            for t in range(TT):
                for h in range(2):
                    act.activation(junk[:, :], m.xf[h][:, t, :], ACT.Square, accum_out=ss[:, h, t:t + 1]).then_inc(summed, 1)
                    act.drain()
            inverse_rms(act, None, ss[:, 0, :], root[:, :], None, D, squares, roots)

        @block.vector
        def _(dve):
            dve.wait_ge(summed, 2 * TT)
            dve.tensor_tensor(ss[:, 0, :], ss[:, 0, :], ss[:, 1, :], ALU.add)
            dve.drain()
            dve.tensor_scalar(ss[:, 0, :], ss[:, 0, :], 1.0 / D, EPS, ALU.mult, ALU.add).then_inc(squares, 1)
            inverse_rms(None, dve, None, root[:, :], inv[:, :], D, squares, roots)
            dve.wait_ge(gain_arrived, 16)
            for t in range(TT):
                for h in range(2):
                    x = m.xf[h][:, t, :]
                    dve.scalar_tensor_tensor(x, x, inv[:, t:t + 1], gain[:, h * HALF:(h + 1) * HALF], ALU.mult, ALU.mult)\
                        .then_inc(normed, 1)



def program(nc, a, out):
    _names.clear()
    _rounded.clear()
    with ExitStack() as ctx:
        ctx.enter_context(nc.allow_non_contiguous_dma(reason="columns and broadcasts"))
        sb = lambda n, s, d=F32: ctx.enter_context(nc.sbuf_tensor(n, s, d))
        dram = lambda n, s, d=F32: nc.dram_tensor(n, s, d).ap()
        m = Parts()
        PAD = TAPS - 1
        size2 = KT * (T + PAD)
        m.big = both_kinds(nc, ctx, "big", [P, 3 * 8 * D + size2], parts=4, part=8 * D)
        cut = lambda at, w=D: m.big[:, at:at + 8 * w].rearrange("p (t n) -> p t n", t=8)
        m.b1, m.b3, m.b4 = cut(0), cut(8 * D), cut(16 * D)
        m.b2, m.raw = cut(24 * D), cut(24 * D, T + PAD)
        m.uT = m.big[:, 8 * D:(8 + FT) * D].rearrange("p (t n) -> p t n", t=FT)
        m.ident, m.ones = sb("ident", [P, P]), sb("ones", [P, P])
        m.upto, m.after, m.before = sb("upto", [P, P]), sb("after", [P, P]), sb("before", [P, P])
        m.chunk_ones = sb("chunk_ones", [P, 2, P])
        m.expert_iota_i, m.expert_iota = sb("expert_iota_i", [P, EXPERTS], I32), sb("expert_iota", [P, EXPERTS])
        m.part_iota_i, m.part_iota = sb("part_iota_i", [P, 1], I32), sb("part_iota", [P, 1])
        m.codes_i = sb("codes_i", [P, 2 * TT], I32)
        m.cols, m.conv_cols = sb("vector_cols", [P, VROWS]), sb("conv_cols", [P, FROWS])
        m.gate_mix, m.gate_ffn = sb("gate_mix", [P, D]), sb("gate_ffn", [P, D])
        m.shift_mix, m.scale_mix = sb("shift_mix", [P, KT]), sb("scale_mix", [P, KT])
        m.shift_ffn, m.scale_ffn = sb("shift_ffn", [P, KT]), sb("scale_ffn", [P, KT])
        m.w13 = [b[:, 4 * j:4 * j + 4, :].rearrange("p a n -> p (a n)").rearrange("p (w k n) -> p w k n", w=2, k=KT)
                 for b in (m.b3, m.b1) for j in range(2)]
        m.w2 = [m.b2[:, 2 * j:2 * j + 2, :] for j in range(4)]
        m.w13_loaded = [ctx.enter_context(nc.semaphore(f"w13_loaded{u}")) for u in range(4)]
        m.w2_loaded = [ctx.enter_context(nc.semaphore(f"w2_loaded{u}")) for u in range(4)]
        m.scatter_idx, m.gather_idx = sb("scatter_idx", [SLOTS, EXPERTS], I32), sb("gather_idx", [SLOTS, EXPERTS], I32)
        m.gates2 = sb("expert_gates", [P, 2, TT])
        m.info_row, m.n_extra = sb("info_row", [1, 2 * P], I32), sb("n_extra", [1, 1], I32)
        m.info_dram = dram("block_info_d", (P, 2), I32)
        words = lambda b, t: b[:, t:t + 4, :].rearrange("p a n -> p (a n)").rearrange("p (t n) -> p t n", n=HALF)
        m.z, m.v, m.att = words(m.b4, 0), words(m.b4, 4), words(m.b1, 0)
        m.cat = (by_tile(m.b2), lambda k: m.b1[:, 4 + k, :] if k < 4 else m.b4[:, k, :])
        m.xf = [words(m.b1, 4), words(m.b3, 0)]
        m.dt, m.adt, m.d_skip = sb("dt", [P, TT, SH]), sb("adt", [P, TT, SH]), sb("d_skip_wide", [P, SH])
        m.codes = dram("slot_codes", (T * EXPERTS, 1), I32)
        m.bias_lines = dram("bias_lines", (AH, P, BAND + P))
        m.xn_dram = dram("normed_tokens", (T, D))
        m.contrib = dram("contributions", (2 * T, D))
        m.x2_dram = dram("x2", (T, D))
        m.r_dram = dram("gla_gate", (T, D))
        m.z_dram, m.v_dram = dram("silu_z", (T, HALF)), dram("values", (T, HALF))
        m.x3_dram = dram("x3", (T, D))

        w1 = a["gla_w_in"][0]
        w2 = a["w_in_2"][0]
        c = lambda w, at, n=HALF: w[:, at:at + n]
        sources = [[c(w1, b * HALF)] for b in range(4)] + [[c(w1, 2064 + b * HALF)] for b in range(2)]
        sources += [[c(a["gla_w_o"][0], b * HALF)] for b in range(2)]
        sources += [[c(w2, at)] for at in (IN_AT["xbc"], IN_AT["xbc"] + HALF, IN_AT["q"], IN_AT["k"], IN_AT["z"], IN_AT["v"])]
        sources += [[c(a["w_out_2"][0], b * HALF)] for b in range(2)]
        sources += [[c(a["w_up_2"][0], f * 256, 256), c(a["w_up_2"][0], FDIM + f * 256, 256)] for f in range(FT // 2)]
        m.ring = Ring(nc, ctx, sources)

        x = a["x"][0]
        m.carried = ctx.enter_context(nc.semaphore("waits_carried"))
        col = lambda name: (lambda k: m.cols[:, VEC[name][0] + k:VEC[name][0] + k + 1])

        m.resets = sb("resets", [P, T])
        with nc.cleanup_on_exit():
            constants(nc, m, a)
            modulation(nc, m, a)
            rms_to_channels(nc, m, m.b2, m.b2, m.b4, col("attn_norm"), None, high=m.b1, loads=x)
            with nc.sbuf_tensor("log_gates", [P, GH, T], F32) as m.gates:
                gla_projections(nc, m, a)
                gla_chunks(nc, m, a)
            gla_output(nc, m, a)
            project_back(nc, m, (by_tile(m.b1), by_tile(m.b2)), m.b4, x, 6)
        with nc.cleanup_on_exit():
            rms_to_channels(nc, m, m.b4, m.b3, m.b1, col("ffn_norm"), None, to_dram=m.xn_dram)
            router(nc, m, a)
            experts(nc, m, a)
            more_blocks(nc, m, a)
            combine(nc, m, a)
        with nc.cleanup_on_exit():
            rms_to_channels(nc, m, m.b4, m.b3, m.b4, lambda k: m.scale_mix[:, k:k + 1], lambda k: m.shift_mix[:, k:k + 1],
                            high=m.b1)
            mixer_projections(nc, m, a)
            state_space(nc, m, a)
            band_attention(nc, m, a)
            mixer_norm(nc, m, a)
            project_back(nc, m, m.cat, m.b3, m.x2_dram, 14, gate=m.gate_mix)
            rms_to_channels(nc, m, m.b3, m.b4, m.b1, lambda k: m.scale_ffn[:, k:k + 1], lambda k: m.shift_ffn[:, k:k + 1],
                            spill=m.x3_dram)
            ffn_up(nc, m, a)
            ffn_down(nc, m, a)
            final_norm(nc, m, a, out)


INPUTS = ("a_log_2", "attn_norm", "b_ada_2", "c_2", "d_skip_2", "dt_bias_2", "ffn_conv_w_2", "ffn_norm",
          "final_norm", "final_norm_w_2", "gla_b_gate", "gla_out_norm", "gla_w_gate", "gla_w_in", "gla_w_o",
          "moe_w1", "moe_w2", "moe_w3", "moe_w_expert", "moe_w_group", "norm_ffn_w_2", "norm_mix_w_2",
          "rel_bias_2", "ssd_conv_b_2", "ssd_conv_w_2", "ssd_norm_w_2", "w_ada_2", "w_down_2", "w_in_2",
          "w_out_2", "w_up_2", "x")


def kernel(**inputs):
    import numpy as np
    import concourse.bacc as bacc
    from concourse import mybir
    from concourse.bass_utils import run_bass_kernel_spmd

    nc = bacc.Bacc("TRN2", target_bir_lowering=False, num_devices=1)
    arrays, aps = {}, {}
    for name in INPUTS:
        array = np.ascontiguousarray(inputs[name])
        arrays[f"in_{name}_dram"] = array
        aps[name] = nc.dram_tensor(f"in_{name}_dram", array.shape, mybir.dt.from_np(array.dtype), kind="ExternalInput").ap()
    out = nc.dram_tensor("out_0_dram", (1, T, D), mybir.dt.float32, kind="ExternalOutput").ap()
    program(nc, aps, out)
    result = run_bass_kernel_spmd(nc, [arrays], core_ids=[0])
    return result.results[0]["out_0_dram"]
```

```python
import numpy as np
import concourse.bass as bass
from concourse import mybir
from contextlib import ExitStack

F32 = mybir.dt.float32
F32R = mybir.dt.float32r
I32 = mybir.dt.int32
U32 = mybir.dt.uint32
ALU = mybir.AluOpType
ACT = mybir.ActivationFunctionType
AX = mybir.AxisListType

P = 128
T = 1024
D = 1024
TT = T // P
KT = D // P
HALF = 512
EPS = 1e-6
CH = 64

GH, GDK, GDV, RANK, TAU = 4, 128, 256, 16, 16.0
GROUPS, PER_GROUP, EXPERTS, FF = 8, 8, 64, 256
SLOTS = 64
NOWHERE = 8192
SH, SHD, SG, SN = 8, 64, 2, 128
HPG = SH // SG
TAPS = 4
AH, AHD = 8, 64
BANDT = 5
BAND = BANDT * P
NREL, MAXREL = 257, 128
MASKED = -1e30
FDIM = 2816
FT = FDIM // P
FTAPS = 3

IN_AT = {"z": 0, "xbc": 512, "dt": 1536, "q": 1544, "k": 2056, "v": 2568}

VEC = {}
_row = 0
for _name, _n in (("attn_norm", KT), ("ffn_norm", KT), ("gla_b_gate", GH), ("norm_mix_w_2", KT), ("norm_ffn_w_2", KT),
                  ("ssd_norm_w_2", 4), ("ssd_conv_b_2", KT), ("ssd_conv_w_2", TAPS * KT), ("c_2", KT),
                  ("gla_out_norm", GDV // P)):
    VEC[_name] = (_row, _n)
    _row += _n
VROWS = _row
FROWS = FTAPS * 2 * FT
FSPLIT = FROWS // 2


_names = {}


def fresh(name):
    _names[name] = _names.get(name, 0) + 1
    return f"{name}_{_names[name]}"


def rows_of(ap):
    return ap.rearrange("(r c) -> r c", c=P)


def spread(ap, n=P):
    return ap.to_broadcast([n, ap.shape[1]])


class Parts:
    pass


def carry(engine, m):
    engine.sem_inc(m.carried, 1)


_rounded = {}


def both_kinds(nc, ctx, name, shape, parts=1, part=None):
    start = -(-nc.sbuf_base // 32) * 32
    t = ctx.enter_context(nc.sbuf_tensor(name, shape, F32))
    words = int(np.prod(shape[1:]))
    assert nc.sbuf_base == start + 4 * words
    part = part or words
    _rounded[t.name] = (part, [nc.alloc_sbuf_tensor_at(f"{name}_rounded{i}", [P, part], F32R, offset=start + 4 * part * i)
                               for i in range(parts)])
    return t


def R(ap):
    part, tensors = _rounded[ap.tensor.name]
    return bass.AP(tensor=tensors[ap.offset // part], offset=ap.offset % part, ap=[[part, P]] + list(ap.ap)[1:])


def rounded(ap):
    return R(ap).bitcast(F32)


def by_tile(buf):
    return lambda k: buf[:, k, :]



def transposes(pe, m, src, tiles_ready, ps, ps_ready, ps_free):
    for n in range(2 * KT):
        k, half = n // 2, n % 2
        if n == 0:
            tiles_ready(pe)
        if n >= 4:
            pe.wait_ge(ps_free, n - 3)
        for j in range(4):
            last = pe.transpose(ps[:, n % 4, j * P:(j + 1) * P], src[:, 4 * half + j, k * P:(k + 1) * P],
                                m.ident[:, :])
        last.then_inc(ps_ready, 1)


def transposes_out(dve, dst, gain, bias, ps, ps_ready, ps_free, high=None, high_made=None):
    def low_part(k):
        dve.wait_ge(high_made, k + 1)
        dve.tensor_tensor(R(dst(k)), dst(k), rounded(high(k)), ALU.subtract)

    for n in range(2 * KT):
        k, half = n // 2, n % 2
        dve.wait_ge(ps_ready, n + 1)
        out = dst(k)[:, half * HALF:(half + 1) * HALF]
        g = gain(k)
        if g is None:
            ins = dve.tensor_copy(out, ps[:, n % 4, :])
        elif bias is None:
            ins = dve.tensor_scalar(out, ps[:, n % 4, :], g, None, ALU.mult)
        else:
            ins = dve.tensor_scalar(out, ps[:, n % 4, :], g, bias(k), ALU.mult, ALU.add)
        ins.then_inc(ps_free, 1)
        if high is not None and n % 2 == 1 and k > 0:
            low_part(k - 1)
    if high is not None:
        low_part(KT - 1)


def high_from_banks(act, high, gain, ps, ps_ready, high_made):
    for n in range(2 * KT):
        k, cols = n // 2, slice(n % 2 * HALF, (n % 2 + 1) * HALF)
        act.wait_ge(ps_ready, n + 1)
        g = gain(k)
        act.activation(R(high(k)[:, cols]), ps[:, n % 4, :], ACT.Copy, scale=1.0 if g is None else g).then_inc(high_made, 1)


def low_from_banks(dve, high, low, gain, ps, ps_free, high_made):
    for n in range(2 * KT):
        k, cols = n // 2, slice(n % 2 * HALF, (n % 2 + 1) * HALF)
        dve.wait_ge(high_made, n + 1)
        g = gain(k)
        dve.scalar_tensor_tensor(R(low(k)[:, cols]), ps[:, n % 4, :], 1.0 if g is None else g, rounded(high(k)[:, cols]),
                                 ALU.mult, ALU.subtract).then_inc(ps_free, 1)


def high_parts(act, src, high, ps_free, high_made):
    for k in range(KT):
        act.wait_ge(ps_free, 2 * k + 2)
        act.activation(R(high(k)), src(k), ACT.Copy).then_inc(high_made, 1)


def sum_squares(act, dve, parts, junk, sums, arrived=None):
    for i, (src, total) in enumerate(parts):
        engine = (act, dve)[i % 2]
        if arrived and engine is not None:
            engine.wait_ge(arrived[i], 16)
        if i % 2 == 0 and act is not None:
            act.activation(junk[:, 0, 0:src.shape[1]], src, ACT.Square, accum_out=total).then_inc(sums, 1)
            act.drain()
        if i % 2 == 1 and dve is not None:
            dve.tensor_tensor_reduce(junk[:, 1, 0:src.shape[1]], src, src, 1.0, 0.0, ALU.mult, ALU.add, total)
            dve.drain()
            dve.sem_inc(sums, 1)


def inverse_rms(act, dve, ss, root, inv, width, squares, roots):
    if act is not None:
        act.wait_ge(squares, 1)
        act.activation(root, ss, ACT.Sqrt).then_inc(roots, 1)
    if dve is not None:
        dve.wait_ge(roots, 1)
        dve.reciprocal(inv, root)
        dve.drain()


def rms_to_channels(nc, m, src, xn, dst, gain, bias, high=None, loads=None, to_dram=None, spill=None):
    with ExitStack() as ctx:
        sem = lambda n: nc.alloc_semaphore(fresh(n))
        arrived = [sem(f"x_tile_arrived{t}") for t in range(TT)] if loads is not None else None
        squares, roots, scaled = sem("squares_summed"), sem("roots_taken"), sem("tiles_scaled")
        ps_ready, ps_free, stored = sem("transposed"), sem("transposed_out"), sem("normed_stored")
        ss = ctx.enter_context(nc.sbuf_tensor(fresh("sum_sq"), [P, TT], F32))
        root = ctx.enter_context(nc.sbuf_tensor(fresh("root"), [P, TT], F32))
        inv = ctx.enter_context(nc.sbuf_tensor(fresh("inv_rms"), [P, TT], F32))
        junk = ctx.enter_context(nc.sbuf_tensor(fresh("squares"), [P, 2, D], F32))
        squared = [(src[:, t, :], ss[:, t:t + 1]) for t in range(TT)]
        sums, high_made = sem("act_sums"), sem("high_made")
        ps = ctx.enter_context(nc.psum_tensor(fresh("ps_transposed"), [P, 4, HALF], F32))
        block = ctx.enter_context(nc.Block())

        @block.sync
        def _(sp):
            if loads is not None:
                for t in range(TT):
                    sp.dma_start(src[:, t, :], loads[t * P:(t + 1) * P, :]).then_inc(arrived[t], 16)
            if spill is not None:
                sp.dma_start(spill.rearrange("(t p) d -> p t d", p=P), src).then_inc(stored, 16)
                sp.wait_ge(stored, 16)
            if to_dram is not None:
                sp.wait_ge(scaled, TT)
                sp.dma_start(to_dram.rearrange("(t p) d -> p t d", p=P), xn).then_inc(stored, 16)
                sp.wait_ge(stored, 16)

        @block.scalar
        def _(act):
            sum_squares(act, None, squared, junk, sums, arrived)
            inverse_rms(act, None, ss[:, :], root[:, :], None, D, squares, roots)
            if high is not None and bias is None:
                high_from_banks(act, by_tile(high), gain, ps, ps_ready, high_made)
            elif high is not None:
                high_parts(act, by_tile(dst), by_tile(high), ps_free, high_made)

        @block.vector
        def _(dve):
            sum_squares(None, dve, squared, junk, sums, arrived)
            dve.wait_ge(sums, TT)
            dve.tensor_scalar(ss[:, :], ss[:, :], 1.0 / D, EPS, ALU.mult, ALU.add).then_inc(squares, 1)
            inverse_rms(None, dve, None, root[:, :], inv[:, :], D, squares, roots)
            for t in range(TT):
                dve.tensor_scalar(xn[:, t, :], src[:, t, :], inv[:, t:t + 1], None, ALU.mult).then_inc(scaled, 1)
            if high is not None and bias is None:
                low_from_banks(dve, by_tile(high), by_tile(dst), gain, ps, ps_free, high_made)
            else:
                transposes_out(dve, by_tile(dst), gain, bias, ps, ps_ready, ps_free, None if high is None else by_tile(high), high_made)

        @block.tensor
        def _(pe):
            transposes(pe, m, xn, lambda e: e.wait_ge(scaled, TT), ps, ps_ready, ps_free)


class Ring:

    def __init__(self, nc, ctx, sources):
        self.buf = both_kinds(nc, ctx, "weight_ring", [P, 4, KT // 2, HALF])
        self.low = [self.buf[:, s] for s in range(2)]
        self.high = [self.buf[:, 2 + s] for s in range(2)]
        self.loaded = [ctx.enter_context(nc.semaphore(f"weights_loaded{s}")) for s in range(2)]
        self.used = ctx.enter_context(nc.semaphore("weights_used"))
        self.high_made = ctx.enter_context(nc.semaphore("weights_high"))
        self.split = ctx.enter_context(nc.semaphore("weights_split"))
        self.sources, self.issued = sources, 0

    def issue(self, sp, end):
        for i in range(self.issued, end):
            if i >= 2:
                sp.wait_ge(self.used, i - 1)
            at, h = 0, i % 2
            for src in self.sources[i // 2]:
                n = src.shape[1]
                sp.dma_start(self.low[h][:, :, at:at + n],
                             src[h * D // 2:(h + 1) * D // 2, :].rearrange("(k p) n -> p k n", p=P)).then_inc(self.loaded[h], 16)
                at += n
        self.issued = end

    def loads_before(self, b):
        return 16 * sum(len(self.sources[c]) for c in range(b + 1))

    def make_high(self, act, i):
        act.wait_ge(self.loaded[i % 2], self.loads_before(i // 2))
        act.activation(R(self.high[i % 2]), self.low[i % 2], ACT.Copy).then_inc(self.high_made, 1)

    def make_low(self, dve, i):
        dve.wait_ge(self.high_made, i + 1)
        dve.tensor_tensor(R(self.low[i % 2]), self.low[i % 2], rounded(self.high[i % 2]), ALU.subtract).then_inc(self.split, 1)

    def release(self, engine):
        engine.sem_inc(self.used, 1)


def evacuate_split(act, m, blocks, evacuate, before_last=None):
    first, end = blocks
    for i in range(2):
        m.ring.make_high(act, 2 * first + i)
    if before_last is not None:
        before_last()
    for b in range(first, end):
        for j in range(8):
            evacuate((b - first) * 8 + j, j == 7)
            if j == 2 and b + 1 < end:
                m.ring.make_high(act, 2 * b + 2)
        if b + 1 < end:
            m.ring.make_high(act, 2 * b + 3)


def gemm(pe, m, acts, weights_ready, n0, ps, ps_ready, ps_free, tokens, tiles=range(4)):
    for h in range(2):
        weights_ready(h)
        weights = (m.ring.high[h], m.ring.low[h]) if len(acts) == 2 else (m.ring.low[h],)
        pairs = ((0, 0), (0, 1), (1, 0)) if len(acts) == 2 else ((0, 0),)
        view = R if len(acts) == 2 else (lambda ap: ap)
        for n in range(8):
            if h == 0:
                pe.wait_ge(ps_free, n0 + n + 1)
            for k in range(4):
                for i, j in pairs:
                    first, final = h == k == i == j == 0, h == 1 and k == 3 and (i, j) == pairs[-1]
                    if tokens:
                        left, right = acts[i](4 * h + k)[:, n * P:(n + 1) * P], weights[j][:, k, :]
                    else:
                        c, half = tiles[n // 2], n % 2
                        left, right = weights[i][:, k, c * P:(c + 1) * P], acts[j](4 * h + k)[:, half * HALF:(half + 1) * HALF]
                    last = pe.matmul(ps[:, n, :], view(left), view(right), start=first, stop=final)
            if h == 1:
                last.then_inc(ps_ready, 1)
            elif n == 7:
                last.then_inc(m.ring.used, 1)


def store_stage(act, sp_free, n):
    if n >= 4:
        act.wait_ge(sp_free[n % 4], 16 * (n // 4))



def constants(nc, m, a):
    with ExitStack() as ctx:
        sem = lambda n: nc.alloc_semaphore(fresh(n))
        sb = lambda n, s, d=F32: ctx.enter_context(nc.sbuf_tensor(n, s, d))
        rows_arrived, rel_arrived, made, cast = sem("rows_arrived"), sem("rel_arrived"), sem("masks_made"), sem("columns")
        frows_arrived, bias_rows, bias_stored, filled = sem("conv_rows"), sem("bias_rows"), sem("bias_stored"), sem("filled")
        vrows = sb("vector_rows", [VROWS, P])
        frows = sb("conv_rows", [FSPLIT, 2, P])
        rel = sb("rel_bias_rows", [AH, NREL])
        line = sb("bias_line", [AH, BAND + P])
        nowhere = sb("nowhere", [P, T * EXPERTS // P], I32)
        ps = ctx.enter_context(nc.psum_tensor("ps_columns", [P, 3, HALF], F32))
        block = ctx.enter_context(nc.Block())

        @block.sync
        def _(sp):
            for name, (row, n) in VEC.items():
                src = a[name]
                if name == "ssd_conv_w_2":
                    src = src[0].rearrange("k (r c) -> (k r) c", c=P)
                else:
                    src = rows_of(src[0] if len(src.shape) == 2 else src)
                sp.dma_start(vrows[row:row + n, :], src).then_inc(rows_arrived, 16)
            conv = a["ffn_conv_w_2"][0].rearrange("k (r c) -> (k r) c", c=P)
            for s in range(2):
                sp.dma_start(frows[:, s, :], conv[s * FSPLIT:(s + 1) * FSPLIT, :]).then_inc(frows_arrived, 16)
            sp.dma_start(rel[:, :], a["rel_bias_2"][0]).then_inc(rel_arrived, 16)
            m.ring.issue(sp, 2)
            sp.wait_ge(filled, 1)
            sp.dma_start(m.codes.rearrange("(p n) o -> p (n o)", p=P), nowhere[:, :]).then_inc(bias_stored, 16)
            sp.wait_ge(bias_rows, 1)
            for h in range(AH):
                sp.dma_start(m.bias_lines[h], line[h:h + 1, None, :].to_broadcast([1, P, BAND + P])).then_inc(bias_stored, 16)
            sp.wait_ge(bias_stored, 16 * (AH + 1))

        @block.gpsimd
        def _(pool):
            pool.memset(m.ident[:, :], 0.0)
            pool.memset(m.ones[:, :], 1.0)
            pool.memset(m.upto[:, :], 1.0)
            pool.memset(m.after[:, :], 1.0)
            pool.memset(m.before[:, :], 1.0)
            pool.memset(m.chunk_ones[:, :, :], 0.0)
            pool.memset(nowhere[:, :], NOWHERE)
            pool.drain()
            pool.affine_select(out=m.ident[:, :], in_=m.ident[:, :], compare_op=ALU.not_equal, fill=1.0, base=0,
                               pattern=[[-1, P]], channel_multiplier=1)
            pool.affine_select(out=m.upto[:, :], in_=m.upto[:, :], compare_op=ALU.is_ge, fill=0.0, base=0,
                               pattern=[[1, P]], channel_multiplier=-1)
            pool.affine_select(out=m.after[:, :], in_=m.after[:, :], compare_op=ALU.is_gt, fill=0.0, base=0,
                               pattern=[[-1, P]], channel_multiplier=1)
            pool.affine_select(out=m.before[:, :], in_=m.before[:, :], compare_op=ALU.is_gt, fill=0.0, base=0,
                               pattern=[[1, P]], channel_multiplier=-1)
            pool.drain()
            pool.memset(m.upto[0:CH, CH:P], 0.0)
            pool.drain()
            pool.memset(m.after[CH:P, 0:CH], 0.0)
            for c in range(2):
                pool.drain()
                pool.memset(m.chunk_ones[c * CH:(c + 1) * CH, c, :], 1.0)
            pool.drain()
            pool.memset(m.resets[:, :], 1.0)
            pool.drain()
            pool.memset(m.resets[:, :].rearrange("p (n c) -> p n c", c=CH)[:, :, 0:1], 0.0)
            pool.iota(m.expert_iota_i[:, :], pattern=[[1, EXPERTS]], base=0, channel_multiplier=0)
            pool.iota(m.codes_i[:, :], pattern=[[T, 2], [P, TT]], base=0, channel_multiplier=1)
            pool.iota(m.part_iota_i[:, :], pattern=[[0, 1]], base=0, channel_multiplier=1)
            pool.drain()
            pool.tensor_copy(m.expert_iota[:, :], m.expert_iota_i[:, :])
            pool.tensor_copy(m.part_iota[:, :], m.part_iota_i[:, :])
            pool.drain()
            pool.sem_inc(made, 1)
            pool.sem_inc(filled, 1)

        @block.tensor
        def _(pe):
            pe.wait_ge(made, 1)
            pe.wait_ge(rows_arrived, 16 * len(VEC))
            pe.transpose(ps[:, 0, 0:VROWS], vrows[:, :], m.ident[0:VROWS, 0:VROWS])
            pe.wait_ge(frows_arrived, 32)
            pe.transpose(ps[:, 1, 0:FSPLIT], frows[:, 0, :], m.ident[0:FSPLIT, 0:FSPLIT])
            pe.transpose(ps[:, 2, 0:FSPLIT], frows[:, 1, :], m.ident[0:FSPLIT, 0:FSPLIT]).then_inc(cast, 1)

        @block.vector
        def _(dve):
            dve.wait_ge(rel_arrived, 16)
            far = BAND + P - 1 - (NREL - 2)
            dve.memset(line[:, :], 0.0)
            dve.drain()
            dve.tensor_scalar(line[:, 0:far + 1], line[:, 0:far + 1], rel[:, NREL - 1:NREL], None, ALU.add)
            dve.drain()
            dve.tensor_copy(line[:, far:far + NREL - 2], rel[:, NREL - 2:0:-1]).then_inc(bias_rows, 1)
            dve.wait_ge(cast, 1)
            dve.tensor_copy(m.cols[:, :], ps[:, 0, 0:VROWS])
            dve.tensor_copy(m.conv_cols[:, 0:FSPLIT], ps[:, 1, 0:FSPLIT])
            dve.tensor_copy(m.conv_cols[:, FSPLIT:FROWS], ps[:, 2, 0:FSPLIT])
            dve.drain()



def modulation(nc, m, a):
    NB = 6 * D // HALF
    with ExitStack() as ctx:
        sem = lambda n: nc.alloc_semaphore(fresh(n))
        sb = lambda n, s, d=F32: ctx.enter_context(nc.sbuf_tensor(n, s, d))
        c_act = sb("c_act", [P, KT])
        c_wide = sb("c_wide", [P, KT, P])
        mod = m.big[:, 0:6 * D]
        w = [m.big[:, 6 * D + s * KT * HALF:6 * D + (s + 1) * KT * HALF].rearrange("p (k n) -> p k n", k=KT)
             for s in range(4)]
        b_row = sb("b_ada_row", [1, 6 * D])
        ps = ctx.enter_context(nc.psum_tensor("ps_mod", [P, 4, HALF], F32))
        pst = ctx.enter_context(nc.psum_tensor("ps_mod_t", [P, 4, HALF], F32))
        loaded = [sem(f"ada_loaded{s}") for s in range(4)]
        bias_row, activated, wide = sem("ada_bias"), sem("c_activated"), sem("c_widened")
        ps_ready, ps_free, turned = sem("mod_ready"), sem("mod_free"), sem("mod_turned")
        block = ctx.enter_context(nc.Block())

        @block.sync
        def _(sp):
            sp.dma_start(b_row[:, :], a["b_ada_2"]).then_inc(bias_row, 16)
            for b in range(NB):
                if b >= 4:
                    sp.wait_ge(ps_ready, b - 3)
                sp.dma_start(w[b % 4], a["w_ada_2"][0][:, b * HALF:(b + 1) * HALF]
                             .rearrange("(k p) n -> p k n", p=P)).then_inc(loaded[b % 4], 16)

        @block.scalar
        def _(act):
            row, n = VEC["c_2"]
            act.activation(c_act[:, :], m.cols[:, row:row + n], ACT.Silu).then_inc(activated, 1)

        @block.vector
        def _(dve):
            dve.wait_ge(activated, 1)
            dve.tensor_copy(c_wide[:, :, :], c_act[:, :, None].to_broadcast([P, KT, P])).then_inc(wide, 1)
            for b in range(NB):
                dve.wait_ge(ps_ready, b + 1)
                dve.tensor_copy(mod[:, b * HALF:(b + 1) * HALF], ps[:, b % 4, :]).then_inc(ps_free, 1)
            dve.drain()
            dve.tensor_copy(m.gate_mix[:, :], mod[:, 2 * D:3 * D])
            dve.tensor_copy(m.gate_ffn[:, :], mod[:, 5 * D:6 * D])
            for i, (dst, gain) in enumerate(((m.shift_mix, None), (m.scale_mix, "norm_mix_w_2"),
                                             (m.shift_ffn, None), (m.scale_ffn, "norm_ffn_w_2"))):
                for half in range(2):
                    n = 2 * i + half
                    dve.wait_ge(turned, n + 1)
                    src = pst[:, n % 4, :].rearrange("p (j c) -> p j c", j=4)[:, :, 0:1]
                    out = dst[:, 4 * half:4 * half + 4, None]
                    if gain is None:
                        dve.tensor_copy(out, src).then_inc(ps_free, 1)
                    else:
                        row = VEC[gain][0] + 4 * half
                        dve.tensor_scalar(out, src, 1.0, None, ALU.add).then_inc(ps_free, 1)
                        dve.drain()
                        dve.tensor_tensor(out, out, m.cols[:, row:row + 4, None], ALU.mult)
            dve.drain()

        @block.tensor
        def _(pe):
            pe.wait_ge(wide, 1)
            pe.wait_ge(bias_row, 16)
            for b in range(NB):
                pe.wait_ge(loaded[b % 4], 16 * (b // 4 + 1))
                if b >= 4:
                    pe.wait_ge(ps_free, b - 3)
                for k in range(KT):
                    pe.matmul(ps[:, b % 4, :], c_wide[:, k, :], w[b % 4][:, k, :], start=(k == 0), stop=False)
                pe.matmul(ps[:, b % 4, :], m.ones[0:1, :], b_row[:, b * HALF:(b + 1) * HALF],
                          start=False, stop=True).then_inc(ps_ready, 1)
            pe.wait_ge(ps_free, NB)
            for i, part in enumerate((0, 1, 3, 4)):
                for half in range(2):
                    n = 2 * i + half
                    if n >= 4:
                        pe.wait_ge(ps_free, NB + n - 3)
                    for j in range(4):
                        at = part * D + (4 * half + j) * P
                        last = pe.transpose(pst[:, n % 4, j * P:(j + 1) * P], mod[:, at:at + P], m.ident[:, :])
                    last.then_inc(turned, 1)



def gla_projections(nc, m, a):
    acts = (by_tile(m.b1), by_tile(m.b4))
    qk, v = m.b2, m.b3
    with ExitStack() as ctx:
        sem = lambda n: nc.alloc_semaphore(fresh(n))
        sb = lambda n, s, d=F32: ctx.enter_context(nc.sbuf_tensor(n, s, d))
        w_lr = [both_kinds(nc, ctx, f"w_low_rank{i}", [P, KT, RANK]) for i in range(2)]
        mag = m.b3[:, 0:GH, :]
        lrT = m.b3[0:RANK, GH, :]
        w_gate = m.b3[0:RANK, GH + 1, 0:GH * GDK]
        stage = sb("r_stage", [P, 4, HALF])
        gates = m.gates
        ps = ctx.enter_context(nc.psum_tensor("ps_gla_in", [P, 8, HALF], F32))
        ps_lr = ps[:, 6:8, :]
        small_loaded, ps_ready, ps_free = sem("gate_weights"), sem("proj_ready"), sem("proj_free")
        lr_high, lr_split, staged = sem("lr_high"), sem("lr_split"), sem("r_staged")
        stored = [sem(f"r_stored{s}") for s in range(4)]
        lr_ready, lr_sb, gate_ready, gate_free = sem("lr_ready"), sem("lr_in_sbuf"), sem("gate_ready"), sem("gate_free")
        biased, logged, scanned = sem("biased"), sem("logged"), sem("scanned")
        block = ctx.enter_context(nc.Block())
        a_col = 2 * GH * GDK + GH * GDV

        @block.sync
        def _(sp):
            with nc.allow_non_contiguous_dma(reason="sixteen columns of w_in"):
                sp.dma_start(w_lr[1][:, :, :], a["gla_w_in"][0][:, a_col:a_col + RANK]
                             .rearrange("(k p) n -> p k n", p=P)).then_inc(small_loaded, 16)
            sp.dma_start(w_gate, a["gla_w_gate"][0]).then_inc(small_loaded, 16)
            for b in (4, 5):
                m.ring.issue(sp, 2 * b + 3)
                for t in range(TT):
                    n = (b - 4) * TT + t
                    sp.wait_ge(staged, n + 1)
                    sp.dma_start(m.r_dram[t * P:(t + 1) * P, (b - 4) * HALF:(b - 3) * HALF], stage[:, n % 4, :])\
                        .then_inc(stored[n % 4], 16)
                m.ring.issue(sp, 2 * b + 4)
            for s in range(4):
                sp.wait_ge(stored[s], 16 * 4)

        @block.tensor
        def _(pe):
            pe.wait_ge(lr_split, 1)
            for half in range(2):
                for k in range(KT):
                    for i, j in ((0, 0), (0, 1), (1, 0)):
                        last = pe.matmul(ps_lr[0:RANK, half, :], R(w_lr[i][:, k, :]), R(acts[j](k)[:, half * HALF:(half + 1) * HALF]),
                                         start=(k == i == j == 0), stop=(k == KT - 1 and i == 1))
            last.then_inc(lr_ready, 1)
            pe.wait_ge(small_loaded, 32)
            pe.wait_ge(lr_sb, 1)
            for n in range(2 * GH):
                if n >= 2:
                    pe.wait_ge(gate_free, n - 1)
                pe.matmul(ps_lr[:, n % 2, :], w_gate[:, (n // 2) * P:(n // 2 + 1) * P],
                          lrT[:, (n % 2) * HALF:(n % 2 + 1) * HALF], start=True, stop=True).then_inc(gate_ready, 1)
            pe.wait_ge(gate_free, 2 * GH)
            for first, tokens in ((0, False), (2, True)):
                with pe.Fori(0, 2 if first == 0 else 4) as i:
                    gemm(pe, m, acts, lambda h: pe.wait_ge(m.ring.split, i * 2 + (2 * first + h + 1)), i * 8 + 8 * first,
                         ps, ps_ready, ps_free, tokens)

        @block.vector
        def _(dve):
            dve.wait_ge(lr_high, 1)
            dve.tensor_tensor(R(w_lr[1][:, :, :]), w_lr[1][:, :, :], rounded(w_lr[0][:, :, :]), ALU.subtract).then_inc(lr_split, 1)
            for i in range(2):
                m.ring.make_low(dve, i)
            dve.wait_ge(lr_ready, 1)
            dve.tensor_copy(lrT[:, :].rearrange("p (h n) -> p h n", h=2), ps_lr[0:RANK, :, :]).then_inc(lr_sb, 1)
            row = VEC["gla_b_gate"][0]
            for n in range(2 * GH):
                dve.wait_ge(gate_ready, n + 1)
                dve.tensor_scalar(gates[:, n // 2, (n % 2) * HALF:(n % 2 + 1) * HALF], ps_lr[:, n % 2, :],
                                  m.cols[:, row + n // 2:row + n // 2 + 1], None, ALU.add).then_inc(gate_free, 1)
            dve.drain()
            dve.tensor_scalar(mag[:, :, :], gates[:, :, :], -1.0, None, ALU.mult)
            dve.drain()
            dve.tensor_tensor(mag[:, :, :], mag[:, :, :], gates[:, :, :], ALU.max).then_inc(biased, 1)
            dve.wait_ge(logged, 1)
            dve.tensor_scalar(gates[:, :, :], gates[:, :, :], 0.0, None, ALU.min)
            dve.drain()
            dve.tensor_tensor(gates[:, :, :], gates[:, :, :], mag[:, :, :], ALU.subtract)
            dve.drain()
            dve.tensor_scalar(mag[:, :, :], gates[:, :, :], 1.0 / TAU, None, ALU.mult)
            dve.drain()
            for h in range(GH):
                dve.tensor_tensor_scan(gates[:, h, :], m.resets[:, :], mag[:, h, :], 0.0, ALU.mult, ALU.add)\
                    .then_inc(scanned, 1)
            for i in range(2, 12):
                m.ring.make_low(dve, i)

        @block.scalar
        def _(act):
            act.wait_ge(small_loaded, 32)
            act.activation(R(w_lr[0][:, :, :]), w_lr[1][:, :, :], ACT.Copy).then_inc(lr_high, 1)
            act.sem_inc(ps_free, 8)

            def magnitudes():
                act.wait_ge(biased, 1)
                act.activation(mag[:, :, :], mag[:, :, :], ACT.Exp, scale=-1.0)
                act.drain()
                act.activation(mag[:, :, :], mag[:, :, :], ACT.Ln, bias=1.0).then_inc(logged, 1)

            def evacuate(n, last):
                act.wait_ge(ps_ready, n + 1)
                if last:
                    m.ring.release(act)
                src, t, cols = ps[:, n % 8, :], n % 8, slice((n // 8 % 2) * HALF, (n // 8 % 2 + 1) * HALF)
                if n < 16:
                    out = qk[:, n // 2, (n % 2) * HALF:(n % 2 + 1) * HALF]
                    if n // 2 < GH:
                        act.mul(out, src, float(GDK) ** -0.5).then_inc(ps_free, 1)
                    else:
                        act.copy(out, src).then_inc(ps_free, 1)
                elif n < 32:
                    if n == 16:
                        act.wait_ge(scanned, GH)
                    act.copy(v[:, t, cols], src).then_inc(ps_free, 1)
                else:
                    store_stage(act, stored, n - 32)
                    act.copy(stage[:, n % 4, :], src)
                    act.drain()
                    act.sem_inc(staged, 1)
                    act.sem_inc(ps_free, 1)

            evacuate_split(act, m, (0, 6), evacuate, magnitudes)


def gla_chunks(nc, m, a):
    qk, v, gates = m.b2, m.b3, m.gates
    with ExitStack() as ctx:
        sem = lambda n: nc.alloc_semaphore(fresh(n))
        sb = lambda n, s, d=F32: ctx.enter_context(nc.sbuf_tensor(n, s, d))
        W = GH * P
        part = lambda buf, i: buf[:, i // 2, (i % 2) * W:(i % 2 + 1) * W].rearrange("p (h n) -> p h n", h=GH)
        diff = [part(m.b1, s) for s in range(2)]
        e = {n: part(m.b1, 2 + i) for i, n in enumerate(("up", "down", "full", "left"))}
        scaled_qk = [[part(buf, 6 + i) for i in range(4)] for buf in (m.b1, m.b4)]
        v_now = [m.b1[:, 5, :], m.b4[:, 5, :]]
        decay = [sb(f"chunk_decay{s}", [P, GH, 2]) for s in range(2)]
        att = sb("att", [P, GH, P])
        kst = sb("k_state_tokens", [P, GH, P])
        S = sb("state", [P, GH, GDV])
        S_mid = sb("state_mid", [P, GH, GDV])
        psA = ctx.enter_context(nc.psum_tensor("ps_att", [P, 2, HALF], F32))
        psO = ctx.enter_context(nc.psum_tensor("ps_o", [P, 2, HALF], F32))
        psU = ctx.enter_context(nc.psum_tensor("ps_update", [P, 2, 2, HALF], F32))
        diffs, exps, scaled, v_copied = sem("diffs"), sem("exps"), sem("scaled"), sem("v_copied")
        att_ready, att_masked, kst_sb = sem("att_ready"), sem("att_masked"), sem("kst_sb")
        upd_ready, mid_ready, state_ready = sem("update_ready"), sem("mid_state"), sem("state_ready")
        o_ready, o_copied = sem("o_ready"), sem("o_copied")
        block = ctx.enter_context(nc.Block())
        PAIR = 2 * GH

        def over_units(engine, step):
            with engine.Fori(0, TT // 2 - 1) as i:
                for j in range(PAIR):
                    step(i, j, False)
            for j in range(PAIR):
                step(TT // 2 - 1, j, True)

        @block.vector
        def _(dve):
            dve.memset(S[:, :, :], 0.0).then_inc(state_ready, GH)
            dve.memset(S_mid[:, :, :], 0.0)
            dve.drain()

            def differences(p):
                g4 = gates[:, :, bass.ds(p * P, P)].rearrange("p h (c n) -> p h c n", c=2)
                d0, d1 = (diff[i].rearrange("p h (c n) -> p h c n", c=2) for i in range(2))
                for h in range(GH):
                    mid = g4[:, h, :, CH // 2:CH // 2 + 1].to_broadcast([P, 2, CH])
                    end = g4[:, h, :, CH - 1:CH].to_broadcast([P, 2, CH])
                    dve.tensor_tensor(d0[:, h], g4[:, h], mid, ALU.subtract)
                    last = dve.tensor_tensor(d1[:, h], end, g4[:, h], ALU.subtract)
                last.then_inc(diffs, 1)

            def scale(p, s):
                now = lambda c0: qk[:, c0:c0 + GH, bass.ds(p * P, P)]
                dve.wait_ge(exps, p + 1)
                for i, (c0, name) in enumerate(((0, "up"), (GH, "down"), (0, "full"), (GH, "left"))):
                    last = dve.tensor_tensor(scaled_qk[s][i], now(c0), e[name], ALU.mult)
                last.then_inc(scaled, 1)

            def mask(i, j):
                h = j % GH
                dve.wait_ge(att_ready, i * PAIR + (j + 1))
                dve.tensor_tensor(att[:, h, :], psA[:, j % 2, 0:P], m.upto[:, :], ALU.mult).then_inc(att_masked, 1)
                dve.tensor_copy(kst[:, h, :], psA[:, j % 2, P:2 * P]).then_inc(kst_sb, 1)

            def middle(i, j):
                h = j % GH
                dve.wait_ge(upd_ready, i * PAIR + (j + 1))
                dve.scalar_tensor_tensor(S_mid[:, h, :], S[:, h, :], decay[j // GH % 2][:, h, 0:1], psU[:, j % 2, 0, 0:GDV],
                                         ALU.mult, ALU.add).then_inc(mid_ready, 1)

            differences(0)
            scale(0, 0)
            mask(0, 0)
            mask(0, 1)
            middle(0, 0)

            def step(i, j, tail):
                h, s = j % GH, j // GH
                if not (tail and j + 2 >= PAIR):
                    mask(i, j + 2)
                if not (tail and j + 1 >= PAIR):
                    middle(i, j + 1)
                dve.drain()
                dve.wait_ge(o_ready, i * PAIR + (j + 1))
                dve.scalar_tensor_tensor(S[:, h, :], S_mid[:, h, :], decay[s][:, h, 1:2],
                                         psU[:, j % 2, 1, 0:GDV], ALU.mult, ALU.add).then_inc(state_ready, 1)
                if not (tail and s == 1):
                    if h == 0:
                        differences(i * 2 + (s + 1))
                    if h == 1:
                        scale(i * 2 + (s + 1), 1 - s)
            over_units(dve, step)

        @block.scalar
        def _(act):
            act.sem_inc(o_copied, 2)

            def exponentials(p, s):
                act.wait_ge(diffs, p + 1)
                act.activation(e["up"], diff[0], ACT.Exp)
                act.activation(e["down"], diff[0], ACT.Exp, scale=-1.0)
                g_now = gates[:, :, bass.ds(p * P, P)]
                act.activation(e["full"], g_now, ACT.Exp)
                act.activation(e["left"], diff[1], ACT.Exp)
                act.activation(decay[s][:, :, :],
                               g_now.rearrange("p h (c n) -> p h c n", c=2)[:, :, :, CH - 1], ACT.Exp).then_inc(exps, 1)

            exponentials(0, 0)
            act.copy(v_now[0], v[:, 0, :]).then_inc(v_copied, 1)

            def step(i, j, tail):
                h, s = j % GH, j // GH
                act.wait_ge(o_ready, i * PAIR + (j + 1))
                carry(act, m)
                act.activation(v[:, i * 2 + s, h * GDV:(h + 1) * GDV], psO[:, j % 2, 0:GDV], ACT.Copy).then_inc(o_copied, 1)
                if not (tail and s == 1):
                    if h == 0:
                        exponentials(i * 2 + (s + 1), 1 - s)
                    if h == 1:
                        act.activation(v_now[1 - s], v[:, i * 2 + (s + 1), :], ACT.Copy).then_inc(v_copied, 1)
            over_units(act, step)

        @block.tensor
        def _(pe):
            def attend(i, j):
                s, h = j // GH % 2, j % GH
                qi, ki, qn, ks = (scaled_qk[s][x] for x in (0, 1, 2, 3))
                if h == 0:
                    pe.wait_ge(scaled, i * 2 + (j // GH + 1))
                pe.matmul(psA[:, j % 2, 0:P], ki[:, h, :], qi[:, h, :], start=True, stop=True)
                pe.transpose(psA[:, j % 2, P:2 * P], ks[:, h, :], m.ident[:, :]).then_inc(att_ready, 1)

            def update(i, j):
                s, h = j // GH % 2, j % GH
                if h == 0:
                    pe.wait_ge(v_copied, i * 2 + (j // GH + 1))
                pe.wait_ge(kst_sb, i * PAIR + (j + 1))
                pe.wait_ge(att_masked, i * PAIR + (j + 1))
                pe.wait_ge(state_ready, i * PAIR + (j + GH - 1))
                for c in range(2):
                    last = pe.matmul(psU[:, j % 2, c, 0:GDV], kst[c * CH:(c + 1) * CH, h, :],
                                     v_now[s][c * CH:(c + 1) * CH, h * GDV:(h + 1) * GDV], start=True, stop=True)
                last.then_inc(upd_ready, 1)

            attend(0, 0)
            attend(0, 1)
            update(0, 0)

            def step(i, j, tail):
                s, h = j // GH, j % GH
                if not (tail and j + 2 >= PAIR):
                    attend(i, j + 2)
                if not (tail and j + 1 >= PAIR):
                    update(i, j + 1)
                pe.wait_ge(o_copied, i * PAIR + (j + 1))
                pe.wait_ge(state_ready, i * PAIR + (j + 1))
                for c, state in enumerate((S, S_mid)):
                    part = slice(c * CH, (c + 1) * CH)
                    pe.matmul(psO[part, j % 2, 0:GDV], att[:, h, part], v_now[s][:, h * GDV:(h + 1) * GDV], start=True, stop=False)
                    if c == 1:
                        pe.wait_ge(mid_ready, i * PAIR + (j + 1))
                    last = pe.matmul(psO[part, j % 2, 0:GDV], scaled_qk[s][2][:, h, part], state[:, h, :], start=False, stop=True)
                last.then_inc(o_ready, 1)
            over_units(pe, step)


def gla_output(nc, m, a):
    o, r, yT = m.b3, m.b4, (by_tile(m.b1), by_tile(m.b2))
    with ExitStack() as ctx:
        sem = lambda n: nc.alloc_semaphore(fresh(n))
        sb = lambda n, s, d=F32: ctx.enter_context(nc.sbuf_tensor(n, s, d))
        ss, root, inv = sb("o_ss", [P, TT * GH]), sb("o_root", [P, TT * GH]), sb("o_inv", [P, TT * GH])
        junk = sb("o_squares", [P, 2, GDV])
        squared = [(o[:, t, h * GDV:(h + 1) * GDV], ss[:, t * GH + h:t * GH + h + 1]) for t in range(TT) for h in range(GH)]
        row = VEC["gla_out_norm"][0]
        gain = lambda k: m.cols[:, row + k % (GDV // P):row + k % (GDV // P) + 1]
        ps = ctx.enter_context(nc.psum_tensor("ps_yT", [P, 4, HALF], F32))
        summed, squares, roots, gated = (sem(n) for n in ("o_summed", "o_meaned", "o_rooted", "gated"))
        normed, ps_ready, ps_free, high_made = sem("o_normed"), sem("yT_ready"), sem("yT_free"), sem("yT_high")
        r_arrived = [sem(f"r_arrived{t}") for t in range(TT)]
        block = ctx.enter_context(nc.Block())

        @block.sync
        def _(sp):
            for t in range(TT):
                sp.dma_start(r[:, t, :], m.r_dram[t * P:(t + 1) * P, :]).then_inc(r_arrived[t], 16)

        @block.scalar
        def _(act):
            sum_squares(act, None, squared, junk, summed)
            inverse_rms(act, None, ss[:, :], root[:, :], None, GDV, squares, roots)
            for t in range(TT):
                act.wait_ge(r_arrived[t], 16)
                act.activation(r[:, t, :], r[:, t, :], ACT.Silu).then_inc(gated, 1)
            high_from_banks(act, yT[0], gain, ps, ps_ready, high_made)

        @block.vector
        def _(dve):
            sum_squares(None, dve, squared, junk, summed)
            dve.wait_ge(summed, TT * GH)
            dve.tensor_scalar(ss[:, :], ss[:, :], 1.0 / GDV, EPS, ALU.mult, ALU.add).then_inc(squares, 1)
            inverse_rms(None, dve, None, root[:, :], inv[:, :], GDV, squares, roots)
            for t in range(TT):
                dve.wait_ge(gated, t + 1)
                for h in range(GH):
                    cols = slice(h * GDV, (h + 1) * GDV)
                    ins = dve.scalar_tensor_tensor(o[:, t, cols], o[:, t, cols], inv[:, t * GH + h:t * GH + h + 1], r[:, t, cols],
                                                   ALU.mult, ALU.mult)
                ins.then_inc(normed, 1)
            low_from_banks(dve, yT[0], yT[1], gain, ps, ps_free, high_made)

        @block.tensor
        def _(pe):
            transposes(pe, m, o, lambda e: e.wait_ge(normed, TT), ps, ps_ready, ps_free)


def project_back(nc, m, acts, resid, resid_src, first, ahead, gate=None):
    with ExitStack() as ctx:
        sem = lambda n: nc.alloc_semaphore(fresh(n))
        ps = ctx.enter_context(nc.psum_tensor(fresh("ps_back"), [P, 8, HALF], F32))
        got = ctx.enter_context(nc.sbuf_tensor(fresh("product"), [P, 4, HALF], F32))
        arrived = [sem(f"resid{t}") for t in range(TT)]
        ps_ready, ps_free, got_sb, added = sem("back_ready"), sem("back_free"), sem("product_in_sbuf"), sem("back_added")
        block = ctx.enter_context(nc.Block())

        @block.sync
        def _(sp):
            for t in range(TT):
                sp.dma_start(resid[:, t, :], resid_src[t * P:(t + 1) * P, :]).then_inc(arrived[t], 16)
            m.ring.issue(sp, 2 * first + 4 + ahead)

        @block.tensor
        def _(pe):
            with pe.Fori(0, 2) as i:
                gemm(pe, m, acts, lambda h: pe.wait_ge(m.ring.split, i * 2 + (2 * first + h + 1)), i * 8,
                     ps, ps_ready, ps_free, True)

        @block.scalar
        def _(act):
            act.sem_inc(ps_free, 8)

            def evacuate(n, last):
                act.wait_ge(ps_ready, n + 1)
                if last:
                    m.ring.release(act)
                if n >= 4:
                    act.wait_ge(added, n - 3)
                act.copy(got[:, n % 4, :], ps[:, n % 8, :])
                act.drain()
                act.sem_inc(got_sb, 1)
                act.sem_inc(ps_free, 1)

            evacuate_split(act, m, (first, first + 2), evacuate)

        @block.vector
        def _(dve):
            for i in range(2):
                m.ring.make_low(dve, 2 * first + i)
            for n in range(2 * TT):
                t, cols, x = n % TT, slice((n // TT) * HALF, (n // TT + 1) * HALF), got[:, n % 4, :]
                if n < TT:
                    dve.wait_ge(arrived[t], 16)
                dve.wait_ge(got_sb, n + 1)
                if gate is not None:
                    dve.tensor_tensor(x, x, gate[:, cols], ALU.mult)
                    dve.drain()
                dve.tensor_tensor(resid[:, t, cols], x, resid[:, t, cols], ALU.add).then_inc(added, 1)
                if n == 4:
                    m.ring.make_low(dve, 2 * first + 2)
                if n == 7:
                    m.ring.make_low(dve, 2 * first + 3)



UNROLL = 4


def load_expert(sp, m, a, e, u):
    for i, w in enumerate(("moe_w1", "moe_w3")):
        sp.dma_start(m.w13[u][:, i], a[w][0, e].rearrange("(k p) n -> p k n", p=P)).then_inc(m.w13_loaded[u], 16)
    sp.dma_start(m.w2[u], a["moe_w2"][0, e].rearrange("(k p) n -> p k n", p=P)).then_inc(m.w2_loaded[u], 16)


def router(nc, m, a):
    hT = m.b1
    NL = GROUPS + EXPERTS
    with ExitStack() as ctx:
        sem = lambda n: nc.alloc_semaphore(fresh(n))
        sb = lambda n, s, d=F32: ctx.enter_context(nc.sbuf_tensor(n, s, d))
        w = sb("w_router", [P, KT, NL])
        lg = sb("logits", [P, TT, NL])
        gmx, emx = sb("group_max", [P, TT, 8]), sb("expert_max", [P, TT, 8])
        gix, eix = sb("group_index", [P, TT, 8], U32), sb("expert_index", [P, TT, 8], U32)
        gid, eid = sb("group_id", [P, TT]), sb("expert_id", [P, 2, TT])
        in_group = sb("in_group", [P, TT, GROUPS])
        prod = sb("selected", [P, TT, GROUPS, PER_GROUP])
        el = sb("group_logits", [P, TT, PER_GROUP])
        gexp, gsum, ez, den = sb("group_exp", [P, TT, GROUPS]), sb("group_sum", [P, TT]), sb("second_exp", [P, TT]), sb("pair_sum", [P, TT])
        one = [sb(f"one_hot{k}", [P, TT, EXPERTS]) for k in range(2)]
        both = sb("assigned", [P, TT, EXPERTS])
        rank, dest = sb("rank", [P, 2, TT]), sb("slot_row", [P, 2 * TT], I32)
        cnt, extra, cum = sb("counts", [P, EXPERTS]), sb("extra_blocks", [P, EXPERTS]), sb("extra_cum", [P, EXPERTS])
        le, per_part, info_i = sb("passed", [P, EXPERTS]), sb("block_info", [P, 4]), sb("block_info_i", [P, 2], I32)
        ps = ctx.enter_context(nc.psum_tensor("ps_logits", [P, 2, HALF], F32))
        psp = ctx.enter_context(nc.psum_tensor("ps_rank", [P, TT, EXPERTS], F32))
        psc = ctx.enter_context(nc.psum_tensor("ps_counts", [P, EXPERTS], F32))
        w_arrived, logits_ready, shifted, exped = sem("router_w"), sem("logits_ready"), sem("shifted"), sem("exped")
        assigned, ranked, placed, scattered, tables = sem("assigned_s"), sem("ranked"), sem("placed"), sem("codes_scattered"), sem("tables")
        listed, info_stored, diffed = sem("listed"), sem("info_stored"), sem("diffed")
        block = ctx.enter_context(nc.Block())

        @block.sync
        def _(sp):
            sp.dma_start(w[:, :, 0:GROUPS], a["moe_w_group"][0].rearrange("(k p) n -> p k n", p=P)).then_inc(w_arrived, 16)
            sp.dma_start(w[:, :, GROUPS:NL], a["moe_w_expert"][0].rearrange("(k p) n -> p k n", p=P)).then_inc(w_arrived, 16)
            for e in range(2):
                load_expert(sp, m, a, e, e)
            sp.wait_ge(scattered, 16 * 2 * TT)
            sp.dma_start(m.scatter_idx[:, :], m.codes[0:SLOTS * EXPERTS, :].rearrange("(s e) o -> s (e o)", s=SLOTS))\
                .then_inc(tables, 16)
            sp.wait_ge(listed, 1)
            sp.dma_start(m.info_dram, info_i[:, :]).then_inc(info_stored, 16)
            sp.wait_ge(info_stored, 16)
            sp.dma_start(m.info_row[:, :], m.info_dram.rearrange("(o p) c -> o (p c)", o=1)).then_inc(info_stored, 16)
            sp.wait_ge(info_stored, 32)

        @block.tensor
        def _(pe):
            pe.wait_ge(w_arrived, 32)
            for t in range(TT):
                for k in range(KT):
                    last = pe.matmul(ps[:, t // 4, (t % 4) * NL:(t % 4 + 1) * NL], hT[:, k, t * P:(t + 1) * P], w[:, k, :],
                                     start=(k == 0), stop=(k == KT - 1))
            last.then_inc(logits_ready, 1)
            pe.wait_ge(assigned, 1)
            for t in range(TT):
                for s in range(t):
                    pe.matmul(psp[:, t, :], m.ones[:, :], both[:, s, :], start=(s == 0), stop=False)
                pe.matmul(psp[:, t, :], m.before[:, :], both[:, t, :], start=(t == 0), stop=True)
            for t in range(TT):
                last = pe.matmul(psc[:, :], m.ones[:, :], both[:, t, :], start=(t == 0), stop=(t == TT - 1))
            last.then_inc(ranked, 1)

        @block.scalar
        def _(act):
            act.wait_ge(shifted, 1)
            act.activation(gexp[:, :, :], gexp[:, :, :], ACT.Exp).then_inc(exped, 1)
            act.wait_ge(diffed, 1)
            act.activation(ez[:, :], ez[:, :], ACT.Exp).then_inc(exped, 1)

        @block.vector
        def _(dve):
            dve.wait_ge(logits_ready, 1)
            for h in range(2):
                dve.tensor_copy(lg[:, 4 * h:4 * h + 4, :], ps[:, h, 0:4 * NL].rearrange("p (t n) -> p t n", t=4))
            dve.drain()
            for t in range(TT):
                dve.max(gmx[:, t, :], lg[:, t, 0:GROUPS])
            dve.drain()
            for t in range(TT):
                dve.max_index(gix[:, t, :], gmx[:, t, :], lg[:, t, 0:GROUPS])
            dve.tensor_tensor(gexp[:, :, :], lg[:, :, 0:GROUPS], gmx[:, :, 0:1].to_broadcast([P, TT, GROUPS]),
                              ALU.subtract).then_inc(shifted, 1)
            dve.drain()
            dve.tensor_copy(gid[:, :], gix[:, :, 0])
            dve.drain()
            dve.tensor_tensor(in_group[:, :, :], m.expert_iota[:, None, 0:GROUPS].to_broadcast([P, TT, GROUPS]),
                              gid[:, :, None].to_broadcast([P, TT, GROUPS]), ALU.is_equal)
            dve.drain()
            dve.tensor_tensor(prod[:, :, :, :], lg[:, :, GROUPS:NL].rearrange("p t (g e) -> p t g e", g=GROUPS),
                              in_group[:, :, :, None].to_broadcast([P, TT, GROUPS, PER_GROUP]), ALU.mult)
            dve.drain()
            dve.reduce_sum(el[:, :, :], prod[:, :, :, :].rearrange("p t g e -> p t e g"), axis=AX.X)
            dve.drain()
            for t in range(TT):
                dve.max(emx[:, t, :], el[:, t, :])
            dve.drain()
            for t in range(TT):
                dve.max_index(eix[:, t, :], emx[:, t, :], el[:, t, :])
            dve.tensor_tensor(ez[:, :], emx[:, :, 1], emx[:, :, 0], ALU.subtract).then_inc(diffed, 1)
            dve.drain()
            for k in range(2):
                dve.tensor_copy(eid[:, k, :], eix[:, :, k])
            dve.drain()
            for k in range(2):
                dve.scalar_tensor_tensor(eid[:, k, :], gid[:, :], float(PER_GROUP), eid[:, k, :], ALU.mult, ALU.add)
            dve.drain()
            for k in range(2):
                dve.tensor_tensor(one[k][:, :, :], m.expert_iota[:, None, :].to_broadcast([P, TT, EXPERTS]),
                                  eid[:, k, :, None].to_broadcast([P, TT, EXPERTS]), ALU.is_equal)
            dve.drain()
            dve.tensor_tensor(both[:, :, :], one[0][:, :, :], one[1][:, :, :], ALU.add).then_inc(assigned, 1)
            dve.wait_ge(exped, 2)
            dve.reduce_sum(gsum[:, :], gexp[:, :, :], axis=AX.X)
            dve.tensor_scalar(den[:, :], ez[:, :], 1.0, None, ALU.add)
            dve.drain()
            dve.tensor_tensor(den[:, :], den[:, :], gsum[:, :], ALU.mult)
            dve.drain()
            dve.reciprocal(m.gates2[:, 0, :], den[:, :])
            dve.drain()
            dve.tensor_tensor(m.gates2[:, 1, :], m.gates2[:, 0, :], ez[:, :], ALU.mult)
            dve.wait_ge(ranked, 1)
            for k in range(2):
                dve.tensor_tensor(one[k][:, :, :], psp[:, :, :], one[k][:, :, :], ALU.mult)
            dve.drain()
            for k in range(2):
                dve.reduce_sum(rank[:, k, :], one[k][:, :, :], axis=AX.X)
            dve.drain()
            dve.scalar_tensor_tensor(dest[:, :].rearrange("p (k t) -> p k t", k=2), rank[:, :, :], float(EXPERTS),
                                     eid[:, :, :], ALU.mult, ALU.add).then_inc(placed, 1)
            dve.tensor_copy(cnt[:, :], psc[:, :])
            dve.memset(extra[:, :], 0.0)
            dve.drain()
            for j in range(1, T // SLOTS):
                dve.scalar_tensor_tensor(extra[:, :], cnt[:, :], float(SLOTS * j), extra[:, :], ALU.is_gt, ALU.add)
                dve.drain()
            dve.tensor_tensor_scan(cum[:, :], m.ones[:, 0:EXPERTS], extra[:, :], 0.0, ALU.mult, ALU.add)
            dve.drain()
            dve.tensor_scalar(le[:, :], cum[:, :], m.part_iota[:, 0:1], None, ALU.is_le)
            dve.tensor_copy(m.n_extra[:, :], cum[0:1, EXPERTS - 1:EXPERTS])
            dve.drain()
            dve.reduce_sum(per_part[:, 0:1], le[:, :], axis=AX.X)
            dve.tensor_tensor(extra[:, :], extra[:, :], le[:, :], ALU.mult)
            dve.drain()
            dve.reduce_sum(per_part[:, 1:2], extra[:, :], axis=AX.X)
            dve.drain()
            dve.tensor_tensor(per_part[:, 2:3], m.part_iota[:, 0:1], per_part[:, 1:2], ALU.subtract)
            dve.drain()
            dve.tensor_scalar(per_part[:, 3:4], per_part[:, 2:3], 1.0, float(SLOTS * EXPERTS), ALU.add, ALU.mult)
            dve.drain()
            dve.tensor_tensor(info_i[:, 1:2], per_part[:, 3:4], per_part[:, 0:1], ALU.add)
            dve.tensor_copy(info_i[:, 0:1], per_part[:, 0:1]).then_inc(listed, 1)
            dve.wait_ge(tables, 16)
            code_tokens(dve, m.gather_idx[:, :], m.scatter_idx[:, :])

        @block.gpsimd
        def _(pool):
            pool.wait_ge(placed, 1)
            for n in range(2 * TT):
                pool.indirect_dma_start(m.codes, bass.IndirectOffsetOnAxis(dest[:, n:n + 1], 0), m.codes_i[:, n:n + 1],
                                        None).then_inc(scattered, 16)


def code_tokens(dve, tokens, codes):
    dve.tensor_scalar(tokens, codes, float(T), -float(T), ALU.is_ge, ALU.mult)
    dve.drain()
    dve.tensor_tensor(tokens, tokens, codes, ALU.add)
    dve.drain()


class ExpertBuffers:

    def __init__(self, nc, ctx):
        sb = lambda n, s, d=F32: ctx.enter_context(nc.sbuf_tensor(fresh(n), s, d))
        self.xg = [sb("gathered", [SLOTS, D]) for _ in range(2)]
        self.y = [sb("expert_out", [SLOTS, D]) for _ in range(2)]
        self.xT = [sb("gatheredT", [P, KT, SLOTS]) for _ in range(2)]
        self.sil = [sb("silu", [P, 2, SLOTS]) for _ in range(2)]
        self.hid = [sb("hidden", [P, 2, SLOTS]) for _ in range(2)]
        self.gi = [sb("gather_now", [SLOTS, 1], I32) for _ in range(2)]
        self.si = [sb("scatter_now", [SLOTS, 1], I32) for _ in range(2)]
        pb = lambda n, s: ctx.enter_context(nc.psum_tensor(fresh(n), s, F32))
        self.psT, self.psH, self.psY = pb("ps_xT", [P, 2, HALF]), pb("ps_hid", [P, 2, HALF]), pb("ps_y", [P, 2, 2, HALF])


def expert_turn(pe, m, B, s):
    for k in range(KT):
        last = pe.transpose(B.psT[:, s, k * SLOTS:(k + 1) * SLOTS], B.xg[s][:, k * P:(k + 1) * P],
                            m.ident[0:SLOTS, 0:SLOTS])
    return last


def expert_up(pe, m, B, s, u):
    for f in range(4):
        for k in range(KT):
            last = pe.matmul(B.psH[:, s, f * SLOTS:(f + 1) * SLOTS], m.w13[u][:, f // 2, k, (f % 2) * P:(f % 2 + 1) * P],
                             B.xT[s][:, k, :], start=(k == 0), stop=(k == KT - 1))
    return last


def expert_down(pe, m, B, s, u):
    for h in range(2):
        for f in range(2):
            last = pe.matmul(B.psY[0:SLOTS, s, h, :], B.hid[s][:, f, :], m.w2[u][:, f, h * HALF:(h + 1) * HALF],
                             start=(f == 0), stop=(f == 1))
    return last


def expert_xT(dve, m, B, s):
    row = VEC["ffn_norm"][0]
    return dve.tensor_tensor(B.xT[s][:, :, :], B.psT[:, s, :].rearrange("p (k n) -> p k n", k=KT),
                             m.cols[:, row:row + KT, None].to_broadcast([P, KT, SLOTS]), ALU.mult)


def expert_silu(act, B, s):
    return act.activation(B.sil[s][:, :, :], B.psH[:, s, 0:2 * SLOTS].rearrange("p (f n) -> p f n", f=2), ACT.Silu)


def expert_hidden(dve, B, s):
    return dve.tensor_tensor(B.hid[s][:, :, :], B.psH[:, s, 2 * SLOTS:4 * SLOTS].rearrange("p (f n) -> p f n", f=2),
                             B.sil[s][:, :, :], ALU.mult)


def gather_tokens(pool, m, B, s):
    return pool.indirect_dma_start(B.xg[s][:, :], None, m.xn_dram, bass.IndirectOffsetOnAxis(B.gi[s][:, 0:1], 0),
                                   bounds_check=T - 1, oob_is_err=False)


def scatter_tokens(pool, m, B, s):
    return pool.indirect_dma_start(m.contrib, bass.IndirectOffsetOnAxis(B.si[s][:, 0:1], 0), B.y[s][:, :], None,
                                   bounds_check=2 * T - 1, oob_is_err=False)


def experts(nc, m, a):
    with ExitStack() as ctx:
        sem = lambda n: nc.alloc_semaphore(fresh(n))
        B = ExpertBuffers(nc, ctx)
        gathered = [sem(f"gathered{s}") for s in range(2)]
        scattered = [sem(f"scattered{s}") for s in range(2)]
        gi_ready, turned, xT_sb, up_done, silu_done, hid_done, down_done = (
            sem(n) for n in ("gather_index", "turned", "xT_in_sbuf", "up_done", "silu_done", "hid_done", "down_done"))
        y_sb = [sem(f"y_half{h}_in_sbuf") for h in range(2)]
        block = ctx.enter_context(nc.Block())
        ITERS = EXPERTS // UNROLL

        @block.sync
        def _(sp):
            for e in range(2, UNROLL):
                load_expert(sp, m, a, e, e)
            with sp.Fori(0, ITERS - 1) as i:
                for u in range(UNROLL):
                    e = i * UNROLL + (UNROLL + u)
                    sp.wait_ge(up_done, i * UNROLL + (u + 1))
                    for j, w in enumerate(("moe_w1", "moe_w3")):
                        sp.dma_start(m.w13[u][:, j], a[w][0, e].rearrange("(k p) n -> p k n", p=P)).then_inc(m.w13_loaded[u], 16)
                    sp.wait_ge(down_done, i * UNROLL + (u + 1))
                    sp.dma_start(m.w2[u], a["moe_w2"][0, e].rearrange("(k p) n -> p k n", p=P)).then_inc(m.w2_loaded[u], 16)

        def over_experts(engine, step):
            for u in range(UNROLL):
                step(u, 0, u, False)
            with engine.Fori(1, ITERS - 1) as i:
                for u in range(UNROLL):
                    step(i * UNROLL + u, i, u, False)
            for u in range(UNROLL):
                step((ITERS - 1) * UNROLL + u, ITERS - 1, u, True)

        def out_is_stored(engine, i, u):
            before = i * 2 + u // 2
            if not isinstance(before, int) or before > 0:
                engine.wait_ge(scattered[u % 2], before * 16)

        @block.gpsimd
        def _(pool):
            for s in range(2):
                pool.memset(B.xg[s][:, :], 0.0)
            pool.drain()
            for e in range(2):
                pool.wait_ge(gi_ready, e + 1)
                gather_tokens(pool, m, B, e).then_inc(gathered[e], 16)

            def step(e, i, u, tail):
                s = u % 2
                if not (tail and u >= UNROLL - 2):
                    pool.wait_ge(gi_ready, e + 3)
                    carry(pool, m)
                    gather_tokens(pool, m, B, s).then_inc(gathered[s], 16)
                pool.wait_ge(y_sb[0], e + 3)
                pool.wait_ge(y_sb[1], e + 3)
                carry(pool, m)
                scatter_tokens(pool, m, B, s).then_inc(scattered[s], 16)

            over_experts(pool, step)
            for s in range(2):
                pool.wait_ge(scattered[s], 16 * (EXPERTS // 2))

        @block.tensor
        def _(pe):
            pe.wait_ge(gathered[0], 16)
            expert_turn(pe, m, B, 0).then_inc(turned, 1)

            def step(e, i, u, tail):
                s = u % 2
                pe.wait_ge(xT_sb, e + 1)
                pe.wait_ge(m.w13_loaded[u], (i + 1) * 32)
                expert_up(pe, m, B, s, u).then_inc(up_done, 1)
                if not (tail and u == UNROLL - 1):
                    pe.wait_ge(gathered[1 - s], (i * 2 + ((u + 1) // 2 + 1)) * 16)
                    carry(pe, m)
                    expert_turn(pe, m, B, 1 - s).then_inc(turned, 1)
                pe.wait_ge(hid_done, e + 1)
                pe.wait_ge(m.w2_loaded[u], (i + 1) * 16)
                for h in range(2):
                    pe.wait_ge(y_sb[h], e + 1)
                expert_down(pe, m, B, s, u).then_inc(down_done, 1)

            over_experts(pe, step)

        @block.scalar
        def _(act):
            act.sem_inc(y_sb[1], 2)
            def step(e, i, u, tail):
                s = u % 2
                act.wait_ge(up_done, e + 1)
                expert_silu(act, B, s).then_inc(silu_done, 1)
                out_is_stored(act, i, u)
                act.wait_ge(down_done, e + 1)
                act.copy(B.y[s][:, HALF:D], B.psY[0:SLOTS, s, 1, :]).then_inc(y_sb[1], 1)

            over_experts(act, step)

        @block.vector
        def _(dve):
            dve.sem_inc(y_sb[0], 2)
            for e in range(2):
                dve.tensor_copy(B.gi[e][:, :], m.gather_idx[:, e:e + 1]).then_inc(gi_ready, 1)
            dve.wait_ge(turned, 1)
            expert_xT(dve, m, B, 0).then_inc(xT_sb, 1)
            dve.tensor_copy(B.gi[0][:, :], m.gather_idx[:, 2:3]).then_inc(gi_ready, 1)

            def step(e, i, u, tail):
                s = u % 2
                dve.wait_ge(silu_done, e + 1)
                expert_hidden(dve, B, s).then_inc(hid_done, 1)
                if not (tail and u == UNROLL - 1):
                    dve.wait_ge(turned, e + 2)
                    expert_xT(dve, m, B, 1 - s).then_inc(xT_sb, 1)
                if not (tail and u >= UNROLL - 3):
                    dve.tensor_copy(B.gi[1 - s][:, :], m.gather_idx[:, col(e + 3)]).then_inc(gi_ready, 1)
                out_is_stored(dve, i, u)
                carry(dve, m)
                dve.tensor_copy(B.si[s][:, :], m.scatter_idx[:, col(e)])
                dve.wait_ge(down_done, e + 1)
                dve.tensor_copy(B.y[s][:, 0:HALF], B.psY[0:SLOTS, s, 0, :])
                dve.drain()
                dve.sem_inc(y_sb[0], 1)

            over_experts(dve, step)


def more_blocks(nc, m, a):
    MOST = 2 * T // SLOTS
    with ExitStack() as ctx:
        sem = lambda n: nc.alloc_semaphore(fresh(n))
        B = ExpertBuffers(nc, ctx)
        weights, indices, tokens, gathered, turned, xT_sb, up_done, silu_done, hid_done, down_done, y_sb, scattered, free = (
            sem("more_" + n) for n in ("weights", "indices", "tokens", "gathered", "turned", "xT", "up", "silu",
                                       "hid", "down", "y", "scattered", "free"))
        block = ctx.enter_context(nc.Block())

        def over_blocks(engine, step):
            n = engine.value_load(m.n_extra[0:1, 0:1], min_val=0, max_val=MOST)
            with engine.If(n > 0):
                with engine.Fori(0, n) as b:
                    step(b)

        @block.sync
        def _(sp):
            def step(b):
                e = sp.value_load(m.info_row[0:1, bass.ds(b * 2, 1)], min_val=0, max_val=EXPERTS - 1)
                row = sp.value_load(m.info_row[0:1, bass.ds(b * 2 + 1, 1)], min_val=0, max_val=(T - SLOTS) * EXPERTS + EXPERTS - 1)
                sp.wait_ge(free, b + 1)
                for j, w in enumerate(("moe_w1", "moe_w3")):
                    sp.dma_start(m.w13[0][:, j], a[w][0, e].rearrange("(k p) n -> p k n", p=P)).then_inc(weights, 16)
                sp.dma_start(m.w2[0], a["moe_w2"][0, e].rearrange("(k p) n -> p k n", p=P)).then_inc(weights, 16)
                sp.dma_start(B.si[0][:, :], m.codes[bass.ds(row, SLOTS, EXPERTS), :])\
                    .then_inc(indices, 16)
            over_blocks(sp, step)

        @block.gpsimd
        def _(pool):
            pool.memset(B.xg[0][:, :], 0.0)
            pool.drain()
            pool.sem_inc(free, 1)
            def step(b):
                pool.wait_ge(tokens, b + 1)
                carry(pool, m)
                gather_tokens(pool, m, B, 0).then_inc(gathered, 16)
                pool.wait_ge(y_sb, b + 1)
                carry(pool, m)
                scatter_tokens(pool, m, B, 0).then_inc(scattered, 16)
                pool.wait_ge(scattered, (b + 1) * 16)
                pool.sem_inc(free, 1)
            over_blocks(pool, step)

        @block.tensor
        def _(pe):
            def step(b):
                pe.wait_ge(gathered, (b + 1) * 16)
                carry(pe, m)
                expert_turn(pe, m, B, 0).then_inc(turned, 1)
                pe.wait_ge(xT_sb, b + 1)
                pe.wait_ge(weights, (b + 1) * 48)
                expert_up(pe, m, B, 0, 0).then_inc(up_done, 1)
                pe.wait_ge(hid_done, b + 1)
                expert_down(pe, m, B, 0, 0).then_inc(down_done, 1)
            over_blocks(pe, step)

        @block.scalar
        def _(act):
            def step(b):
                act.wait_ge(up_done, b + 1)
                expert_silu(act, B, 0).then_inc(silu_done, 1)
            over_blocks(act, step)

        @block.vector
        def _(dve):
            def step(b):
                dve.wait_ge(indices, (b + 1) * 16)
                code_tokens(dve, B.gi[0][:, :], B.si[0][:, :])
                dve.sem_inc(tokens, 1)
                dve.wait_ge(turned, b + 1)
                expert_xT(dve, m, B, 0).then_inc(xT_sb, 1)
                dve.wait_ge(silu_done, b + 1)
                expert_hidden(dve, B, 0).then_inc(hid_done, 1)
                dve.wait_ge(down_done, b + 1)
                dve.tensor_copy(B.y[0][:, :].rearrange("p (h n) -> p h n", h=2), B.psY[0:SLOTS, 0, :, :]).then_inc(y_sb, 1)
            over_blocks(dve, step)


def combine(nc, m, a):
    x = m.b4
    parts = (m.b1, m.b2)
    with ExitStack() as ctx:
        sem = lambda n: nc.alloc_semaphore(fresh(n))
        sb = lambda n, s, d=F32: ctx.enter_context(nc.sbuf_tensor(n, s, d))
        gain = sb("final_norm_wide", [P, D])
        ss, root, inv, junk = sb("x2_ss", [P, TT]), sb("x2_root", [P, TT]), sb("x2_inv", [P, TT]), sb("x2_squares", [P, D])
        arrived = [sem(f"contrib_arrived{t}") for t in range(TT)]
        gain_arrived, added, summed, squares, roots, normed, stored = (
            sem(n) for n in ("final_gain", "contrib_added", "x2_summed", "x2_meaned", "x2_rooted", "x2_normed", "x2_stored"))
        block = ctx.enter_context(nc.Block())

        @block.sync
        def _(sp):
            sp.dma_start(gain[:, :], spread(a["final_norm"].rearrange("(o d) -> o d", o=1))).then_inc(gain_arrived, 16)
            for t in range(TT):
                for k in range(2):
                    sp.dma_start(parts[k][:, t, :], m.contrib[k * T + t * P:k * T + (t + 1) * P, :]).then_inc(arrived[t], 16)
            for t in range(TT):
                sp.wait_ge(normed, t + 1)
                sp.dma_start(m.x2_dram[t * P:(t + 1) * P, :], x[:, t, :]).then_inc(stored, 16)
            sp.wait_ge(stored, 16 * TT)

        @block.vector
        def _(dve):
            for t in range(TT):
                dve.wait_ge(arrived[t], 32)
                for k in range(2):
                    ins = dve.scalar_tensor_tensor(x[:, t, :], parts[k][:, t, :], m.gates2[:, k, t:t + 1], x[:, t, :],
                                                   ALU.mult, ALU.add)
                    if k == 0:
                        dve.drain()
                ins.then_inc(added, 1)
            dve.wait_ge(summed, TT)
            dve.tensor_scalar(ss[:, :], ss[:, :], 1.0 / D, EPS, ALU.mult, ALU.add).then_inc(squares, 1)
            inverse_rms(None, dve, None, root[:, :], inv[:, :], D, squares, roots)
            dve.wait_ge(gain_arrived, 16)
            for t in range(TT):
                dve.scalar_tensor_tensor(x[:, t, :], x[:, t, :], inv[:, t:t + 1], gain[:, :], ALU.mult, ALU.mult)\
                    .then_inc(normed, 1)

        @block.scalar
        def _(act):
            for t in range(TT):
                act.wait_ge(added, t + 1)
                act.activation(junk[:, :], x[:, t, :], ACT.Square, accum_out=ss[:, t:t + 1]).then_inc(summed, 1)
                act.drain()
            inverse_rms(act, None, ss[:, :], root[:, :], None, D, squares, roots)



def mixer_projections(nc, m, a):
    acts = (by_tile(m.b1), by_tile(m.b4))
    raw, qk = m.raw, m.b3
    FIRST = 8
    with ExitStack() as ctx:
        sem = lambda n: nc.alloc_semaphore(fresh(n))
        sb = lambda n, s, d=F32: ctx.enter_context(nc.sbuf_tensor(n, s, d))
        w_dt = [both_kinds(nc, ctx, f"w_dt{i}", [P, KT, SH]) for i in range(2)]
        dt_bias, a_log = sb("dt_bias_wide", [P, SH]), sb("a_log_wide", [P, SH])
        mag = sb("dt_magnitude", [P, TT, SH])
        conv = [sb(f"conv_sum{s}", [P, T]) for s in range(2)]
        stage = sb("zv_stage", [P, 4, HALF])
        ps = ctx.enter_context(nc.psum_tensor("ps_mix_in", [P, 8, HALF], F32))
        psd = ps[:, 7, 0:TT * SH].rearrange("p (t n) -> p t n", t=TT)
        small, dt_ready, dt_read, ps_ready, ps_free = sem("dt_weights"), sem("dt_ready"), sem("dt_read"), sem("mix_ready"), sem("mix_free")
        dt_high, dt_split, staged = sem("dt_high"), sem("dt_split"), sem("zv_staged")
        stored = [sem(f"zv_stored{s}") for s in range(4)]
        dt_mag, dt_log, a_exp, raw_sb, convolved, silued = (
            sem(n) for n in ("dt_mag", "dt_log", "a_exp", "raw_in_sbuf", "convolved", "conv_silu"))
        block = ctx.enter_context(nc.Block())

        @block.sync
        def _(sp):
            at = IN_AT["dt"]
            sp.dma_start(w_dt[1][:, :, :], a["w_in_2"][0][:, at:at + SH].rearrange("(k p) n -> p k n", p=P)).then_inc(small, 16)
            sp.dma_start(dt_bias[:, :], spread(a["dt_bias_2"])).then_inc(small, 16)
            sp.dma_start(a_log[:, :], spread(a["a_log_2"])).then_inc(small, 16)
            sp.dma_start(m.d_skip[:, :], spread(a["d_skip_2"])).then_inc(small, 16)
            for i, dst in enumerate((m.z_dram, m.v_dram)):
                b = FIRST + 4 + i
                m.ring.issue(sp, 2 * b + 3)
                for t in range(TT):
                    n = i * TT + t
                    sp.wait_ge(staged, n + 1)
                    sp.dma_start(dst[t * P:(t + 1) * P, :], stage[:, n % 4, :]).then_inc(stored[n % 4], 16)
                m.ring.issue(sp, 2 * b + 4)
            for s in range(4):
                sp.wait_ge(stored[s], 16 * 4)

        @block.tensor
        def _(pe):
            pe.wait_ge(dt_split, 1)
            for t in range(TT):
                for k in range(KT):
                    for i, j in ((0, 0), (0, 1), (1, 0)):
                        last = pe.matmul(psd[:, t, :], R(acts[i](k)[:, t * P:(t + 1) * P]), R(w_dt[j][:, k, :]),
                                         start=(k == i == j == 0), stop=(k == KT - 1 and i == 1))
            last.then_inc(dt_ready, 1)
            pe.wait_ge(dt_read, 1)
            for first, tokens in ((0, False), (4, True)):
                with pe.Fori(0, 2 if tokens else 4) as i:
                    gemm(pe, m, acts, lambda h: pe.wait_ge(m.ring.split, i * 2 + (2 * (FIRST + first) + h + 1)), i * 8 + 8 * first,
                         ps, ps_ready, ps_free, tokens)

        @block.scalar
        def _(act):
            act.sem_inc(ps_free, 8)
            act.wait_ge(small, 64)
            act.activation(R(w_dt[0][:, :, :]), w_dt[1][:, :, :], ACT.Copy).then_inc(dt_high, 1)
            act.activation(a_log[:, :], a_log[:, :], ACT.Exp).then_inc(a_exp, 1)

            def silu(c):
                act.wait_ge(convolved, c + 1)
                act.activation(raw[:, c, TAPS - 1:], conv[c % 2][:, :], ACT.Silu).then_inc(silued, 1)

            def softplus():
                act.wait_ge(dt_mag, 1)
                act.activation(mag[:, :, :], mag[:, :, :], ACT.Exp, scale=-1.0)
                act.drain()
                act.activation(mag[:, :, :], mag[:, :, :], ACT.Ln, bias=1.0).then_inc(dt_log, 1)

            def evacuate(n, last):
                act.wait_ge(ps_ready, n + 1)
                if last:
                    m.ring.release(act)
                src, cols = ps[:, n % 8, :], slice((n % 2) * HALF, (n % 2 + 1) * HALF)
                if n < 16:
                    act.copy(raw[:, n // 2, TAPS - 1 + (n % 2) * HALF:TAPS - 1 + (n % 2 + 1) * HALF], src).then_inc(ps_free, 1)
                    act.drain()
                    act.sem_inc(raw_sb, 1)
                    if n % 8 in (4, 6):
                        silu(n // 8 * 4 + (n % 8 - 4) // 2)
                elif n < 24:
                    act.mul(qk[:, n // 2 - 8, cols], src, float(AHD) ** -0.5).then_inc(ps_free, 1)
                elif n < 32:
                    act.copy(qk[:, n // 2 - 8, cols], src).then_inc(ps_free, 1)
                else:
                    store_stage(act, stored, n - 32)
                    act.activation(stage[:, n % 4, :], src, ACT.Silu if n < 40 else ACT.Copy)
                    act.drain()
                    act.sem_inc(staged, 1)
                    act.sem_inc(ps_free, 1)
                if n in (8, 16):
                    silu(n // 2 - 2)
                    silu(n // 2 - 1)

            evacuate_split(act, m, (FIRST, FIRST + 6), evacuate, softplus)

        @block.vector
        def _(dve):
            dve.memset(raw[:, :, 0:TAPS - 1], 0.0)
            dve.wait_ge(dt_high, 1)
            dve.tensor_tensor(R(w_dt[1][:, :, :]), w_dt[1][:, :, :], rounded(w_dt[0][:, :, :]), ALU.subtract).then_inc(dt_split, 1)
            for i in range(2):
                m.ring.make_low(dve, 2 * FIRST + i)
            dve.wait_ge(dt_ready, 1)
            dve.tensor_tensor(m.dt[:, :, :], psd, dt_bias[:, None, :].to_broadcast([P, TT, SH]), ALU.add).then_inc(dt_read, 1)
            dve.drain()
            dve.tensor_scalar(mag[:, :, :], m.dt[:, :, :], -1.0, None, ALU.mult)
            dve.drain()
            dve.tensor_tensor(mag[:, :, :], mag[:, :, :], m.dt[:, :, :], ALU.max).then_inc(dt_mag, 1)
            dve.wait_ge(dt_log, 1)
            dve.tensor_scalar(m.dt[:, :, :], m.dt[:, :, :], 0.0, None, ALU.max)
            dve.drain()
            dve.tensor_tensor(m.dt[:, :, :], m.dt[:, :, :], mag[:, :, :], ALU.add)
            dve.drain()
            dve.scalar_tensor_tensor(m.adt[:, :, :], m.dt[:, :, :], -1.0, a_log[:, None, :].to_broadcast([P, TT, SH]),
                                     ALU.mult, ALU.mult)
            row, bias = VEC["ssd_conv_w_2"][0], VEC["ssd_conv_b_2"][0]
            for c in range(KT):
                out = conv[c % 2][:, :]
                dve.wait_ge(raw_sb, 2 * c + 2)
                if c >= 2:
                    dve.wait_ge(silued, c - 1)
                w = lambda j: m.cols[:, row + j * KT + c:row + j * KT + c + 1]
                dve.tensor_scalar(out, raw[:, c, 0:T], w(0), m.cols[:, bias + c:bias + c + 1], ALU.mult, ALU.add)
                for j in range(1, TAPS):
                    dve.drain()
                    ins = dve.scalar_tensor_tensor(out, raw[:, c, j:j + T], w(j), out, ALU.mult, ALU.add)
                ins.then_inc(convolved, 1)
                if c % 4 == 0:
                    m.ring.make_low(dve, 2 * FIRST + c // 2 + 2)
                if c % 4 == 3:
                    m.ring.make_low(dve, 2 * FIRST + c // 2 + 2)
            for i in range(6, 12):
                m.ring.make_low(dve, 2 * FIRST + i)


def state_space(nc, m, a):
    W = SH * SHD
    with ExitStack() as ctx:
        sem = lambda n: nc.alloc_semaphore(fresh(n))
        sb = lambda n, s, d=F32: ctx.enter_context(nc.sbuf_tensor(n, s, d))
        cur = m.b1[:, 4, :].rearrange("p (c n) -> p c n", c=KT)
        later = m.b1[:, 5, :].rearrange("p (h n) -> p h n", h=SH)
        dec = m.b1[:, 6, :].rearrange("p (h n) -> p h n", h=SH)
        M = m.b1[:, 7, :].rearrange("p (h n) -> p h n", h=SH)
        adt, dt, es, es_next = sb("adt_now", [P, SH]), sb("dt_now", [P, SH]), sb("decays", [P, 4, SH]), sb("decays_next", [P, 4, SH])
        X, XE, XD = sb("x_dt", [P, SH, SHD]), sb("x_to_end", [P, SH, SHD]), sb("x_skip", [P, SH, SHD])
        Bt, CB = sb("b_tokens", [P, SG, SN]), sb("cb", [P, SG, P])
        S, S_mid, tmp, y = sb("ssd_state", [P, SH, SHD]), sb("ssd_mid", [P, SH, SHD]), sb("ssd_tmp", [P, SH, SHD]), sb("ssd_y", [P, SH, SHD])
        psT = ctx.enter_context(nc.psum_tensor("ps_tokens", [P, 2, HALF], F32))
        psS = ctx.enter_context(nc.psum_tensor("ps_small", [P, 4, SH], F32))
        psG = ctx.enter_context(nc.psum_tensor("ps_seg", [P, SH, P], F32))
        psY = ctx.enter_context(nc.psum_tensor("ps_diag", [P, SH, SHD], F32))
        psZ = ctx.enter_context(nc.psum_tensor("ps_off", [P, SH, SHD], F32))
        (cur_ready, adt_ready, later_ready, small_ready, small_exp, T_ready, seg_ready, dec_ready, x_ready, M_ready,
         diag_ready, upd_ready, mid_ready, state_ready, off0_ready, off_ready) = (sem("s_" + n) for n in (
             "current", "adt", "later", "small", "small_exp", "tokens", "seg", "decay", "x", "M", "diag", "update", "mid",
             "state", "off0", "off"))
        zv_arrived, y_read = sem("zv_arrived"), sem("y_read")
        block = ctx.enter_context(nc.Block())
        heads = lambda v: v[:, :, None].to_broadcast([P, SH, SHD])
        group = lambda g: slice(g * HPG, (g + 1) * HPG)

        def over_tiles(engine, step):
            with engine.Fori(0, TT - 1) as p:
                step(p, False)
            step(TT - 1, True)

        @block.sync
        def _(sp):
            for dst, src in ((m.z, m.z_dram), (m.v, m.v_dram)):
                sp.dma_start(dst, src.rearrange("(t p) n -> p t n", p=P)).then_inc(zv_arrived, 16)
            sp.wait_ge(zv_arrived, 32)

        @block.scalar
        def _(act):
            act.sem_inc(off_ready, 1)

            def decays(p):
                act.wait_ge(small_ready, p + 1)
                act.activation(es_next[:, :, :], psS[:, :, :], ACT.Exp).then_inc(small_exp, 1)
                act.wait_ge(seg_ready, p + 1)
                act.activation(dec, psG[:, :, :], ACT.Exp).then_inc(dec_ready, 1)

            def step(p, last_tile):
                act.wait_ge(off_ready, p + 1)
                carry(act, m)
                act.activation(cur, m.raw[:, :, bass.ds(p * P + (TAPS - 1), P)], ACT.Copy).then_inc(cur_ready, 1)
                if not last_tile:
                    act.wait_ge(M_ready, p + 1)
                    decays(p + 1)
            decays(0)
            over_tiles(act, step)

        @block.tensor
        def _(pe):
            def sums(p):
                pe.wait_ge(adt_ready, p + 1)
                for i, mask in enumerate((m.upto[:, :], m.after[:, :], m.chunk_ones[:, 0, :], m.chunk_ones[:, 1, :])):
                    last = pe.matmul(psS[:, i, :], mask, adt[:, :], start=True, stop=True)
                last.then_inc(small_ready, 1)
                pe.wait_ge(later_ready, p + 1)
                for h in range(SH):
                    last = pe.matmul(psG[:, h, :], later[:, h, :], m.upto[:, :], start=True, stop=True)
                last.then_inc(seg_ready, 1)

            def step(p, last_tile):
                pe.wait_ge(cur_ready, p + 1)
                pe.wait_ge(state_ready, p + 1)
                for c in range(4):
                    pe.transpose(psT[:, 0, c * P:(c + 1) * P], cur[:, c, :], m.ident[:, :])
                for g in range(SG):
                    pe.transpose(psT[:, 1, g * P:(g + 1) * P], cur[:, 4 + g, :], m.ident[:, :])
                for g in range(SG):
                    last = pe.matmul(psT[:, 1, (2 + g) * P:(3 + g) * P], cur[:, 4 + g, :], cur[:, 6 + g, :], start=True, stop=True)
                last.then_inc(T_ready, 1)
                pe.wait_ge(y_read, p + 1)
                for g in range(SG):
                    last = pe.matmul(psZ[0:CH, group(g), :], cur[:, 6 + g, 0:CH], S[:, group(g), :], start=True, stop=True)
                last.then_inc(off0_ready, 1)
                pe.wait_ge(x_ready, p + 1)
                for c in range(2):
                    for g in range(SG):
                        last = pe.matmul(psT[:, c, g * 2 * P:(g + 1) * 2 * P], Bt[c * CH:(c + 1) * CH, g, :],
                                         XE[c * CH:(c + 1) * CH, group(g), :], start=True, stop=True)
                last.then_inc(upd_ready, 1)
                pe.wait_ge(M_ready, p + 1)
                for h in range(SH):
                    last = pe.matmul(psY[:, h, :], M[:, h, :], X[:, h, :], start=True, stop=True)
                last.then_inc(diag_ready, 1)
                pe.wait_ge(mid_ready, p + 1)
                for g in range(SG):
                    last = pe.matmul(psZ[CH:P, group(g), :], cur[:, 6 + g, CH:P], S_mid[:, group(g), :], start=True, stop=True)
                last.then_inc(off_ready, 1)
                if not last_tile:
                    sums(p + 1)
            sums(0)
            over_tiles(pe, step)

        @block.vector
        def _(dve):
            dve.memset(S[:, :, :], 0.0).then_inc(state_ready, 1)
            dve.wait_ge(zv_arrived, 32)
            def exponents(p):
                dve.tensor_copy(adt[:, :], m.adt[:, p, :])
                dve.tensor_copy(dt[:, :], m.dt[:, p, :])
                dve.drain()
                dve.sem_inc(adt_ready, 1)
                dve.tensor_tensor(later, m.after[:, None, :].to_broadcast([P, SH, P]),
                                  adt[:, :, None].to_broadcast([P, SH, P]), ALU.mult).then_inc(later_ready, 1)

            def step(p, last_tile):
                dve.wait_ge(T_ready, p + 1)
                xs = psT[:, 0, :].rearrange("p (h n) -> p h n", h=SH)
                dve.tensor_tensor(X[:, :, :], xs, heads(dt), ALU.mult)
                dve.tensor_tensor(XD[:, :, :], xs, heads(m.d_skip), ALU.mult)
                dve.tensor_copy(Bt[:, :, :], psT[:, 1, 0:2 * P].rearrange("p (g n) -> p g n", g=SG))
                dve.tensor_tensor(CB[:, :, :], psT[:, 1, 2 * P:4 * P].rearrange("p (g n) -> p g n", g=SG),
                                  m.upto[:, None, :].to_broadcast([P, SG, P]), ALU.mult)
                dve.wait_ge(small_exp, p + 1)
                dve.tensor_copy(es[:, :, :], es_next[:, :, :])
                dve.drain()
                dve.tensor_tensor(XE[:, :, :], X[:, :, :], heads(es[:, 1]), ALU.mult).then_inc(x_ready, 1)
                dve.wait_ge(dec_ready, p + 1)
                for g in range(SG):
                    ins = dve.tensor_tensor(M[:, group(g), :], dec[:, group(g), :],
                                            CB[:, g, None, :].to_broadcast([P, HPG, P]), ALU.mult)
                ins.then_inc(M_ready, 1)
                if not last_tile:
                    exponents(p + 1)
                dve.tensor_tensor(tmp[:, :, :], S[:, :, :], heads(es[:, 2]), ALU.mult)
                dve.drain()
                dve.wait_ge(upd_ready, p + 1)
                dve.tensor_tensor(S_mid[:, :, :], psT[:, 0, :].rearrange("p (h n) -> p h n", h=SH), tmp[:, :, :],
                                  ALU.add).then_inc(mid_ready, 1)
                dve.drain()
                dve.tensor_tensor(tmp[:, :, :], S_mid[:, :, :], heads(es[:, 3]), ALU.mult)
                dve.drain()
                dve.wait_ge(off0_ready, p + 1)
                dve.tensor_tensor(S[:, :, :], psT[:, 1, :].rearrange("p (h n) -> p h n", h=SH), tmp[:, :, :],
                                  ALU.add).then_inc(state_ready, 1)
                dve.wait_ge(off_ready, p + 2)
                dve.tensor_tensor(y[:, :, :], psZ[:, :, :], heads(es[:, 0]), ALU.mult)
                dve.drain()
                dve.wait_ge(diag_ready, p + 1)
                dve.tensor_tensor(y[:, :, :], psY[:, :, :], y[:, :, :], ALU.add).then_inc(y_read, 1)
                dve.drain()
                dve.tensor_tensor(y[:, :, :], y[:, :, :], XD[:, :, :], ALU.add)
                dve.drain()
                z = m.z[:, p, :]
                dve.tensor_tensor(z, z, y[:, :, :].rearrange("p h n -> p (h n)"), ALU.mult)
                dve.drain()
            dve.sem_inc(y_read, 1)
            exponents(0)
            over_tiles(dve, step)


def band_attention(nc, m, a):
    qk, v = m.b3, m.v
    with ExitStack() as ctx:
        sem = lambda n: nc.alloc_semaphore(fresh(n))
        sb = lambda n, s, d=F32: ctx.enter_context(nc.sbuf_tensor(n, s, d))
        q = m.raw[:, 0, 0:T]
        k = m.raw[:, 1, 0:T]
        bias = [m.raw[:, 2 + u, 0:BAND] for u in range(2)]
        sc = [m.raw[:, 4 + u, 0:BAND] for u in range(2)]
        pT = [m.raw[:, 6 + u, 0:BAND] for u in range(2)]
        nmx, rs, ri = sb("minus_max", [P, 4]), sb("prob_sum", [P, 4]), sb("prob_inv", [P, 4])
        psS = [ctx.enter_context(nc.psum_tensor(f"ps_scores{u}", [P, 2 * HALF], F32)) for u in range(2)]
        psT = [ctx.enter_context(nc.psum_tensor(f"ps_probsT{u}", [P, 2 * HALF], F32)) for u in range(2)]
        psO = [psT[u][:, HALF + P:HALF + P + AHD] for u in range(2)]
        bias_arrived = [sem(f"bias_arrived{u}") for u in range(2)]
        (copied, scores, read_s, maxed, exped, turned, pT_sb, out_ready, out_sb) = (sem("b_" + n) for n in (
            "qk_copied", "scores", "scores_read", "maxed", "exped", "turned", "probsT", "out", "out_in_sbuf"))
        block = ctx.enter_context(nc.Block())
        PAIRS = AH // 2
        WARM = 2
        UNITS = 2 * TT
        units = [(u, j) for j in range(TT) for u in range(2)]
        tiles = lambda n: min(units[n][1], BANDT - 1) + 1

        @block.sync
        def _(sp):
            for u in range(2):
                sp.dma_start(bias[u], shifted(m.bias_lines[u])).then_inc(bias_arrived[u], 16)
            with sp.Fori(1, PAIRS) as hp:
                for u in range(2):
                    sp.wait_ge(read_s, hp * UNITS + 2)
                    sp.dma_start(bias[u], shifted(m.bias_lines[hp * 2 + u])).then_inc(bias_arrived[u], 16)

        @block.scalar
        def _(act):
            act.sem_inc(out_ready, 1)
            with act.Fori(0, PAIRS) as hp:
                act.wait_ge(out_ready, hp * UNITS + 1)
                carry(act, m)
                act.activation(q, qk[:, hp, :], ACT.Copy)
                act.activation(k, qk[:, hp + PAIRS, :], ACT.Copy).then_inc(copied, 1)

                def exponentials(n):
                    w, i = tiles(n) * P, n % 4
                    act.wait_ge(maxed, hp * UNITS + (n + 1))
                    act.activation(sc[n % 2][:, 0:w], sc[n % 2][:, 0:w], ACT.Exp, bias=nmx[:, i:i + 1], scale=-1.0, accum_out=rs[:, i:i + 1])
                    act.drain()
                    act.sem_inc(exped, 1)

                exponentials(0)
                exponentials(1)
                for n in range(UNITS):
                    w = tiles(n) * P
                    act.wait_ge(turned, hp * UNITS + (n + 1))
                    if n >= 2:
                        act.wait_ge(out_ready, hp * UNITS + n)
                    act.activation(pT[n % 2][:, 0:w], psT[n % 2][:, 0:w], ACT.Copy).then_inc(pT_sb, 1)
                    if n + 2 < UNITS:
                        exponentials(n + 2)

        @block.tensor
        def _(pe):
            with pe.Fori(0, PAIRS) as hp:
                def score(n):
                    u, j = units[n]
                    first, w = j + 1 - tiles(n), tiles(n) * P
                    pe.wait_ge(read_s, hp * UNITS + (n + 1))
                    rows = slice(u * AHD, (u + 1) * AHD)
                    for c0 in range(0, w, HALF):
                        c1 = min(w, c0 + HALF)
                        last = pe.matmul(psS[u][:, c0:c1], q[rows, j * P:(j + 1) * P], k[rows, first * P + c0:first * P + c1],
                                         start=True, stop=True)
                    last.then_inc(scores, 1)

                def turn(n):
                    u = n % 2
                    pe.wait_ge(exped, hp * UNITS + (n + 1))
                    pe.wait_ge(out_sb, hp * UNITS + (n + 1))
                    for t in range(tiles(n)):
                        last = pe.transpose(psT[u][:, t * P:(t + 1) * P], sc[u][:, t * P:(t + 1) * P], m.ident[:, :])
                    last.then_inc(turned, 1)

                pe.wait_ge(copied, hp + 1)
                score(0)
                score(1)
                pe.wait_ge(out_sb, hp * UNITS + 1)
                for n in range(WARM):
                    pe.matmul(psT[0][:, 0:HALF], m.ident[:, :], k[:, 0:HALF], start=True, stop=True)
                turn(0)
                for n, (u, j) in enumerate(units):
                    if n + 2 < UNITS:
                        score(n + 2)
                    if n + 1 < UNITS:
                        turn(n + 1)
                    pe.wait_ge(pT_sb, hp * UNITS + (n + 1))
                    for t in range(tiles(n)):
                        last = pe.matmul(psO[u], pT[u][:, t * P:(t + 1) * P],
                                         v[:, j + 1 - tiles(n) + t, bass.ds(hp * 2 * AHD + u * AHD, AHD)],
                                         start=(t == 0), stop=(t == tiles(n) - 1))
                    last.then_inc(out_ready, 1)

        @block.vector
        def _(dve):
            dve.sem_inc(read_s, 2)
            dve.sem_inc(out_sb, 2)
            with dve.Fori(0, PAIRS) as hp:
                for u in range(2):
                    dve.wait_ge(bias_arrived[u], (hp + 1) * 16)
                    dve.memset(bias[u][0:CH, BAND - CH:BAND], MASKED)
                    dve.memset(bias[u][CH:P, 0:CH], MASKED)
                dve.drain()

                def biased(n):
                    u, w, i = n % 2, tiles(n) * P, n % 4
                    dve.wait_ge(scores, hp * UNITS + (n + 1))
                    if n >= 2:
                        dve.wait_ge(turned, hp * UNITS + (n - 1))
                    carry(dve, m)
                    dve.tensor_tensor_reduce(sc[u][:, 0:w], psS[u][:, 0:w], bias[u][:, BAND - w:BAND], -1.0, -MASKED,
                                             ALU.add, ALU.min, nmx[:, i:i + 1])
                    dve.drain()
                    dve.sem_inc(maxed, 1)
                    dve.sem_inc(read_s, 1)

                biased(0)
                biased(1)
                for n, (u, j) in enumerate(units):
                    i = n % 4
                    if n + 2 < UNITS:
                        biased(n + 2)
                    dve.wait_ge(out_ready, hp * UNITS + (n + 2))
                    dve.reciprocal(ri[:, i:i + 1], rs[:, i:i + 1])
                    dve.drain()
                    dve.tensor_scalar(m.att[:, j, bass.ds(hp * 2 * AHD + u * AHD, AHD)], psO[u], ri[:, i:i + 1],
                                      None, ALU.mult).then_inc(out_sb, 1)
                dve.drain()


def shifted(lines):
    w = BAND + P
    flat = lines.rearrange("p n -> (p n)")
    return flat[P - 1:P - 1 + P * (w - 1)].rearrange("(p n) -> p n", n=w - 1)[:, 0:BAND]


def mixer_norm(nc, m, a):
    with ExitStack() as ctx:
        sem = lambda n: nc.alloc_semaphore(fresh(n))
        sb = lambda n, s, d=F32: ctx.enter_context(nc.sbuf_tensor(n, s, d))
        ss, root, inv, junk = sb("y_ss", [P, TT]), sb("y_root", [P, TT]), sb("y_inv", [P, TT]), sb("y_squares", [P, 2, HALF])
        ps = ctx.enter_context(nc.psum_tensor("ps_catT", [P, 4, HALF], F32))
        summed, squares, roots, normed, ps_ready, ps_free, high_made = (
            sem(n) for n in ("y_summed", "y_meaned", "y_rooted", "y_normed", "catT_ready", "catT_free", "catT_high"))
        block = ctx.enter_context(nc.Block())
        y = m.z
        squared = [(y[:, t, :], ss[:, t:t + 1]) for t in range(TT)]
        row = VEC["ssd_norm_w_2"][0]
        gain = lambda k: m.cols[:, row + k:row + k + 1] if k < 4 else None

        @block.scalar
        def _(act):
            sum_squares(act, None, squared, junk, summed)
            inverse_rms(act, None, ss[:, :], root[:, :], None, HALF, squares, roots)
            high_from_banks(act, m.cat[0], gain, ps, ps_ready, high_made)

        @block.vector
        def _(dve):
            sum_squares(None, dve, squared, junk, summed)
            dve.wait_ge(summed, TT)
            dve.tensor_scalar(ss[:, :], ss[:, :], 1.0 / (SH * SHD), EPS, ALU.mult, ALU.add).then_inc(squares, 1)
            inverse_rms(None, dve, None, root[:, :], inv[:, :], HALF, squares, roots)
            for t in range(TT):
                dve.tensor_scalar(y[:, t, :], y[:, t, :], inv[:, t:t + 1], None, ALU.mult).then_inc(normed, 1)
            low_from_banks(dve, m.cat[0], m.cat[1], gain, ps, ps_free, high_made)

        @block.tensor
        def _(pe):
            pe.wait_ge(normed, TT)
            for n in range(2 * KT):
                k, half = n // 2, n % 2
                src = y if k < 4 else m.att
                if n >= 4:
                    pe.wait_ge(ps_free, n - 3)
                for j in range(4):
                    last = pe.transpose(ps[:, n % 4, j * P:(j + 1) * P], src[:, 4 * half + j, (k % 4) * P:(k % 4 + 1) * P],
                                        m.ident[:, :])
                last.then_inc(ps_ready, 1)



TH = TT // 2
UP_ITEMS = 4 * (FT // 2)
HALF_ITEMS = UP_ITEMS + FT


class Feed:

    def __init__(self, nc, ctx, m, a):
        self.low = [m.ring.buf[:, s // 2, 2 * (s % 2):2 * (s % 2) + 2, :] for s in range(4)]
        self.high = [m.ring.buf[:, 2 + s // 2, 2 * (s % 2):2 * (s % 2) + 2, :] for s in range(4)]
        sem = lambda n: ctx.enter_context(nc.semaphore(n))
        self.loaded = [sem(f"feed_loaded{s}") for s in range(4)]
        self.high_made, self.split, self.used = sem("feed_high"), sem("feed_split"), sem("feed_used")
        self.up_ready, self.down_ready = sem("up_ready"), sem("down_ready")
        self.w_up, self.w_down, self.issued = a["w_up_2"][0], a["w_down_2"][0], 0

    def done(self, sp, i):
        h, j = i // HALF_ITEMS, i % HALF_ITEMS
        if j < UP_ITEMS and j % 4 == 3:
            sp.wait_ge(self.up_ready, 4 * (h * (UP_ITEMS // 4) + j // 4 + 1))
        elif j == HALF_ITEMS - 1:
            sp.wait_ge(self.down_ready, 8 * (h + 1))
        else:
            sp.wait_ge(self.used, self.uses(i))

    def uses(self, i):
        h, j = i // HALF_ITEMS, i % HALF_ITEMS
        up = min(j + 1, UP_ITEMS)
        return h * (HALF_ITEMS - UP_ITEMS // 4 - 1) + up - up // 4 + j + 1 - up

    def issue(self, sp, end):
        for i in range(self.issued, min(end, 2 * HALF_ITEMS)):
            if i >= 4:
                self.done(sp, i - 4)
            j, s = i % HALF_ITEMS, i % 4
            for part in range(2):
                if j < UP_ITEMS:
                    b, rows = j // 4, slice(j % 4 * 2 * P, (j % 4 + 1) * 2 * P)
                    sp.dma_start(self.low[s][:, :, part * 2 * P:(part + 1) * 2 * P],
                                 self.w_up[rows, part * FDIM + b * 2 * P:part * FDIM + (b + 1) * 2 * P]
                                 .rearrange("(k p) n -> p k n", p=P)).then_inc(self.loaded[s], 16)
                else:
                    k = j - UP_ITEMS
                    sp.dma_start(self.low[s][:, part, :], self.w_down[k * P:(k + 1) * P, part * HALF:(part + 1) * HALF])\
                        .then_inc(self.loaded[s], 16)
            self.issued = i + 1

    def make_high(self, act, i, b=0):
        s = i % 4
        act.wait_ge(self.loaded[s], b * 32 + (i // 4 + 1) * 32)
        act.activation(R(self.high[s]), self.low[s], ACT.Copy).then_inc(self.high_made, 1)

    def make_low(self, dve, i, b=0):
        s = i % 4
        dve.wait_ge(self.high_made, b * 4 + (i + 1))
        dve.tensor_tensor(R(self.low[s]), self.low[s], rounded(self.high[s]), ALU.subtract).then_inc(self.split, 1)


def ffn_norm(nc, m, h):
    src, xn = m.b3[:, 0:TH, :], m.b4[:, 0:TH, :]
    with ExitStack() as ctx:
        sem = lambda n: nc.alloc_semaphore(fresh(n))
        sb = lambda n, s, d=F32: ctx.enter_context(nc.sbuf_tensor(fresh(n), s, d))
        ss, root, inv, junk = sb("h_ss", [P, TH]), sb("h_root", [P, TH]), sb("h_inv", [P, TH]), sb("h_squares", [P, 2, D])
        squared = [(src[:, t, :], ss[:, t:t + 1]) for t in range(TH)]
        ps = ctx.enter_context(nc.psum_tensor(fresh("ps_h"), [P, KT, HALF], F32))
        sums, squares, roots, scaled, turned, made, high_made, stored = (
            sem("h_" + n) for n in ("sums", "meaned", "rooted", "scaled", "turned", "made", "high", "x3_stored"))
        block = ctx.enter_context(nc.Block())

        @block.sync
        def _(sp):
            if h == 0:
                sp.dma_start(m.x3_dram.rearrange("(t p) d -> p t d", p=P), m.b3).then_inc(stored, 16)
                m.feed.issue(sp, 4)
                sp.wait_ge(stored, 16)

        @block.scalar
        def _(act):
            if h == 1:
                act.wait_ge(m.x3_arrived, 16)
            sum_squares(act, None, squared, junk, sums)
            inverse_rms(act, None, ss[:, :], root[:, :], None, D, squares, roots)
            for k in range(KT):
                act.wait_ge(made, k + 1)
                act.activation(R(m.hT[0](k)), m.hT[1](k), ACT.Copy).then_inc(high_made, 1)

        @block.vector
        def _(dve):
            if h == 1:
                dve.wait_ge(m.x3_arrived, 16)
            sum_squares(None, dve, squared, junk, sums)
            dve.wait_ge(sums, TH)
            dve.tensor_scalar(ss[:, :], ss[:, :], 1.0 / D, EPS, ALU.mult, ALU.add).then_inc(squares, 1)
            inverse_rms(None, dve, None, root[:, :], inv[:, :], D, squares, roots)
            for t in range(TH):
                dve.tensor_scalar(xn[:, t, :], src[:, t, :], inv[:, t:t + 1], None, ALU.mult).then_inc(scaled, 1)

            def low_part(k):
                dve.wait_ge(high_made, k + 1)
                dve.tensor_tensor(R(m.hT[1](k)), m.hT[1](k), rounded(m.hT[0](k)), ALU.subtract)

            for k in range(KT):
                dve.wait_ge(turned, k + 1)
                dve.tensor_scalar(m.hT[1](k), ps[:, k, :], m.scale_ffn[:, k:k + 1], m.shift_ffn[:, k:k + 1],
                                  ALU.mult, ALU.add).then_inc(made, 1)
                if k:
                    low_part(k - 1)
            low_part(KT - 1)

        @block.tensor
        def _(pe):
            pe.wait_ge(scaled, TH)
            for k in range(KT):
                for t in range(TH):
                    last = pe.transpose(ps[:, k, t * P:(t + 1) * P], xn[:, t, k * P:(k + 1) * P], m.ident[:, :])
                last.then_inc(turned, 1)


def ffn_up(nc, m, h):
    PAD = FTAPS - 1
    BLOCKS = FT // 2
    BASE = h * HALF_ITEMS
    feed = m.feed
    with ExitStack() as ctx:
        sem = lambda n: nc.alloc_semaphore(fresh(n))
        sb = lambda n, s, d=F32: ctx.enter_context(nc.sbuf_tensor(fresh(n), s, d))
        raw = [[sb(f"up_raw{x}{c}", [P, HALF + PAD]) for x in range(2)] for c in range(2)]
        conv = [[sb(f"up_conv{x}{c}", [P, HALF]) for x in range(2)] for c in range(2)]
        ps = ctx.enter_context(nc.psum_tensor(fresh("ps_up"), [P, 8, HALF], F32))
        ps_free, raw_sb, raw_free, gate_conv, silued, u_made, u_high = (
            sem("up_" + n) for n in ("free", "raw_in_sbuf", "raw_free", "convolved", "silu", "u", "u_high"))
        block = ctx.enter_context(nc.Block())

        def over_blocks(engine, step):
            with engine.Fori(0, BLOCKS // 2) as i:
                for s in range(2):
                    step(i * 2 + s, s, False)
            step(BLOCKS - 1, 0, True)

        @block.sync
        def _(sp):
            feed.issue(sp, BASE + UP_ITEMS + 4)

        @block.tensor
        def _(pe):
            def step(b, s, last_block):
                for q in range(4):
                    pe.wait_ge(feed.split, b * 4 + (BASE + q + 1))
                    slot = (BASE + q) % 4
                    weights = (feed.high[slot], feed.low[slot])
                    for n, c in enumerate((0, 2, 1, 3)):
                        if q == 0:
                            pe.wait_ge(ps_free, b * 4 + (n + 1))
                        for k in range(2):
                            for i, j in ((0, 0), (0, 1), (1, 0)):
                                last = pe.matmul(ps[:, 4 * s + n, :], R(weights[i][:, k, c * P:(c + 1) * P]),
                                                 R(m.hT[j](2 * q + k)), start=(q == k == i == j == 0),
                                                 stop=(q == 3 and k == 1 and i == 1))
                        if q == 3:
                            last.then_inc(feed.up_ready, 1)
                    if q < 3:
                        last.then_inc(feed.used, 1)
            over_blocks(pe, step)

        @block.scalar
        def _(act):
            act.sem_inc(ps_free, 8)
            for q in range(4):
                feed.make_high(act, BASE + q)

            def step(b, s, last_block):
                def ahead(q):
                    if not last_block:
                        feed.make_high(act, BASE + 4 + q, b)

                ahead(0)
                ahead(1)
                for c in range(2):
                    act.wait_ge(raw_free, b * 2 + (c + 1))
                    for x in range(2):
                        act.wait_ge(feed.up_ready, b * 4 + (h * 4 * BLOCKS + 2 * c + x + 1))
                        act.copy(raw[c][x][:, PAD:PAD + HALF], ps[:, 4 * s + 2 * c + x, :]).then_inc(ps_free, 1)
                    act.drain()
                    act.sem_inc(raw_sb, 1)
                ahead(2)
                for c in range(2):
                    act.wait_ge(gate_conv, b * 2 + (c + 1))
                    act.activation(conv[c][0][:, :], conv[c][0][:, :], ACT.Silu).then_inc(silued, 1)
                    if c == 0:
                        ahead(3)
                for c in range(2):
                    act.wait_ge(u_made, b * 2 + (c + 1))
                    carry(act, m)
                    act.activation(m.u_high[:, col(b * 2 + c), :], m.u_low[:, col(b * 2 + c), :], ACT.Copy).then_inc(u_high, 1)
            over_blocks(act, step)

        @block.vector
        def _(dve):
            dve.sem_inc(raw_free, 2)
            if h == 0:
                dve.memset(m.history[:, :, :], 0.0)
                dve.drain()
            for q in range(4):
                feed.make_low(dve, BASE + q)

            def step(b, s, last_block):
                def ahead(q):
                    if not last_block:
                        feed.make_low(dve, BASE + 4 + q, b)

                def convolve(c):
                    dve.wait_ge(raw_sb, b * 2 + (c + 1))
                    carry(dve, m)
                    for x in range(2):
                        tile = b * 2 + (x * FT + c)
                        dve.tensor_copy(raw[c][x][:, 0:PAD], m.history[:, col(tile), :])
                    dve.drain()
                    for x in range(2):
                        tile = b * 2 + (x * FT + c)
                        dve.tensor_copy(m.history[:, col(tile), :], raw[c][x][:, HALF:HALF + PAD])
                        dve.tensor_scalar(conv[c][x][:, :], raw[c][x][:, 0:HALF], m.conv_cols[:, col(tile)], None, ALU.mult)
                    for j in range(1, FTAPS):
                        dve.drain()
                        for x in range(2):
                            ins = dve.scalar_tensor_tensor(conv[c][x][:, :], raw[c][x][:, j:j + HALF],
                                                           m.conv_cols[:, col(b * 2 + (j * 2 * FT + x * FT + c))], conv[c][x][:, :],
                                                           ALU.mult, ALU.add)
                    ins.then_inc(gate_conv, 1)
                    dve.sem_inc(raw_free, 1)

                ahead(0)
                ahead(1)
                convolve(0)
                ahead(2)
                convolve(1)
                for c in range(2):
                    dve.wait_ge(silued, b * 2 + (c + 1))
                    dve.tensor_tensor(m.u_low[:, col(b * 2 + c), :], conv[c][0][:, :], conv[c][1][:, :], ALU.mult).then_inc(u_made, 1)
                    if c == 0:
                        ahead(3)
                for c in range(2):
                    dve.wait_ge(u_high, b * 2 + (c + 1))
                    n = col(b * 2 + c)
                    dve.tensor_tensor(m.u_low_r[:, n, :], m.u_low[:, n, :], m.u_high[:, n, :].bitcast(F32), ALU.subtract)
            over_blocks(dve, step)


def col(n):
    return slice(n, n + 1) if isinstance(n, int) else bass.ds(n, 1)


def ffn_down(nc, m, h):
    feed = m.feed
    BASE = h * HALF_ITEMS + UP_ITEMS
    x3, x = m.b1[:, TH:TT, :], m.b1[:, 0:TH, :]
    u = (m.u_high, m.u_low_r)
    with ExitStack() as ctx:
        sem = lambda n: nc.alloc_semaphore(fresh(n))
        ps = ctx.enter_context(nc.psum_tensor(fresh("ps_down"), [P, TH, 2, HALF], F32))
        arrived = sem("x3_arrived")
        block = ctx.enter_context(nc.Block())

        @block.sync
        def _(sp):
            sp.dma_start(x3, m.x3_dram[h * TH * P:(h + 1) * TH * P, :].rearrange("(t p) d -> p t d", p=P)).then_inc(arrived, 16)
            feed.issue(sp, BASE + FT + 4)

        @block.tensor
        def _(pe):
            for k in range(FT):
                pe.wait_ge(feed.split, BASE + k + 1)
                slot = (BASE + k) % 4
                weights = (feed.high[slot], feed.low[slot])
                for t in range(TH):
                    for c in range(2):
                        for i, j in ((0, 0), (0, 1), (1, 0)):
                            last = pe.matmul(ps[:, t, c, :], u[i][:, k, t * P:(t + 1) * P], R(weights[j][:, c, :]),
                                             start=(k == i == j == 0), stop=(k == FT - 1 and i == 1))
                        if k == FT - 1:
                            last.then_inc(feed.down_ready, 1)
                if k < FT - 1:
                    last.then_inc(feed.used, 1)

        @block.scalar
        def _(act):
            for k in range(FT):
                feed.make_high(act, BASE + k)

        @block.vector
        def _(dve):
            for k in range(FT):
                feed.make_low(dve, BASE + k)
            dve.wait_ge(arrived, 16)
            for t in range(TH):
                for c in range(2):
                    cols = slice(c * HALF, (c + 1) * HALF)
                    dve.wait_ge(feed.down_ready, h * 8 + 2 * t + c + 1)
                    dve.tensor_tensor(x[:, t, cols], ps[:, t, c, :], m.gate_ffn[:, cols], ALU.mult)
                dve.drain()
                dve.tensor_tensor(x[:, t, :], x[:, t, :], x3[:, t, :], ALU.add)


def final_norm(nc, m, a, out, h):
    x = m.b1[:, 0:TH, :]
    with ExitStack() as ctx:
        sem = lambda n: nc.alloc_semaphore(fresh(n))
        sb = lambda n, s, d=F32: ctx.enter_context(nc.sbuf_tensor(fresh(n), s, d))
        ss, root, inv, junk = sb("f_ss", [P, TH]), sb("f_root", [P, TH]), sb("f_inv", [P, TH]), sb("f_squares", [P, 2, D])
        squared = [(x[:, t, :], ss[:, t:t + 1]) for t in range(TH)]
        gain = sb("final_norm_2_wide", [P, D])
        gain_arrived, summed, squares, roots, normed, stored = (
            sem(n) for n in ("f_gain", "f_summed", "f_meaned", "f_rooted", "f_normed", "out_stored"))
        block = ctx.enter_context(nc.Block())

        @block.sync
        def _(sp):
            sp.dma_start(gain[:, :], spread(a["final_norm_w_2"].rearrange("(o d) -> o d", o=1))).then_inc(gain_arrived, 16)
            if h == 0:
                sp.dma_start(m.b3[:, 0:TH, :], m.x3_dram[TH * P:T, :].rearrange("(t p) d -> p t d", p=P)).then_inc(m.x3_arrived, 16)
            for t in range(TH):
                sp.wait_ge(normed, t + 1)
                at = (h * TH + t) * P
                sp.dma_start(out[0, at:at + P, :], x[:, t, :]).then_inc(stored, 16)
            sp.wait_ge(stored, 16 * TH)

        @block.scalar
        def _(act):
            sum_squares(act, None, squared, junk, summed)
            inverse_rms(act, None, ss[:, :], root[:, :], None, D, squares, roots)

        @block.vector
        def _(dve):
            sum_squares(None, dve, squared, junk, summed)
            dve.wait_ge(summed, TH)
            dve.tensor_scalar(ss[:, :], ss[:, :], 1.0 / D, EPS, ALU.mult, ALU.add).then_inc(squares, 1)
            inverse_rms(None, dve, None, root[:, :], inv[:, :], D, squares, roots)
            dve.wait_ge(gain_arrived, 16)
            for t in range(TH):
                dve.scalar_tensor_tensor(x[:, t, :], x[:, t, :], inv[:, t:t + 1], gain[:, :], ALU.mult, ALU.mult).then_inc(normed, 1)



def program(nc, a, out):
    _names.clear()
    _rounded.clear()
    with ExitStack() as ctx:
        ctx.enter_context(nc.allow_non_contiguous_dma(reason="columns and broadcasts"))
        sb = lambda n, s, d=F32: ctx.enter_context(nc.sbuf_tensor(n, s, d))
        dram = lambda n, s, d=F32: nc.dram_tensor(n, s, d).ap()
        m = Parts()
        PAD = TAPS - 1
        size2 = KT * (T + PAD)
        m.big = both_kinds(nc, ctx, "big", [P, 3 * 8 * D + size2], parts=4, part=8 * D)
        cut = lambda at, w=D: m.big[:, at:at + 8 * w].rearrange("p (t n) -> p t n", t=8)
        m.b1, m.b3, m.b4 = cut(0), cut(8 * D), cut(16 * D)
        m.b2, m.raw = cut(24 * D), cut(24 * D, T + PAD)
        m.hT = [by_tile(m.big[:, i * 4 * D:(i + 1) * 4 * D].rearrange("p (k n) -> p k n", n=HALF)) for i in range(2)]
        m.u_low = m.big[:, 8 * D + FT * HALF:8 * D + 2 * FT * HALF].rearrange("p (k n) -> p k n", n=HALF)
        start = nc.sbuf_base - 4 * (3 * 8 * D + size2)
        m.u_high, m.u_low_r = (nc.alloc_sbuf_tensor_at(f"hidden_rounded{i}", [P, FT, HALF], F32R,
                                                       offset=start + 4 * (8 * D + i * FT * HALF)) for i in range(2))
        m.history = sb("up_history", [P, 2 * FT, FTAPS - 1])
        m.ident, m.ones = sb("ident", [P, P]), sb("ones", [P, P])
        m.upto, m.after, m.before = sb("upto", [P, P]), sb("after", [P, P]), sb("before", [P, P])
        m.chunk_ones = sb("chunk_ones", [P, 2, P])
        m.expert_iota_i, m.expert_iota = sb("expert_iota_i", [P, EXPERTS], I32), sb("expert_iota", [P, EXPERTS])
        m.part_iota_i, m.part_iota = sb("part_iota_i", [P, 1], I32), sb("part_iota", [P, 1])
        m.codes_i = sb("codes_i", [P, 2 * TT], I32)
        m.cols, m.conv_cols = sb("vector_cols", [P, VROWS]), sb("conv_cols", [P, FROWS])
        m.gate_mix, m.gate_ffn = sb("gate_mix", [P, D]), sb("gate_ffn", [P, D])
        m.shift_mix, m.scale_mix = sb("shift_mix", [P, KT]), sb("scale_mix", [P, KT])
        m.shift_ffn, m.scale_ffn = sb("shift_ffn", [P, KT]), sb("scale_ffn", [P, KT])
        m.w13 = [b[:, 4 * j:4 * j + 4, :].rearrange("p a n -> p (a n)").rearrange("p (w k n) -> p w k n", w=2, k=KT)
                 for b in (m.b3, m.b1) for j in range(2)]
        m.w2 = [m.b2[:, 2 * j:2 * j + 2, :] for j in range(4)]
        m.w13_loaded = [ctx.enter_context(nc.semaphore(f"w13_loaded{u}")) for u in range(4)]
        m.w2_loaded = [ctx.enter_context(nc.semaphore(f"w2_loaded{u}")) for u in range(4)]
        m.scatter_idx, m.gather_idx = sb("scatter_idx", [SLOTS, EXPERTS], I32), sb("gather_idx", [SLOTS, EXPERTS], I32)
        m.gates2 = sb("expert_gates", [P, 2, TT])
        m.info_row, m.n_extra = sb("info_row", [1, 2 * P], I32), sb("n_extra", [1, 1], I32)
        m.info_dram = dram("block_info_d", (P, 2), I32)
        words = lambda b, t: b[:, t:t + 4, :].rearrange("p a n -> p (a n)").rearrange("p (t n) -> p t n", n=HALF)
        m.z, m.v, m.att = words(m.b4, 0), words(m.b4, 4), words(m.b1, 0)
        m.cat = (by_tile(m.b2), lambda k: m.b1[:, 4 + k, :] if k < 4 else m.b4[:, k, :])
        m.dt, m.adt, m.d_skip = sb("dt", [P, TT, SH]), sb("adt", [P, TT, SH]), sb("d_skip_wide", [P, SH])
        m.codes = dram("slot_codes", (T * EXPERTS, 1), I32)
        m.bias_lines = dram("bias_lines", (AH, P, BAND + P))
        m.xn_dram = dram("normed_tokens", (T, D))
        m.contrib = dram("contributions", (2 * T, D))
        m.x2_dram = dram("x2", (T, D))
        m.r_dram = dram("gla_gate", (T, D))
        m.z_dram, m.v_dram = dram("silu_z", (T, HALF)), dram("values", (T, HALF))
        m.x3_dram = dram("x3", (T, D))

        w1 = a["gla_w_in"][0]
        w2 = a["w_in_2"][0]
        c = lambda w, at, n=HALF: w[:, at:at + n]
        sources = [[c(w1, b * HALF)] for b in range(4)] + [[c(w1, 2064 + b * HALF)] for b in range(2)]
        sources += [[c(a["gla_w_o"][0], b * HALF)] for b in range(2)]
        sources += [[c(w2, at)] for at in (IN_AT["xbc"], IN_AT["xbc"] + HALF, IN_AT["q"], IN_AT["k"], IN_AT["z"], IN_AT["v"])]
        sources += [[c(a["w_out_2"][0], b * HALF)] for b in range(2)]
        m.ring = Ring(nc, ctx, sources)

        x = a["x"][0]
        m.carried = ctx.enter_context(nc.semaphore("waits_carried"))
        col = lambda name: (lambda k: m.cols[:, VEC[name][0] + k:VEC[name][0] + k + 1])

        m.resets = sb("resets", [P, T])
        with nc.cleanup_on_exit():
            constants(nc, m, a)
            modulation(nc, m, a)
            rms_to_channels(nc, m, m.b2, m.b2, m.b4, col("attn_norm"), None, high=m.b1, loads=x)
            with nc.sbuf_tensor("log_gates", [P, GH, T], F32) as m.gates:
                gla_projections(nc, m, a)
                gla_chunks(nc, m, a)
            gla_output(nc, m, a)
            project_back(nc, m, (by_tile(m.b1), by_tile(m.b2)), m.b4, x, 6, 2)
        with nc.cleanup_on_exit():
            rms_to_channels(nc, m, m.b4, m.b3, m.b1, col("ffn_norm"), None, to_dram=m.xn_dram)
            router(nc, m, a)
            experts(nc, m, a)
            more_blocks(nc, m, a)
            combine(nc, m, a)
        with nc.cleanup_on_exit():
            rms_to_channels(nc, m, m.b4, m.b3, m.b4, lambda k: m.scale_mix[:, k:k + 1], lambda k: m.shift_mix[:, k:k + 1],
                            high=m.b1)
            mixer_projections(nc, m, a)
            state_space(nc, m, a)
            band_attention(nc, m, a)
            mixer_norm(nc, m, a)
            project_back(nc, m, m.cat, m.b3, m.x2_dram, 14, 0, gate=m.gate_mix)
            m.feed = Feed(nc, ctx, m, a)
            m.x3_arrived = ctx.enter_context(nc.semaphore("x3_half_arrived"))
            for h in range(2):
                ffn_norm(nc, m, h)
                ffn_up(nc, m, h)
                ffn_down(nc, m, h)
                final_norm(nc, m, a, out, h)


INPUTS = ("a_log_2", "attn_norm", "b_ada_2", "c_2", "d_skip_2", "dt_bias_2", "ffn_conv_w_2", "ffn_norm",
          "final_norm", "final_norm_w_2", "gla_b_gate", "gla_out_norm", "gla_w_gate", "gla_w_in", "gla_w_o",
          "moe_w1", "moe_w2", "moe_w3", "moe_w_expert", "moe_w_group", "norm_ffn_w_2", "norm_mix_w_2",
          "rel_bias_2", "ssd_conv_b_2", "ssd_conv_w_2", "ssd_norm_w_2", "w_ada_2", "w_down_2", "w_in_2",
          "w_out_2", "w_up_2", "x")


def kernel(**inputs):
    import numpy as np
    import concourse.bacc as bacc
    from concourse import mybir
    from concourse.bass_utils import run_bass_kernel_spmd

    nc = bacc.Bacc("TRN2", target_bir_lowering=False, num_devices=1)
    arrays, aps = {}, {}
    for name in INPUTS:
        array = np.ascontiguousarray(inputs[name])
        arrays[f"in_{name}_dram"] = array
        aps[name] = nc.dram_tensor(f"in_{name}_dram", array.shape, mybir.dt.from_np(array.dtype), kind="ExternalInput").ap()
    out = nc.dram_tensor("out_0_dram", (1, T, D), mybir.dt.float32, kind="ExternalOutput").ap()
    program(nc, aps, out)
    result = run_bass_kernel_spmd(nc, [arrays], core_ids=[0])
    return result.results[0]["out_0_dram"]
```
